# Optimizing a Trainium2 kernel written in Bass

```python
import jax, jax.numpy as jnp
from jax import lax
import numpy as np

D_MODEL = 1024
BATCH = 1
SEQ = 128
DEPTH = 2
DEC_BATCH = 1
DEC_SEQ = 512
PAST_LEN = 128

GRID_W = 64
N_EVEN = (DEPTH + 1) // 2
N_ODD = DEPTH // 2
RET_WIDTH = 3 * D_MODEL // 4
RET_DV = 128
RET_HEADS = RET_WIDTH // RET_DV
RET_DK = 128
RET_CHUNK = 128
ROPE_BASE = 10000.0
FNET_WIDTH = D_MODEL // 4
FNET_GROUPS = 4
FNET_GDIM = FNET_WIDTH // FNET_GROUPS
AB_IN = 2 * RET_HEADS * RET_DK + 2 * RET_WIDTH + FNET_WIDTH
AB_MIX = RET_WIDTH + FNET_WIDTH
CONV_K = 31
PEER_HEADS = 8
PEER_NKEYS = 128
PEER_EXPERTS = PEER_NKEYS * PEER_NKEYS
PEER_TOPK = 16
PEER_DQ = 256
PEER_DQH = PEER_DQ // 2
PEER_BLOCK = 128
EPS = 1e-6
GN_EPS = 1e-5

kernel_name = "hybrid_retention_fnet_conformer_peer_diffusion_step"

F32 = jnp.float32

def rmsnorm(x, g):
    xf = x.astype(F32)
    y = xf * lax.rsqrt(jnp.mean(xf * xf, axis=-1, keepdims=True) + EPS)
    return (y * g.astype(F32)).astype(x.dtype)

def layernorm(x, g, b):
    xf = x.astype(F32)
    mu = jnp.mean(xf, axis=-1, keepdims=True)
    var = jnp.mean(jnp.square(xf - mu), axis=-1, keepdims=True)
    y = (xf - mu) * lax.rsqrt(var + GN_EPS)
    return (y * g.astype(F32) + b.astype(F32)).astype(x.dtype)

def ada_mod(cvec, w, b):
    m = jax.nn.silu(cvec) @ w + b
    return [t[:, None, :] for t in jnp.split(m, 6, axis=-1)]

def modulate(h, shift, scale):
    return h * (1 + scale) + shift

def rope_2d(x):
    L = x.shape[1]
    rows = L // GRID_W
    r = jnp.repeat(jnp.arange(rows), GRID_W)
    col = jnp.tile(jnp.arange(GRID_W), rows)
    half = RET_DK // 2
    nf = half // 2
    freqs = ROPE_BASE ** (-jnp.arange(nf, dtype=F32) / nf)

    def rot(xh, pos):
        ang = pos.astype(F32)[:, None] * freqs[None, :]
        cos = jnp.cos(ang)[None, :, None, :]
        sin = jnp.sin(ang)[None, :, None, :]
        x1, x2 = xh[..., :nf], xh[..., nf:]
        return jnp.concatenate([x1 * cos - x2 * sin, x2 * cos + x1 * sin], axis=-1)

    xf = x.astype(F32)
    return jnp.concatenate([rot(xf[..., :half], r), rot(xf[..., half:], col)], axis=-1).astype(x.dtype)

def retention_scan(q, k, v, log_gamma, s0):
    B_, L_, H_, _ = q.shape
    DV_ = v.shape[-1]
    C = RET_CHUNK
    n = L_ // C
    pos = jnp.arange(C, dtype=F32)
    diff = pos[:, None] - pos[None, :]
    lg = log_gamma[:, None, None]
    dmat = jnp.where(diff[None] >= 0, jnp.exp(jnp.maximum(diff, 0.0)[None] * lg), 0.0)
    xi = jnp.exp((pos[None, :] + 1.0) * log_gamma[:, None]).T
    zeta = jnp.exp((C - 1.0 - pos)[None, :] * log_gamma[:, None]).T
    g_chunk = jnp.exp(C * log_gamma)

    def to_chunks(t):
        return t.reshape(B_, n, C, H_, t.shape[-1]).transpose(1, 0, 2, 3, 4)

    def step(S, inp):
        qc, kc, vc = inp
        att = jnp.einsum('bihd,bjhd->bhij', qc, kc) * dmat[None]
        inner = jnp.einsum('bhij,bjhe->bihe', att, vc)
        cross = jnp.einsum('bihd,bhde->bihe', qc, S) * xi[None, :, :, None]
        S_new = g_chunk[None, :, None, None] * S + jnp.einsum('bjhd,bjhe->bhde', kc * zeta[None, :, :, None], vc)
        return S_new, inner + cross

    S_fin, out = lax.scan(step, s0, (to_chunks(q), to_chunks(k), to_chunks(v)))
    out = out.transpose(1, 0, 2, 3, 4).reshape(B_, L_, H_, DV_)
    return out, S_fin

def ab_mixer(h, w_in, w_out, lg_f, lg_b, s0_f, s0_b, latent):
    B_, L_, _ = h.shape
    qk_w = RET_HEADS * RET_DK
    proj = h @ w_in
    q, k, v, gt, f = jnp.split(proj, [qk_w, 2 * qk_w, 2 * qk_w + RET_WIDTH, 2 * qk_w + 2 * RET_WIDTH], axis=-1)
    q = q.reshape(B_, L_, RET_HEADS, RET_DK)
    k = k.reshape(B_, L_, RET_HEADS, RET_DK)
    v = v.reshape(B_, L_, RET_HEADS, RET_DV)
    if latent:
        q = rope_2d(q)
        k = rope_2d(k)
    qf = q.astype(F32)
    kf = k.astype(F32) * (RET_DK ** -0.5)
    vf = v.astype(F32)
    o_f, S_f = retention_scan(qf, kf, vf, lg_f, s0_f.astype(F32))
    o_b, S_b = retention_scan(qf[:, ::-1], kf[:, ::-1], vf[:, ::-1], lg_b, s0_b.astype(F32))
    o = o_f + o_b[:, ::-1]
    mu = jnp.mean(o, axis=-1, keepdims=True)
    var = jnp.mean(jnp.square(o - mu), axis=-1, keepdims=True)
    o = ((o - mu) * lax.rsqrt(var + GN_EPS)).reshape(B_, L_, RET_WIDTH)
    ret_out = (o * jax.nn.silu(gt.astype(F32))).astype(h.dtype)
    fg = f.reshape(B_, L_, FNET_GROUPS, FNET_GDIM).astype(F32)
    fnet = jnp.fft.fft2(fg, axes=(1, 3), norm='ortho').real.reshape(B_, L_, FNET_WIDTH).astype(h.dtype)
    out = jnp.concatenate([ret_out, fnet], axis=-1) @ w_out
    return out, S_f.astype(h.dtype), S_b.astype(h.dtype)

def conv_module(h, w_in, dw_w, dw_b, ln_g, ln_b, w_out):
    D_ = h.shape[-1]
    a = h @ w_in
    u = a[..., :D_] * jax.nn.sigmoid(a[..., D_:])
    pad = CONV_K // 2
    y = lax.conv_general_dilated(u, dw_w[:, None, :].astype(u.dtype), window_strides=(1,),
                                 padding=[(pad, pad)], dimension_numbers=('NWC', 'WIO', 'NWC'),
                                 feature_group_count=D_) + dw_b
    y = jax.nn.silu(layernorm(y, ln_g, ln_b))
    return y @ w_out

def peer(h, w_q, sub_keys, u_tab, v_tab):
    B_, L_, D_ = h.shape
    x = h.reshape(-1, D_)
    T = x.shape[0]
    q = (x @ w_q).reshape(T, PEER_HEADS, 2, PEER_DQH).astype(F32)
    scores = jnp.einsum('thsd,hskd->thsk', q, sub_keys.astype(F32))
    s, i = lax.top_k(scores, PEER_TOPK)
    cand = (s[:, :, 0, :, None] + s[:, :, 1, None, :]).reshape(T, PEER_HEADS, PEER_TOPK * PEER_TOPK)
    cidx = (i[:, :, 0, :, None] * PEER_NKEYS + i[:, :, 1, None, :]).reshape(T, PEER_HEADS, PEER_TOPK * PEER_TOPK)
    top, sel = lax.top_k(cand, PEER_TOPK)
    idx = jnp.take_along_axis(cidx, sel, axis=-1)
    g = jax.nn.softmax(top, axis=-1)
    nb = T // PEER_BLOCK

    def block(args):
        xb, ib, gb = args
        a = jax.nn.gelu(jnp.einsum('td,thkd->thk', xb, u_tab[ib]).astype(F32))
        w = (gb * a).astype(xb.dtype)
        return jnp.einsum('thk,thkd->td', w, v_tab[ib])

    out = lax.map(block, (x.reshape(nb, PEER_BLOCK, D_),
                          idx.reshape(nb, PEER_BLOCK, PEER_HEADS, PEER_TOPK),
                          g.reshape(nb, PEER_BLOCK, PEER_HEADS, PEER_TOPK)))
    return out.reshape(B_, L_, D_)

def setup_inputs(seed: int = 0) -> dict:
    key = jax.random.key(seed)
    ks = jax.random.split(key, 32)

    def nrm(k, shape, scale):
        return jax.random.normal(k, shape, F32) * scale

    D = D_MODEL
    decay_base = jnp.asarray(np.log(2.0 ** (5.0 + np.arange(RET_HEADS)) - 1.0), F32)
    return {
        "x_prompt": nrm(ks[0], (BATCH, SEQ, D), 1.0),
        "x_sample": nrm(ks[1], (DEC_BATCH, DEC_SEQ, D), 1.0),
        "state_ret_fwd": nrm(ks[2], (DEC_BATCH, N_EVEN, RET_HEADS, RET_DK, RET_DV), 1.0),
        "state_ret_bwd": nrm(ks[3], (DEC_BATCH, N_EVEN, RET_HEADS, RET_DK, RET_DV), 1.0),
        "c": nrm(ks[4], (DEC_BATCH, D), 1.0),
        "c_ctx": nrm(ks[5], (D,), 1.0),
        "norm_gain": 1.0 + nrm(ks[6], (DEPTH, 2, D), 0.02),
        "final_gain": 1.0 + nrm(ks[7], (D,), 0.02),
        "ada_w": nrm(ks[8], (DEPTH, D, 6 * D), 0.5 * D ** -0.5),
        "ada_b": nrm(ks[9], (DEPTH, 6 * D), 0.02),
        "ab_w_in": nrm(ks[10], (N_EVEN, D, AB_IN), D ** -0.5),
        "ab_w_out": nrm(ks[11], (N_EVEN, AB_MIX, D), AB_MIX ** -0.5),
        "ret_decay_fwd": decay_base[None, :] + nrm(ks[12], (N_EVEN, RET_HEADS), 0.05),
        "ret_decay_bwd": decay_base[None, :] + nrm(ks[13], (N_EVEN, RET_HEADS), 0.05),
        "conv_w_in": nrm(ks[14], (N_ODD, D, 2 * D), D ** -0.5),
        "conv_dw_w": nrm(ks[15], (N_ODD, CONV_K, D), CONV_K ** -0.5),
        "conv_dw_b": nrm(ks[16], (N_ODD, D), 0.02),
        "conv_ln_g": 1.0 + nrm(ks[17], (N_ODD, D), 0.02),
        "conv_ln_b": nrm(ks[18], (N_ODD, D), 0.02),
        "conv_w_out": nrm(ks[19], (N_ODD, D, D), D ** -0.5),
        "peer_w_q": nrm(ks[20], (DEPTH, D, PEER_HEADS * PEER_DQ), D ** -0.5),
        "peer_sub_keys": nrm(ks[21], (DEPTH, PEER_HEADS, 2, PEER_NKEYS, PEER_DQH), PEER_DQH ** -0.5),
        "peer_u": nrm(ks[22], (DEPTH, PEER_EXPERTS, D), D ** -0.5),
        "peer_v": nrm(ks[23], (DEPTH, PEER_EXPERTS, D), PEER_HEADS ** -0.5),
    }

def reference(x_prompt, x_sample, state_ret_fwd, state_ret_bwd, c, c_ctx, norm_gain, final_gain,
              ada_w, ada_b, ab_w_in, ab_w_out, ret_decay_fwd, ret_decay_bwd, conv_w_in, conv_dw_w,
              conv_dw_b, conv_ln_g, conv_ln_b, conv_w_out, peer_w_q, peer_sub_keys, peer_u, peer_v):
    xp, xs = x_prompt, x_sample
    Bp = xp.shape[0]
    new_f, new_b = [], []
    for l in range(DEPTH):
        mp = ada_mod(c_ctx[None, :], ada_w[l], ada_b[l])
        ms = ada_mod(c, ada_w[l], ada_b[l])
        hp = modulate(rmsnorm(xp, norm_gain[l, 0]), mp[0], mp[1])
        hs = modulate(rmsnorm(xs, norm_gain[l, 0]), ms[0], ms[1])
        if l % 2 == 0:
            e = l // 2
            lg_f = jax.nn.log_sigmoid(ret_decay_fwd[e].astype(F32))
            lg_b = jax.nn.log_sigmoid(ret_decay_bwd[e].astype(F32))
            zeros = jnp.zeros((Bp, RET_HEADS, RET_DK, RET_DV), F32)
            op, sf, sb = ab_mixer(hp, ab_w_in[e], ab_w_out[e], lg_f, lg_b, zeros, zeros, False)
            os_, _, _ = ab_mixer(hs, ab_w_in[e], ab_w_out[e], lg_f, lg_b,
                                 state_ret_fwd[:, e], state_ret_bwd[:, e], True)
            new_f.append(sf)
            new_b.append(sb)
        else:
            o = l // 2
            op = conv_module(hp, conv_w_in[o], conv_dw_w[o], conv_dw_b[o], conv_ln_g[o], conv_ln_b[o], conv_w_out[o])
            os_ = conv_module(hs, conv_w_in[o], conv_dw_w[o], conv_dw_b[o], conv_ln_g[o], conv_ln_b[o], conv_w_out[o])
        xp = xp + mp[2] * op
        xs = xs + ms[2] * os_
        hp = modulate(rmsnorm(xp, norm_gain[l, 1]), mp[3], mp[4])
        hs = modulate(rmsnorm(xs, norm_gain[l, 1]), ms[3], ms[4])
        xp = xp + mp[5] * peer(hp, peer_w_q[l], peer_sub_keys[l], peer_u[l], peer_v[l])
        xs = xs + ms[5] * peer(hs, peer_w_q[l], peer_sub_keys[l], peer_u[l], peer_v[l])
    y_prompt = rmsnorm(xp, final_gain)
    y_sample = rmsnorm(xs, final_gain)
    new_state_fwd = jnp.stack(new_f, axis=1)
    new_state_bwd = jnp.stack(new_b, axis=1)
    return (y_prompt, y_sample, new_state_fwd, new_state_bwd)


_drawn_inputs = setup_inputs


def setup_inputs(seed=0):
    import zlib

    import numpy as np

    out = dict(_drawn_inputs(seed))
    spreads = {}
    factors = {'final_gain': 2.87, 'conv_dw_b': 6.812, 'conv_ln_g': 8.0, 'conv_ln_b': 8.0}
    for name, (base, spread) in spreads.items():
        noise = np.random.default_rng([zlib.crc32(name.encode()), seed]).standard_normal(out[name].shape)
        drawn = base * np.exp(spread * noise) if base else spread * noise
        out[name] = __import__('jax').numpy.asarray(drawn.astype(out[name].dtype))
    for name, factor in factors.items():
        out[name] = (out[name] * factor).astype(out[name].dtype)
    return out
```

```python
from contextlib import ExitStack

import numpy as np
import concourse.bass as bass
from concourse import mybir

F32 = mybir.dt.float32
U32 = mybir.dt.uint32
ALU = mybir.AluOpType
ACT = mybir.ActivationFunctionType
AX = mybir.AxisListType

P = 128
D = 1024
KT = D // P
BLOCKS = 5
LATENT = BLOCKS - 1
T = BLOCKS * P
HEADS = 6
DK = 128
GRID_W = 64
RW = HEADS * DK
HALF = RW // 2
TAPS = 31
PAD = TAPS // 2
UW = (P + 2 * PAD) + (LATENT * P + 2 * PAD)
YW = UW - 2 * PAD
LAT_Y = P + 2 * PAD
PHEADS = 8
TOPK = 16
NKEYS = 128
EXPERTS = NKEYS * NKEYS
AHEAD = 2
RING = 8
NQ = BLOCKS * PHEADS
EPS = 1e-6
GN_EPS = 1e-5
LOWEST = -3.0e38
LAYERS = 2

C_IDENT, C_IOTA, C_POS = 0, 128, 144
C_REL, C_MASK = 148, 404
C_ROPE = 660
C_DFTF = C_ROPE + 2 * LATENT * 64
C_DFTP = C_DFTF + 256
C_KEEP = C_REL
C_ALL = C_DFTP + 256


def constants():
    c = np.zeros((P, C_ALL), np.float32)
    p = np.arange(P)
    c[:, C_IDENT:C_IDENT + P] = np.eye(P)
    c[:, C_IOTA:C_IOTA + TOPK] = np.arange(TOPK)
    c[:, C_POS:C_POS + 4] = np.stack([p + 1, P - 1 - p, P - p, p], 1)
    rel = p[None, :] - p[:, None]
    c[:, C_REL:C_REL + P] = np.maximum(rel, 0)
    c[:, C_REL + P:C_REL + 2 * P] = np.maximum(-rel, 0)
    c[:, C_MASK:C_MASK + P] = (rel >= 0) * DK ** -0.5
    c[:, C_MASK + P:C_MASK + 2 * P] = (rel <= 0) * DK ** -0.5
    nf = DK // 4
    freqs = (np.float32(10000.0) ** (-np.arange(nf, dtype=np.float32) / np.float32(nf))).astype(np.float32)
    tok = np.arange(LATENT * P).reshape(LATENT, P)
    for half, pos in enumerate((tok // GRID_W, tok % GRID_W)):
        ang = pos.astype(np.float32)[:, :, None] * freqs
        for which, fn in enumerate((np.cos, np.sin)):
            for b in range(LATENT):
                at = C_ROPE + which * LATENT * 64 + b * 64 + half * nf
                c[:, at:at + nf] = fn(ang[b])
    g = 64
    a = 2 * np.pi * np.outer(np.arange(g), np.arange(g)) / g
    for i in range(2):
        c[i * g:(i + 1) * g, C_DFTF + i * g:C_DFTF + (i + 1) * g] = np.cos(a) / np.sqrt(g)
        c[i * g:(i + 1) * g, C_DFTF + P + i * g:C_DFTF + P + (i + 1) * g] = np.sin(a) / np.sqrt(g)
    a = 2 * np.pi * (np.outer(p, p) % P) / P
    c[:, C_DFTP:C_DFTP + P] = np.cos(a) / np.sqrt(P)
    c[:, C_DFTP + P:C_DFTP + 2 * P] = -np.sin(a) / np.sqrt(P)
    n = LATENT * P
    k = np.arange(n)
    a = 2 * np.pi * (np.outer(k, k) % n) / n
    m = np.stack([np.cos(a), -np.sin(a)]) / np.sqrt(n)
    m = m.reshape(2, LATENT, P, n).transpose(2, 0, 1, 3)
    return c, np.ascontiguousarray(m.astype(np.float32))


class Count:

    def __init__(self, sem):
        self.sem, self.base, self.n = sem, 0, 0

    def mark(self, ins):
        ins.then_inc(self.sem, 1)
        self.n += 1
        return self.n

    def now(self):
        return self.base + self.n

    def loop(self, base):
        self.base, self.n = base, 0


def apart(eng, passed, sem, value):
    eng.wait_ge(sem, value)
    eng.sem_inc(passed, 1)


def program(nc, x_in, cond_t, norm_gain, final_gain, ada_w, ada_b, ab_w_in, ab_w_out, decays, states,
            conv_w_in, conv_cols, conv_w_out, peer_w_q, keys_t, peer_u, peer_v, const, dft,
            y_out, new_states, mod_rows):
    ctx = ExitStack()
    with ctx:
        def sb(name, shape, dt=F32):
            return ctx.enter_context(nc.sbuf_tensor(name, shape, dt))

        def sem(name):
            return ctx.enter_context(nc.semaphore(name))

        def per_stage(name, n):
            return [sem(f"{name}{i}") for i in range(n)]

        x = sb("x", [P, BLOCKS, D])
        work = sb("work", [P, 5120 + (NQ + AHEAD) * 256])
        hT_t = sb("hT", [P, KT * T])
        bc = sb("bc", [P, 6, D])
        ring = sb("ring", [P, 4 * 4096])
        diag = sb("diag", [P, TOPK, P])
        keep = sb("keep", [P, C_KEEP])
        small = sb("small", [P, 1536])
        zero_t = sb("zero_t", [P, P])
        qcur = sb("qcur", [P, 2, P])
        stat = sb("stat", [P, 96])
        idx_cur = sb("idx_cur", [P, 2, TOPK], U32)
        dots = sb("dots", [P, 2, TOPK])
        bank = ctx.enter_context(nc.psum_tensor("bank", [P, 8, 512], F32))

        ident = keep[:, C_IDENT:C_IDENT + P]
        iota = keep[:, C_IOTA:C_IOTA + TOPK]
        pos = [keep[:, C_POS + i:C_POS + i + 1] for i in range(4)]
        hT = hT_t[:, :].rearrange("p (k t) -> p k t", k=KT)
        h_tok = work[:, 0:BLOCKS * D].rearrange("p (b d) -> p b d", b=BLOCKS)

        rows = [work[0:2, l * 6 * D:(l + 1) * 6 * D] for l in range(LAYERS)]
        gain_rows = hT_t[0:2, 0:4 * D]
        cond = stat[:, 0:2 * KT].rearrange("p (k c) -> p k c", k=KT)

        k_tok = work[:, 0:5 * RW].rearrange("p (b n) -> p b n", b=BLOCKS)
        v_tok = work[:, 5 * RW:10 * RW].rearrange("p (b n) -> p b n", b=BLOCKS)
        gates = work[:, 10 * RW:15 * RW].rearrange("p (b n) -> p b n", b=BLOCKS)
        qT = work[:, 15 * RW:20 * RW].rearrange("p (h t) -> p h t", h=HEADS)
        dft_p = work[:, 20 * RW:20 * RW + 512]
        xf = x[:, :, :].rearrange("p b d -> p (b d)")
        kT = xf[:, 0:5 * RW].rearrange("p (h t) -> p h t", h=HEADS)
        fT = xf[:, 5 * RW:5 * RW + 2 * T].rearrange("p (c t) -> p c t", c=2)
        bcf = bc[:, :, :].rearrange("p a d -> p (a d)")
        s_b = bcf[:, 0:4 * RW].rearrange("p (c n) -> p c n", c=LATENT)
        s_f = bcf[:, 4 * RW:5 * RW]
        diagf = diag[:, :, :].rearrange("p k t -> p (k t)")
        decay = diagf[:, 0:RW]
        rope = diagf[:, RW:RW + 2 * LATENT * 64].rearrange("p (w b c f) -> p w b c f", w=2, b=LATENT, c=2)
        rel = diagf[:, RW + 512:RW + 768]
        mask = diagf[:, RW + 768:RW + 1024]
        over = ring[:, 8192:16384]
        fmix = over[:, 0:2560].rearrange("p (b c w f) -> p b c w f", b=BLOCKS, c=2, w=2)
        att = over[:, 2560:2560 + RW]
        kz = [over[:, 3328 + i * RW:3328 + (i + 1) * RW] for i in range(2)]
        o1 = over[:, 4864:4864 + RW]
        o2 = over[:, 5632:5632 + RW]
        rot = [over[:, 6400 + i * HALF:6400 + (i + 1) * HALF] for i in range(2)]
        rot_t = over[:, 7168:7168 + 192]
        e_rel = [small[:, 0:RW], small[:, RW:2 * RW]]
        new_s = [small[:, i * RW:(i + 1) * RW] for i in range(2)]
        lg = stat[:, 16:28]
        dec_t = [stat[:, 28:40], stat[:, 40:52], stat[:, 52:64]]
        g_chunk = stat[:, 64:76]
        xi_zeta = sb("xi_zeta", [P, 4, HEADS])
        XI_F, ZETA_F, XI_B, ZETA_B = range(4)
        hstat = sb("hstat", [P, 4, HEADS])
        tok_ss = sb("tok_ss", [P, 8])
        tok_rs = sb("tok_rs", [P, 8])
        warm = sb("warm", [P, 2])

        u_pad = work[:, 0:KT * UW].rearrange("p (k t) -> p k t", k=KT)
        y_conv = work[:, KT * UW:KT * (UW + YW)].rearrange("p (k t) -> p k t", k=KT)
        w0 = KT * (UW + YW)
        sig = [work[:, w0 + i * T:w0 + (i + 1) * T] for i in range(2)]
        ln_rs = work[:, w0 + 2 * T:w0 + 3 * T]
        sq = [work[:, w0 + (3 + i) * T:w0 + (4 + i) * T] for i in range(2)]
        cols = small[:, 0:KT * (TAPS + 3)].rearrange("p (k c) -> p k c", k=KT)
        mean_w = small[:, 512:640]
        prod = [work[:, 14848 + i * 512:14848 + (i + 1) * 512] for i in range(2)]

        qP = work[:, 5120:5120 + (NQ + AHEAD) * 256]
        keys = bcf[:, 0:(PHEADS + AHEAD) * 256]
        k1 = (PHEADS + AHEAD) * 256
        idx_all = bcf[:, k1:k1 + (NQ + AHEAD) * TOPK].bitcast(U32)
        g_all = bcf[:, k1 + (NQ + AHEAD) * TOPK:k1 + 2 * (NQ + AHEAD) * TOPK]
        u_rows = [ring[:, s * D:(s + 1) * D] for s in range(RING)]
        v_rows = [ring[:, (RING + s) * D:(RING + s + 1) * D] for s in range(RING)]
        peer_out = hT_t[:, :].rearrange("p (b d) -> p b d", b=BLOCKS)
        left = small[:, 0:256].rearrange("p (s k) -> p s k", s=2)
        cand = small[:, 256:512]
        cand_left = small[:, 512:768]
        onehot = small[:, 768:1280].rearrange("p (s k a) -> p s k a", s=2, k=TOPK)
        side_v = small[:, 1280:1312].rearrange("p (s k) -> p s k", s=2)
        side_i = small[:, 1312:1344].bitcast(U32).rearrange("p (s k) -> p s k", s=2)
        top_v = small[:, 1344:1360]
        top_i = small[:, 1360:1376].bitcast(U32)
        top_e = small[:, 1376:1392]
        pair = small[:, 1392:1424].bitcast(U32).rearrange("p (s k) -> p s k", s=2)
        part_i = small[:, 1424:1456].rearrange("p (s k) -> p s k", s=2)
        top_n = small[:, 1456:1457]
        top_s = small[:, 1457:1458]
        top_r = small[:, 1458:1459]
        act16 = small[:, 1460:1476]
        wgt = small[:, 1476:1492]

        loaded = sem("loaded")
        even_consts = sem("even_consts")
        slot_in = per_stage("slot_in", 4)
        cond_ready = sem("cond_ready")
        ada_sums = sem("ada_sums")
        ada_taken = sem("ada_taken")
        rows_ready = sem("rows_ready")
        rows_out = sem("rows_out")
        ab_in = per_stage("ab_in", 5)
        gate_in = per_stage("gate_in", 4)
        squares = per_stage("squares", 5)
        mean_sq = per_stage("mean_sq", 5)
        roots = per_stage("roots", 5)
        h_ready = per_stage("h_ready", 4)
        h_turned = per_stage("h_turned", 4)
        hT_ready = per_stage("hT_ready", 4)
        x_done = per_stage("x_done", 4)
        dve = Count(sem("dve_steps"))
        act_own = Count(sem("act_steps"))
        dec_ax = sem("dec_ax"); dec_e = sem("dec_e"); dec_u = sem("dec_u"); dec_l = sem("dec_l")
        lg_ready = sem("lg_ready"); exps_ready = sem("exps_ready")
        proj = sem("proj")
        taken_a = sem("taken_a")
        taken_v = sem("taken_v")
        qk_turned = sem("qk_turned")
        qkT_ready = sem("qkT_ready")
        f_proj = sem("f_proj"); fT_ready = sem("fT_ready")
        fmix_sums = sem("fmix_sums"); fmix_ready = sem("fmix_ready")
        fseq_sums = sem("fseq_sums"); fseq_ready = sem("fseq_ready")
        kz_ready = sem("kz_ready"); upd_sums = sem("upd_sums"); state_ready = sem("state_ready")
        att_sums = sem("att_sums"); att_ready = sem("att_ready")
        ret_sums = sem("ret_sums"); ret_var = sem("ret_var"); ret_root = sem("ret_root")
        ret_taken = sem("ret_taken"); ret_ready = sem("ret_ready")
        ret_turned = sem("ret_turned"); retT_ready = sem("retT_ready")
        states_in = sem("states_in"); states_out = sem("states_out"); x_back = sem("x_back")
        conv_in = sem("conv_in"); glu_sums = sem("glu_sums"); sig_ready = sem("sig_ready")
        u_ready = sem("u_ready"); conv_ready = sem("conv_ready")
        ln_mean = sem("ln_mean"); centred = sem("centred"); sq_ready = sem("sq_ready")
        sq_used = sem("sq_used"); ln_var = sem("ln_var"); ln_ve = sem("ln_ve"); ln_root = sem("ln_root")
        normed = sem("normed"); swish_ready = sem("swish_ready")
        out_sums = per_stage("out_sums", LAYERS)
        out_taken = per_stage("out_taken", LAYERS)
        wq_sums = per_stage("wq_sums", LAYERS); q_ready = per_stage("q_ready", LAYERS)
        keys_in = per_stage("keys_in", LAYERS)
        q_head = per_stage("q_head", LAYERS); scores = per_stage("scores", LAYERS)
        top_ready = per_stage("top_ready", LAYERS); exp_ready = per_stage("exp_ready", LAYERS)
        scores_read = per_stage("scores_read", LAYERS)
        idx_ready = per_stage("idx_ready", LAYERS); idx_staged = per_stage("idx_staged", LAYERS)
        u_in = per_stage("u_in", RING); v_in = per_stage("v_in", RING)
        u_free = per_stage("u_free", LAYERS); v_free = per_stage("v_free", LAYERS)
        gelu_ready = per_stage("gelu_ready", LAYERS)
        diag_ready = per_stage("diag_ready", LAYERS)
        peer_steps = per_stage("peer_steps", LAYERS)
        block_out = per_stage("block_out", LAYERS)
        passed_v = sem("passed_v"); passed_a = sem("passed_a"); passed_p = sem("passed_p")
        y_ready = sem("y_ready"); y_stored = sem("y_stored")

        def tall(w, c0, n):
            return w[:, c0:c0 + n].rearrange("(k p) n -> p k n", p=P)

        def slot(s, n):
            return ring[:, s * 4096:s * 4096 + KT * n].rearrange("p (k n) -> p k n", k=KT)

        chunks = []

        def chunk(parts, s, done, after=None):
            chunks.append((parts, s, done, after))
            return len(chunks) - 1

        CH = 512
        ADA = 6 * D // CH
        ada_c = [[chunk([(slot((l * ADA + c) % 4, CH), tall(ada_w[l], c * CH, CH))], (l * ADA + c) % 4,
                        (ada_sums, l * ADA + c + 1)) for c in range(ADA)] for l in range(LAYERS)]
        ab_c = [chunk([(slot(c % 2, HALF), tall(ab_w_in, c * HALF, HALF))], c % 2, (proj, 5 * c + 5))
                for c in range(8)]
        f_c = chunk([(slot(0, 256), tall(ab_w_in, 8 * HALF, 256))], 0, (f_proj, 2))
        dft_c = chunk([(ring[:, 4096:8192].rearrange("p (w b n) -> p w b n", w=2, b=LATENT), dft)], 1, (fseq_sums, 1))
        wo0_c = [chunk([(slot(c, CH), tall(ab_w_out, c * CH, CH))], c, (out_sums[0], 5 * c + 5)) for c in range(2)]
        wq_c = [[], []]
        wq_c[0] = [chunk([(slot((c + 2) % 4, CH), tall(peer_w_q[0], c * CH, CH))], (c + 2) % 4, (wq_sums[0], 4 * c + 4),
                         (retT_ready, BLOCKS) if c < 2 else None) for c in range(4)]
        cin_c = [chunk([(slot(c, CH)[:, :, 256 * i:256 * i + 256], tall(conv_w_in, i * D + 256 * c, 256))
                        for i in range(2)], c, (glu_sums, 2 * c + 2),
                       (block_out[0], BLOCKS + 1)) for c in range(4)]
        wo1_c = [chunk([(slot(c, CH), tall(conv_w_out, c * CH, CH))], c, (out_sums[1], 5 * c + 5)) for c in range(2)]
        wq_c[1] = [chunk([(slot((c + 2) % 4, CH), tall(peer_w_q[1], c * CH, CH))], (c + 2) % 4, (wq_sums[1], 4 * c + 4))
                   for c in range(4)]
        landed_at, so_far = [], [0] * 4
        for parts, s, _, _ in chunks:
            so_far[s] += 16 * len(parts)
            landed_at.append((slot_in[s], so_far[s]))

        def arrived(eng, c):
            eng.wait_ge(*landed_at[c])

        items = [(c, b) for c in range(8) for b in range(BLOCKS)]
        takes, na, nv = [], 0, 0
        for c, b in items:
            if c < 4 and b > 0:
                nv += 1
                takes.append((taken_v, nv))
            else:
                na += 1
                takes.append((taken_a, na))
        updates = [("b", 4), ("b", 3), ("b", 2), ("b", 0), ("f", 0), ("f", 1), ("f", 2), ("f", 3)]
        order = [("u", 0), ("u", 1), ("u", 2), ("u", 3), ("u", 4), ("a", 0), ("a", 1), ("u", 5),
                 ("a", 2), ("u", 6), ("a", 3), ("u", 7), ("a", 4)]
        segs = [(0, P, 0, PAD, 0), (P, LATENT * P, LAT_Y, P + 3 * PAD, 1)]

        def heads3(ap):
            return ap.rearrange("p (b h i) -> p b h i", b=2, h=3)

        def banks3(b0):
            return bank[:, b0:b0 + 2, 0:HALF].rearrange("p b (h i) -> p b h i", h=3)

        def wide(ap, n=DK):
            return ap.rearrange("p (b h) -> p b h", b=2).unsqueeze(3).to_broadcast([P, 2, 3, n])

        block = ctx.enter_context(nc.Block())

        @block.sync
        def _(sp):
            last_in_slot = {}
            for c, (parts, s, done, after) in enumerate(chunks):
                if s in last_in_slot:
                    sp.wait_ge(*chunks[last_in_slot[s]][2])
                if after:
                    sp.wait_ge(*after)
                last_in_slot[s] = c
                for dst, src in parts:
                    sp.dma_start(dst, src).then_inc(slot_in[s], 16)
            for b in range(BLOCKS):
                sp.wait_ge(y_ready, b + 1)
                sp.dma_start(y_out[b * P:(b + 1) * P, :], peer_out[:, b, :]).then_inc(y_stored, 16)
            sp.wait_ge(y_stored, 16 * BLOCKS)
            sp.wait_ge(states_out, 32)

        @block.gpsimd
        def _(pool):
            def load(dst, src, s):
                nc.gpsimd.dma_start(dst, src).then_inc(s, 16)

            load(cond, cond_t, loaded)
            load(keep[:, :], const[:, 0:C_KEEP], loaded)
            for l in range(LAYERS):
                load(rows[l], ada_b[l:l + 1, :].to_broadcast([2, 6 * D]), loaded)
            load(gain_rows, norm_gain.to_broadcast([2, 4 * D]), loaded)
            load(dec_t[0], decays.to_broadcast([P, 2 * HEADS]), loaded)
            load(x[:, :, :], x_in.rearrange("(b p) d -> p b d", p=P), loaded)
            load(diagf[:, RW:RW + 512], const[:, C_ROPE:C_ROPE + 512], even_consts)
            load(diagf[:, RW + 512:RW + 1024], const[:, C_REL:C_REL + 512], even_consts)

            def norm_rows(s):
                l, sub = s // 2, s % 2
                for kind in range(2):
                    for i, r in enumerate((3 * sub + 1, 3 * sub)):
                        load(bc[:, 2 * i + kind, :], mod_rows[l, kind:kind + 1, r * D:(r + 1) * D].to_broadcast([P, D]), ab_in[s])

            def gate_rows(s):
                l, sub = s // 2, s % 2
                for kind in range(2):
                    r = 3 * sub + 2
                    load(bc[:, 4 + kind, :], mod_rows[l, kind:kind + 1, r * D:(r + 1) * D].to_broadcast([P, D]), gate_in[s])

            pool.wait_ge(rows_ready, LAYERS)
            for l in range(LAYERS):
                nc.gpsimd.dma_start(mod_rows[l], rows[l]).then_inc(rows_out, 16)
            pool.wait_ge(rows_out, 16 * LAYERS)
            norm_rows(0)
            gate_rows(0)
            pool.wait_ge(h_ready[0], BLOCKS)
            for dst, i in ((s_f, 0), (s_b[:, LATENT - 1, :], 1)):
                load(dst.rearrange("p (h e) -> p h e", h=HEADS), states[i].rearrange("h d e -> d h e"), states_in)
            load(dft_p, const[:, C_DFTF:C_DFTF + 512], even_consts)
            pool.wait_ge(state_ready, 5)
            for i in range(2):
                nc.gpsimd.dma_start(new_states[i].rearrange("h d e -> d h e"),
                                    new_s[i].rearrange("p (h e) -> p h e", h=HEADS)).then_inc(states_out, 16)
            pool.wait_ge(ret_sums, BLOCKS)
            pool.wait_ge(fmix_ready, BLOCKS)
            load(x[:, :, :], x_in.rearrange("(b p) d -> p b d", p=P), x_back)
            norm_rows(1)

            for l in range(LAYERS):
                if l == 1:
                    pool.wait_ge(x_done[1], BLOCKS)
                    norm_rows(2)
                    gate_rows(2)
                    load(cols, conv_cols, conv_in)
                    pool.wait_ge(h_ready[2], BLOCKS)
                    norm_rows(3)
                pool.wait_ge(x_done[2 * l], BLOCKS)
                gate_rows(2 * l + 1)
                pool.wait_ge(h_ready[2 * l + 1], BLOCKS)
                load(keys[:, 0:PHEADS * 256], keys_t[l], keys_in[l])
                load(keys[:, PHEADS * 256:], keys_t[l][:, 0:AHEAD * 256], keys_in[l])
                pool.wait_ge(wq_sums[l], 16)
                start = l * NQ
                with pool.Fori(0, NQ // 2) as n2:
                    for par in range(2):
                        n = n2 * 2 + par
                        apart(pool, passed_p, idx_ready[l], n + 1)
                        nc.gpsimd.tensor_copy(idx_cur[:, par, :], idx_all[:, bass.ds(n * TOPK, TOPK)]).then_inc(idx_staged[l], 1)
                        apart(pool, passed_p, idx_staged[l], n + 1)
                        for table, rows_, free, landed in ((peer_u, u_rows, u_free, u_in), (peer_v, v_rows, v_free, v_in)):
                            for k in range(TOPK):
                                apart(pool, passed_p, free[l], n * TOPK + k + 1)
                                nc.gpsimd.indirect_dma_start(
                                    rows_[k % RING], None, table,
                                    bass.IndirectOffsetOnAxis(ap=idx_cur[:, par, k:k + 1], axis=0),
                                ).then_inc(landed[k % RING], 16)
            pool.wait_ge(x_done[3], BLOCKS)
            load(bc[:, 0, :], final_gain.to_broadcast([P, D]), ab_in[4])

        @block.tensor
        def _(pe):
            def mm(out, lhsT, rhs, start, stop, **kw):
                return nc.tensor.matmul(out, lhsT, rhs, start=start, stop=stop, **kw)

            pe.wait_ge(cond_ready, 1)
            for l in range(LAYERS):
                for c in range(ADA):
                    g = l * ADA + c
                    arrived(pe, ada_c[l][c])
                    if g >= 4:
                        pe.wait_ge(ada_taken, g - 3)
                    w = slot(g % 4, CH)
                    for k in range(KT):
                        last = mm(bank[0:2, g % 4, :], cond[:, k, :], w[:, k, :], k == 0, k == KT - 1)
                    last.then_inc(ada_sums, 1)

            def turn(s):
                for b in range(BLOCKS):
                    pe.wait_ge(h_ready[s], b + 1)
                    if b >= 4:
                        pe.wait_ge(hT_ready[s], b - 3)
                    b0 = 2 * (b % 4)
                    for k in range(KT):
                        last = nc.tensor.transpose(bank[:, b0 + k // 4, (k % 4) * P:(k % 4 + 1) * P],
                                                   h_tok[:, b, k * P:(k + 1) * P], ident)
                    last.then_inc(h_turned[s], 1)
                pe.wait_ge(hT_ready[s], BLOCKS)

            def project_out(l, cs, ready):
                for g, (c, b) in enumerate((c, b) for c in range(2) for b in range(BLOCKS)):
                    if b == 0:
                        arrived(pe, cs[c])
                    if g >= 4:
                        pe.wait_ge(out_taken[l], g - 3)
                    for k in range(KT):
                        last = mm(bank[:, g % 4, :], hT[:, k, b * P:(b + 1) * P], slot(c, CH)[:, k, :], k == 0, k == KT - 1)
                    last.then_inc(out_sums[l], 1)

            def peer(l):
                turn(2 * l + 1)
                for ft in range(2 * PHEADS):
                    if ft % 4 == 0:
                        arrived(pe, wq_c[l][ft // 4])
                    if ft >= 4:
                        pe.wait_ge(q_ready[l], ft - 3)
                    w = slot((ft // 4 + 2) % 4, CH)[:, :, (ft % 4) * P:(ft % 4 + 1) * P]
                    b0 = 2 * (ft % 4)
                    for k in range(KT):
                        mm(bank[:, b0, :], w[:, k, :], hT[:, k, 0:512], k == 0, k == KT - 1)
                    for k in range(KT):
                        last = mm(bank[:, b0 + 1, 0:P], w[:, k, :], hT[:, k, 512:T], k == 0, k == KT - 1)
                    last.then_inc(wq_sums[l], 1)
                pe.wait_ge(q_ready[l], 2 * PHEADS)
                pe.wait_ge(keys_in[l], 32)

                def score(h):
                    for s in range(2):
                        last = mm(bank[:, 4, s * P:(s + 1) * P], qcur[:, s, :],
                                  keys[:, bass.ds(h * 256 + s * P, P)] if not isinstance(h, int)
                                  else keys[:, h * 256 + s * P:h * 256 + (s + 1) * P], True, True)
                    last.then_inc(scores[l], 1)

                for m in range(AHEAD):
                    pe.wait_ge(q_head[l], m + 1)
                    if m:
                        pe.wait_ge(scores_read[l], m)
                    score(m)
                with pe.Fori(0, BLOCKS) as b:
                    pe.wait_ge(block_out[l], b + 1)
                    for i in range(8):
                        mm(bank[:, i // 4, (i % 4) * P:(i % 4 + 1) * P], zero_t[:, :], ident, i % 4 == 0, False,
                           skip_group_check=True)
                    with pe.Fori(0, PHEADS // 2) as h2:
                        for par in range(2):
                            h = h2 * 2 + par
                            n = b * PHEADS + h
                            pe.wait_ge(q_head[l], n + AHEAD + 1)
                            pe.wait_ge(scores_read[l], n + AHEAD)
                            score(h + AHEAD)
                            pe.wait_ge(diag_ready[l], n + 1)
                            for k in range(TOPK):
                                pe.wait_ge(v_in[k % RING], (l * NQ * 2 + n * 2 + k // RING + 1) * 16)
                                for half in range(2):
                                    last = mm(bank[:, half, :], diag[:, k, :],
                                              v_rows[k % RING][:, half * 512:(half + 1) * 512], False, False,
                                              skip_group_check=True)
                                last.then_inc(v_free[l], 1)

            turn(0)
            def project(i):
                c, b = items[i]
                if b == 0:
                    arrived(pe, ab_c[c])
                if i >= 4:
                    pe.wait_ge(*takes[i - 4])
                for k in range(KT):
                    last = mm(bank[:, i % 4, 0:HALF], hT[:, k, b * P:(b + 1) * P], slot(c % 2, HALF)[:, k, :],
                              k == 0, k == KT - 1)
                last.then_inc(proj, 1)

            def turn_qk(i):
                c, b = items[i]
                pe.wait_ge(*takes[i])
                if i >= 4:
                    pe.wait_ge(qkT_ready, i - 3)
                src = rot[i % 2] if c < 2 else k_tok[:, b, (c - 2) * HALF:(c - 1) * HALF]
                for h in range(3):
                    last = nc.tensor.transpose(bank[:, 4 + i % 4, h * P:(h + 1) * P], src[:, h * P:(h + 1) * P], ident)
                last.then_inc(qk_turned, 1)

            for i in range(len(items)):
                project(i)
                if 0 <= i - 1 < 4 * BLOCKS:
                    turn_qk(i - 1)
            arrived(pe, f_c)
            for c in range(2):
                pe.wait_ge(*takes[36 + 2 * c])
                pe.wait_ge(*takes[37 + 2 * c])
                for t0, n, bk in ((0, 512, 2 * c), (512, P, 2 * c + 1)):
                    for k in range(KT):
                        last = mm(bank[:, bk, 0:n], slot(0, 256)[:, k, c * P:(c + 1) * P], hT[:, k, t0:t0 + n],
                                  k == 0, k == KT - 1)
                last.then_inc(f_proj, 1)
            pe.wait_ge(qkT_ready, 4 * BLOCKS)
            pe.wait_ge(even_consts, 48)
            for b in range(BLOCKS):
                pe.wait_ge(fT_ready, 2)
                for c in range(2):
                    last = mm(bank[:, b, c * 256:(c + 1) * 256] if b < 4 else bank[:, 4, c * 256:(c + 1) * 256],
                              fT[:, c, b * P:(b + 1) * P], dft_p[:, 0:256], True, True)
                last.then_inc(fmix_sums, 1)
            pe.wait_ge(fmix_ready, BLOCKS)
            arrived(pe, dft_c)
            dft_s = ring[:, 4096:8192].rearrange("p (w b n) -> p w b n", w=2, b=LATENT)
            for c in range(2):
                for w in range(2):
                    for b in range(LATENT):
                        mm(bank[:, c, :], fmix[:, b + 1, c, w, :], dft_s[:, w, b, :], w + b == 0, w == 1 and b == LATENT - 1)
                for w in range(2):
                    last = mm(bank[:, 2 + c, 0:P], fmix[:, 0, c, w, :], dft_p[:, 256 + w * P:256 + (w + 1) * P], w == 0, w == 1)
            last.then_inc(fseq_sums, 1)
            pe.wait_ge(fseq_ready, 1)

            for what, j in order:
                if what == "u":
                    b = updates[j][1]
                    pe.wait_ge(kz_ready, j + 1)
                    if j >= 1:
                        pe.wait_ge(state_ready, j)
                    for h in range(HEADS):
                        last = mm(bank[:, h // 3, (h % 3) * P:(h % 3 + 1) * P], kz[j % 2][:, h * P:(h + 1) * P],
                                  v_tok[:, b, h * P:(h + 1) * P], True, True)
                    last.then_inc(upd_sums, 1)
                    continue
                b = j
                tok = slice(b * P, (b + 1) * P)
                pe.wait_ge(state_ready, {0: 5, 1: 5, 2: 6, 3: 7, 4: 8}[b])
                pe.wait_ge(states_in, 32)
                if b:
                    pe.wait_ge(retT_ready, b)
                for h in range(HEADS):
                    last = mm(bank[:, h // 3, (h % 3) * P:(h % 3 + 1) * P], kT[:, h, tok], qT[:, h, tok], True, True)
                last.then_inc(att_sums, 1)
                if b:
                    for h in range(HEADS):
                        at = slice((h % 3) * P, (h % 3 + 1) * P)
                        mm(bank[:, 4 + h // 3, at], qT[:, h, tok], s_f[:, h * P:(h + 1) * P], True, True)
                        mm(bank[:, 6 + h // 3, at], qT[:, h, tok], s_b[:, b - 1, h * P:(h + 1) * P], True, True)
                pe.wait_ge(att_ready, b + 1)
                for h in range(HEADS):
                    last = mm(bank[:, 2 + h // 3, (h % 3) * P:(h % 3 + 1) * P], att[:, h * P:(h + 1) * P],
                              v_tok[:, b, h * P:(h + 1) * P], True, True)
                last.then_inc(ret_sums, 1)
                pe.wait_ge(ret_ready, b + 1)
                for h in range(HEADS):
                    last = nc.tensor.transpose(bank[:, 2 + h // 3, (h % 3) * P:(h % 3 + 1) * P],
                                               gates[:, b, h * P:(h + 1) * P], ident)
                last.then_inc(ret_turned, 1)
            pe.wait_ge(retT_ready, BLOCKS)
            project_out(0, wo0_c, None)
            pe.wait_ge(out_taken[0], 2 * BLOCKS)
            peer(0)

            turn(2)
            for f in range(KT):
                if f % 2 == 0:
                    arrived(pe, cin_c[f // 2])
                if f >= 2:
                    pe.wait_ge(u_ready, f - 1)
                w = slot(f // 2, CH)
                for part in range(2):
                    at = part * 256 + (f % 2) * P
                    for t0, n, _, _, kind in segs:
                        for k in range(KT):
                            last = mm(bank[:, 4 * (f % 2) + 2 * part + kind, 0:n], w[:, k, at:at + P],
                                      hT[:, k, t0:t0 + n], k == 0, k == KT - 1)
                last.then_inc(glu_sums, 1)
            pe.wait_ge(u_ready, KT)
            for f in range(KT):
                pe.wait_ge(conv_ready, f + 1)
                for t0, n, y0, _, kind in segs:
                    last = mm(bank[:, kind, 0:n], mean_w, y_conv[:, f, y0:y0 + n], f == 0, f == KT - 1)
            last.then_inc(ln_mean, 1)
            for f in range(KT):
                pe.wait_ge(sq_ready, f + 1)
                for t0, n, _, _, kind in segs:
                    last = mm(bank[:, 2 + kind, 0:n], mean_w, sq[f % 2][:, t0:t0 + n], f == 0, f == KT - 1)
                last.then_inc(sq_used, 1)
            pe.wait_ge(swish_ready, KT)
            project_out(1, wo1_c, None)
            pe.wait_ge(out_taken[1], 2 * BLOCKS)
            peer(1)

        @block.scalar
        def _(act):
            def f(out, in_, func=ACT.Copy, **kw):
                return nc.scalar.activation(out, in_, func, **kw)

            act.wait_ge(loaded, 16 * 7)
            f(cond, cond, ACT.Silu).then_inc(cond_ready, 1)
            act.wait_ge(dec_ax, 1)
            f(dec_t[1], dec_t[1], ACT.Exp, scale=-1.0).then_inc(dec_e, 1)
            act.wait_ge(dec_u, 1)
            f(lg, dec_t[2], ACT.Ln).then_inc(dec_l, 1)
            act.wait_ge(lg_ready, 1)
            act.wait_ge(even_consts, 32)
            for i in range(4):
                f(xi_zeta[:, i, :], lg[:, (i // 2) * HEADS:(i // 2 + 1) * HEADS], ACT.Exp, scale=pos[i])
            f(g_chunk, lg, ACT.Exp, scale=float(P))
            for d in range(2):
                for h in range(HEADS):
                    last = f(e_rel[d][:, h * P:(h + 1) * P], rel[:, d * P:(d + 1) * P], ACT.Exp,
                             scale=lg[:, d * HEADS + h:d * HEADS + h + 1])
            last.then_inc(exps_ready, 1)

            def norm(s):
                if s == 0:
                    act.wait_ge(rows_out, 16 * LAYERS)
                for b in range(BLOCKS):
                    if s:
                        act.wait_ge(x_done[s - 1], b + 1)
                    dst = h_tok[:, b, :] if s < 4 else hT_t[:, b * D:(b + 1) * D]
                    last = f(dst, x[:, b, :], ACT.Square, accum_out=tok_ss[:, b:b + 1])
                last.then_inc(squares[s], 1)
                act.wait_ge(mean_sq[s], 1)
                f(tok_rs[:, 0:BLOCKS], tok_ss[:, 0:BLOCKS], ACT.Sqrt).then_inc(roots[s], 1)

            def take_turned(s):
                for b in range(BLOCKS):
                    act.wait_ge(h_turned[s], b + 1)
                    b0 = 2 * (b % 4)
                    f(hT[:, :, b * P:(b + 1) * P], bank[:, b0:b0 + 2, :].rearrange("p b (k t) -> p (b k) t", k=4))\
                        .then_inc(hT_ready[s], 1)

            def peer(l):
                norm(2 * l + 1)
                take_turned(2 * l + 1)
                q4 = qP[:, 0:NQ * 256].rearrange("p (b f t) -> p b f t", b=BLOCKS, f=2 * PHEADS)
                for ft in range(2 * PHEADS):
                    act.wait_ge(wq_sums[l], ft + 1)
                    b0 = 2 * (ft % 4)
                    f(q4[:, 0:4, ft, :], bank[:, b0, :].rearrange("p (b t) -> p b t", b=4))
                    last = f(q4[:, 4, ft, :], bank[:, b0 + 1, 0:P])
                    last.then_inc(q_ready[l], 1)
                act.wait_ge(q_ready[l], 2 * PHEADS)

                def soft(m):
                    act.wait_ge(top_ready[l], m + 1)
                    f(top_e, top_v, ACT.Exp, bias=top_n, accum_out=top_s).then_inc(exp_ready[l], 1)

                for m in range(AHEAD):
                    if m:
                        act.wait_ge(scores[l], m)
                    f(qcur[:, :, :].rearrange("p s t -> p (s t)"), qP[:, m * 256:(m + 1) * 256]).then_inc(q_head[l], 1)
                for m in range(AHEAD):
                    soft(m)
                with act.Fori(0, BLOCKS) as b:
                    with act.Fori(0, PHEADS // 2) as h2:
                        for par in range(2):
                            n = b * PHEADS + h2 * 2 + par
                            apart(act, passed_a, scores[l], n + AHEAD)
                            f(qcur[:, :, :].rearrange("p s t -> p (s t)"),
                              qP[:, bass.ds((n + AHEAD) * 256, 256)]).then_inc(q_head[l], 1)
                            apart(act, passed_a, u_free[l], RING + (n + 1) * TOPK)
                            f(act16, dots[:, par, :], ACT.Gelu_apprx_tanh).then_inc(gelu_ready[l], 1)
                            apart(act, passed_a, top_ready[l], n + AHEAD + 1)
                            f(top_e, top_v, ACT.Exp, bias=top_n, accum_out=top_s).then_inc(exp_ready[l], 1)
                    apart(act, passed_a, v_free[l], RING + (b + 1) * PHEADS * TOPK)
                    f(peer_out[:, bass.ds(b, 1), :].rearrange("p b d -> p (b d)"),
                      bank[:, 0:2, :].rearrange("p b d -> p (b d)")).then_inc(block_out[l], 1)

            norm(0)
            take_turned(0)
            for i in range(len(items) + 1):
                if i < len(items):
                    c, b = items[i]
                    if takes[i][0] is taken_a:
                        act.wait_ge(proj, i + 1)
                        if c < 2 and i >= 2:
                            act.wait_ge(qk_turned, i - 1)
                        cc = (c % 2) * HALF
                        dst = (rot[i % 2] if c < 2 else k_tok[:, b, cc:cc + HALF] if c < 4 else
                               v_tok[:, b, cc:cc + HALF] if c < 6 else gates[:, b, cc:cc + HALF])
                        f(dst, bank[:, i % 4, 0:HALF], ACT.Silu if c >= 6 else ACT.Copy).then_inc(taken_a, 1)
                if 0 <= i - 1 < 4 * BLOCKS:
                    c, b = items[i - 1]
                    act.wait_ge(qk_turned, i)
                    dst = qT if c < 2 else kT
                    f(dst[:, (c % 2) * 3:(c % 2) * 3 + 3, b * P:(b + 1) * P],
                      bank[:, 4 + (i - 1) % 4, 0:HALF].rearrange("p (h t) -> p h t", h=3)).then_inc(qkT_ready, 1)
            for c in range(2):
                act.wait_ge(f_proj, c + 1)
                f(fT[:, c, 0:512], bank[:, 2 * c, :])
                f(fT[:, c, 512:T], bank[:, 2 * c + 1, 0:P]).then_inc(fT_ready, 1)
            for b in range(BLOCKS):
                act.wait_ge(fmix_sums, b + 1)
                f(fmix[:, b, :, :, :].rearrange("p c w f -> p (c w f)"), bank[:, b, :]).then_inc(fmix_ready, 1)
            act.wait_ge(fseq_sums, 1)
            for c in range(2):
                f(hT[:, 6 + c, P:T], bank[:, c, :])
                last = f(hT[:, 6 + c, 0:P], bank[:, 2 + c, 0:P])
            last.then_inc(fseq_ready, 1)
            for b in range(BLOCKS):
                act.wait_ge(ret_var, b + 1)
                f(hstat[:, 2, :], hstat[:, 1, :], ACT.Sqrt).then_inc(ret_root, 1)
                act.wait_ge(ret_turned, b + 1)
                f(hT[:, 0:6, b * P:(b + 1) * P].rearrange("p (b h) t -> p b h t", b=2), banks3(2)).then_inc(retT_ready, 1)
            peer(0)

            norm(2)
            take_turned(2)
            for t in range(KT):
                act.wait_ge(glu_sums, t + 1)
                if t >= 2:
                    act.wait_ge(u_ready, t - 1)
                for t0, n, _, _, kind in segs:
                    last = f(sig[t % 2][:, t0:t0 + n], bank[:, 4 * (t % 2) + 2 + kind, 0:n], ACT.Sigmoid)
                last.then_inc(sig_ready, 1)
            for t in range(KT):
                act.wait_ge(centred, t + 1)
                if t >= 2:
                    act.wait_ge(sq_used, t - 1)
                for t0, n, y0, _, kind in segs:
                    last = f(sq[t % 2][:, t0:t0 + n], y_conv[:, t, y0:y0 + n], ACT.Square)
                last.then_inc(sq_ready, 1)
            act.wait_ge(ln_ve, 1)
            f(ln_rs, ln_rs, ACT.Sqrt).then_inc(ln_root, 1)
            for t in range(KT):
                act.wait_ge(normed, t + 1)
                for t0, n, y0, _, kind in segs:
                    last = f(hT[:, t, t0:t0 + n], y_conv[:, t, y0:y0 + n], ACT.Silu,
                             scale=cols[:, t, TAPS + 1:TAPS + 2], bias=cols[:, t, TAPS + 2:TAPS + 3])
                last.then_inc(swish_ready, 1)
            peer(1)
            norm(4)

        @block.vector
        def _(v):
            def step(ins):
                dve.mark(ins)
                v.wait_ge(dve.sem, dve.now())

            step(v.memset(zero_t[:, :], 0.0))
            v.wait_ge(loaded, 16 * 7)
            step(v.tensor_scalar(dec_t[1], dec_t[0], -1.0, None, ALU.mult))
            v.tensor_tensor(dec_t[1], dec_t[1], dec_t[0], ALU.max).then_inc(dec_ax, 1)
            v.wait_ge(dec_e, 1)
            v.tensor_scalar(dec_t[2], dec_t[1], 1.0, None, ALU.add).then_inc(dec_u, 1)
            v.wait_ge(dec_u, 1)
            ctmp, rtmp = stat[:, 76:88], dec_t[0]
            step(v.scalar_tensor_tensor(out=ctmp, in0=dec_t[2], scalar=1.0, in1=dec_t[1], op0=ALU.subtract, op1=ALU.subtract))
            step(v.tensor_scalar(rtmp, dec_t[0], 0.0, None, ALU.min))
            v.wait_ge(dec_l, 1)
            step(v.tensor_tensor(rtmp, rtmp, lg, ALU.subtract))
            step(v.reciprocal(dec_t[2], dec_t[2]))
            step(v.tensor_tensor(ctmp, ctmp, dec_t[2], ALU.mult))
            v.tensor_tensor(lg, rtmp, ctmp, ALU.add).then_inc(lg_ready, 1)
            v.wait_ge(exps_ready, 1)
            for d in range(2):
                e3 = e_rel[d].rearrange("p (h i) -> p h i", h=HEADS)
                m3 = mask[:, d * P:(d + 1) * P].unsqueeze(1).to_broadcast([P, HEADS, P])
                step(v.tensor_tensor(e3, e3, m3, ALU.mult))
            step(v.tensor_tensor(decay, e_rel[0], e_rel[1], ALU.add))
            for i in (ZETA_F, ZETA_B):
                step(v.tensor_scalar(xi_zeta[:, i, :], xi_zeta[:, i, :], DK ** -0.5, None, ALU.mult))

            for g in range(LAYERS * ADA):
                l, c = divmod(g, ADA)
                v.wait_ge(ada_sums, g + 1)
                r = rows[l][:, c * CH:(c + 1) * CH]
                v.tensor_tensor(r, bank[0:2, g % 4, :], r, ALU.add).then_inc(ada_taken, 1)
                if c == ADA - 1:
                    v.wait_ge(ada_taken, g + 1)
                    for sub in range(2):
                        r = rows[l][:, (3 * sub + 1) * D:(3 * sub + 2) * D]
                        last = v.scalar_tensor_tensor(out=r, in0=r, scalar=1.0,
                                                      in1=gain_rows[:, (2 * l + sub) * D:(2 * l + sub + 1) * D],
                                                      op0=ALU.add, op1=ALU.mult)
                        if sub == 0:
                            dve.mark(last)
                    last.then_inc(rows_ready, 1)

            def rsqrt_mean(s):
                v.wait_ge(squares[s], 1)
                v.tensor_scalar(tok_ss[:, 0:BLOCKS], tok_ss[:, 0:BLOCKS], 1.0 / D, EPS, ALU.mult, ALU.add)\
                    .then_inc(mean_sq[s], 1)
                v.wait_ge(roots[s], 1)
                step(v.reciprocal(tok_rs[:, 0:BLOCKS], tok_rs[:, 0:BLOCKS]))

            def norm(s):
                rsqrt_mean(s)
                v.wait_ge(ab_in[s], 64)
                for b in range(BLOCKS):
                    kind = min(b, 1)
                    step(v.scalar_tensor_tensor(out=h_tok[:, b, :], in0=x[:, b, :], scalar=tok_rs[:, b:b + 1],
                                                in1=bc[:, kind, :], op0=ALU.mult, op1=ALU.mult))
                    v.tensor_tensor(h_tok[:, b, :], h_tok[:, b, :], bc[:, 2 + kind, :], ALU.add).then_inc(h_ready[s], 1)

            def add_projection(l):
                v.wait_ge(gate_in[2 * l], 32)
                if l == 0:
                    v.wait_ge(x_back, 16)
                for g, (c, b) in enumerate((c, b) for c in range(2) for b in range(BLOCKS)):
                    v.wait_ge(out_sums[l], g + 1)
                    v.tensor_tensor(prod[g % 2], bank[:, g % 4, :], bc[:, 4 + min(b, 1), c * CH:(c + 1) * CH], ALU.mult)\
                        .then_inc(out_taken[l], 1)
                    v.wait_ge(out_taken[l], g + 1)
                    xs = x[:, b, c * CH:(c + 1) * CH]
                    ins = v.tensor_tensor(xs, xs, prod[g % 2], ALU.add)
                    if c == 1:
                        ins.then_inc(x_done[2 * l], 1)
                        v.wait_ge(x_done[2 * l], b + 1)
                    else:
                        step(ins)

            def peer(l):
                norm(2 * l + 1)
                own = Count(peer_steps[l])
                v.memset(dots[:, :, :], 0.0).then_inc(u_free[l], RING)
                v.memset(warm[:, 0:1], 0.0).then_inc(v_free[l], RING)
                v.memset(warm[:, 1:2], 0.0).then_inc(block_out[l], 1)
                v.wait_ge(hT_ready[2 * l + 1], BLOCKS)
                own.mark(v.memset(qP[:, NQ * 256:], 0.0))


                def settle():
                    apart(v, passed_v, own.sem, own.now())

                def choose(m):
                    apart(v, passed_v, scores[l], m + 1)
                    sc = [bank[:, 4, s * P:(s + 1) * P] for s in range(2)]
                    for s in range(2):
                        own.mark(v.max(side_v[:, s, 0:8], sc[s]))
                    settle()
                    for s in range(2):
                        own.mark(v.match_replace(left[:, s, :], side_v[:, s, 0:8], sc[s], LOWEST))
                    for s in range(2):
                        ins = v.max_index(side_i[:, s, 0:8], side_v[:, s, 0:8], sc[s])
                        if s:
                            ins.then_inc(scores_read[l], 1)
                        else:
                            own.mark(ins)
                    settle()
                    for s in range(2):
                        own.mark(v.max(side_v[:, s, 8:16], left[:, s, :]))
                    settle()
                    for s in range(2):
                        own.mark(v.max_index(side_i[:, s, 8:16], side_v[:, s, 8:16], left[:, s, :]))
                    own.mark(v.tensor_tensor(cand.rearrange("p (a b) -> p a b", a=TOPK),
                                             side_v[:, 0, :].unsqueeze(2).to_broadcast([P, TOPK, TOPK]),
                                             side_v[:, 1, :].unsqueeze(1).to_broadcast([P, TOPK, TOPK]), ALU.add))
                    settle()
                    own.mark(v.max(top_v[:, 0:8], cand))
                    settle()
                    own.mark(v.match_replace(cand_left, top_v[:, 0:8], cand, LOWEST))
                    own.mark(v.tensor_scalar(top_n, top_v[:, 0:1], -1.0, None, ALU.mult))
                    own.mark(v.max_index(top_i[:, 0:8], top_v[:, 0:8], cand))
                    settle()
                    v.max(top_v[:, 8:16], cand_left).then_inc(top_ready[l], 1)
                    apart(v, passed_v, top_ready[l], m + 1)
                    own.mark(v.max_index(top_i[:, 8:16], top_v[:, 8:16], cand_left))
                    settle()
                    own.mark(v.tensor_scalar(pair[:, 0, :], top_i, 4, None, ALU.logical_shift_right))
                    own.mark(v.tensor_scalar(pair[:, 1, :], top_i, TOPK - 1, None, ALU.bitwise_and))
                    settle()
                    own.mark(v.tensor_tensor(onehot.rearrange("p s k a -> p (s k) a"),
                                             pair.rearrange("p s k -> p (s k)").unsqueeze(2).to_broadcast([P, 2 * TOPK, TOPK]),
                                             iota.unsqueeze(1).to_broadcast([P, 2 * TOPK, TOPK]), ALU.is_equal))
                    settle()
                    own.mark(v.tensor_tensor(onehot, onehot, side_i.unsqueeze(2).to_broadcast([P, 2, TOPK, TOPK]), ALU.mult))
                    settle()
                    own.mark(v.tensor_reduce(part_i.rearrange("p s k -> p (s k)"),
                                             onehot.rearrange("p s k a -> p (s k) a"), AX.X, ALU.add))
                    settle()
                    own.mark(v.scalar_tensor_tensor(out=part_i[:, 0, :], in0=part_i[:, 0, :], scalar=float(NKEYS),
                                                    in1=part_i[:, 1, :], op0=ALU.mult, op1=ALU.add))
                    apart(v, passed_v, exp_ready[l], m + 1)
                    own.mark(v.reciprocal(top_r, top_s))
                    settle()
                    at = slice(m * TOPK, (m + 1) * TOPK) if isinstance(m, int) else bass.ds(m * TOPK, TOPK)
                    own.mark(v.tensor_scalar(g_all[:, at], top_e, top_r, None, ALU.mult))
                    v.tensor_scalar(idx_all[:, at], part_i[:, 0, :], float(l * EXPERTS), None, ALU.add)\
                        .then_inc(idx_ready[l], 1)
                    settle()
                    apart(v, passed_v, idx_ready[l], m + 1)

                v.wait_ge(keys_in[l], 32)
                for m in range(AHEAD):
                    choose(m)
                before = own.n
                per = (before - 1) // AHEAD + 1
                with v.Fori(0, BLOCKS) as b:
                    with v.Fori(0, PHEADS // 2) as h2:
                        for par in range(2):
                            n = b * PHEADS + h2 * 2 + par
                            own.loop(n * per + before)
                            for k in range(TOPK):
                                apart(v, passed_v, u_in[k % RING], (l * NQ * 2 + n * 2 + k // RING + 1) * 16)
                                row = u_rows[k % RING]
                                v.scalar_tensor_tensor(out=row, in0=row, scalar=1.0,
                                                       in1=h_tok[:, bass.ds(b, 1), :].rearrange("p b d -> p (b d)"),
                                                       op0=ALU.mult, op1=ALU.mult,
                                                       accum_out=dots[:, par, k:k + 1]).then_inc(u_free[l], 1)
                            apart(v, passed_v, gelu_ready[l], n + 1)
                            own.mark(v.tensor_tensor(wgt, act16, g_all[:, bass.ds(n * TOPK, TOPK)], ALU.mult))
                            settle()
                            apart(v, passed_v, v_free[l], n * TOPK + RING)
                            v.tensor_tensor(diag[:, :, :], ident.unsqueeze(1).to_broadcast([P, TOPK, P]),
                                            wgt.unsqueeze(2).to_broadcast([P, TOPK, P]), ALU.mult)\
                                .then_inc(diag_ready[l], 1)
                            apart(v, passed_v, diag_ready[l], n + 1)
                            choose(n + AHEAD)
                            assert own.n == per
                v.wait_ge(gate_in[2 * l + 1], 32)
                for b in range(BLOCKS):
                    v.wait_ge(block_out[l], b + 2)
                    step(v.tensor_tensor(peer_out[:, b, :], peer_out[:, b, :], bc[:, 4 + min(b, 1), :], ALU.mult))
                    v.tensor_tensor(x[:, b, :], x[:, b, :], peer_out[:, b, :], ALU.add).then_inc(x_done[2 * l + 1], 1)
                    v.wait_ge(x_done[2 * l + 1], b + 1)

            norm(0)
            rt = rot_t.rearrange("p (c h f) -> p c h f", c=2, h=3)
            for i, (c, b) in enumerate(items):
                if takes[i][0] is not taken_v:
                    continue
                v.wait_ge(proj, i + 1)
                if c < 2 and i >= 2:
                    v.wait_ge(qk_turned, i - 1)
                dst = rot[i % 2] if c < 2 else k_tok[:, b, (c - 2) * HALF:(c - 1) * HALF]
                src6 = bank[:, i % 4, 0:HALF].rearrange("p (h c j f) -> p c j h f", h=3, c=2, j=2)
                dst6 = dst.rearrange("p (h c j f) -> p c j h f", h=3, c=2, j=2)
                cos, sin = ([rope[:, w, b - 1, ax, :].unsqueeze(1).to_broadcast([P, 3, 32]) for ax in range(2)] for w in range(2))
                for j, op in ((0, ALU.subtract), (1, ALU.add)):
                    if j == 0 and takes[i][1] > 1:
                        v.wait_ge(taken_v, takes[i][1] - 1)
                    for ax in range(2):
                        dve.mark(v.tensor_tensor(dst6[:, ax, j], src6[:, ax, j], cos[ax], ALU.mult))
                        dve.mark(v.tensor_tensor(rt[:, ax], src6[:, ax, 1 - j], sin[ax], ALU.mult))
                    v.wait_ge(dve.sem, dve.now())
                    for ax in range(2):
                        ins = v.tensor_tensor(dst6[:, ax, j], dst6[:, ax, j], rt[:, ax], op)
                        if j == 1 and ax == 1:
                            ins.then_inc(taken_v, 1)
                        else:
                            dve.mark(ins)
                    if j == 0:
                        v.wait_ge(dve.sem, dve.now())

            v.wait_ge(states_in, 32)
            v.wait_ge(*takes[39])
            v.wait_ge(taken_v, nv)

            def scaled_k(j):
                d, b = updates[j]
                if j >= 2:
                    v.wait_ge(upd_sums, j - 1)
                z = xi_zeta[:, ZETA_F if d == "f" else ZETA_B, :].unsqueeze(2).to_broadcast([P, HEADS, DK])
                v.tensor_tensor(kz[j % 2].rearrange("p (h e) -> p h e", h=HEADS),
                                k_tok[:, b, :].rearrange("p (h e) -> p h e", h=HEADS), z, ALU.mult).then_inc(kz_ready, 1)

            scaled_k(0)
            for what, j in order:
                if what == "u":
                    if j + 1 < len(updates):
                        scaled_k(j + 1)
                    d, b = updates[j]
                    v.wait_ge(upd_sums, j + 1)
                    if b == 0:
                        v.tensor_copy(heads3(new_s[d == "b"]), banks3(0)).then_inc(state_ready, 1)
                    else:
                        old, new = (s_f, s_f) if d == "f" else (s_b[:, b - 1, :], s_b[:, b - 2, :])
                        g = g_chunk[:, 0:HEADS] if d == "f" else g_chunk[:, HEADS:2 * HEADS]
                        if d == "f":
                            v.wait_ge(ret_sums, b + 1)
                        step(v.tensor_tensor(heads3(new), heads3(old), wide(g), ALU.mult))
                        v.tensor_tensor(heads3(new), heads3(new), banks3(0), ALU.add).then_inc(state_ready, 1)
                        v.wait_ge(state_ready, j + 1)
                    continue
                b = j
                v.wait_ge(att_sums, b + 1)
                v.tensor_tensor(heads3(att), banks3(0), heads3(decay), ALU.mult).then_inc(att_ready, 1)
                v.wait_ge(ret_sums, b + 1)
                if b == 0:
                    v.tensor_copy(heads3(o1), banks3(2)).then_inc(ret_taken, 1)
                    v.wait_ge(ret_taken, 1)
                else:
                    dve.mark(v.tensor_tensor(heads3(o1), banks3(4), wide(xi_zeta[:, XI_F, :]), ALU.mult))
                    step(v.tensor_tensor(heads3(o2), banks3(6), wide(xi_zeta[:, XI_B, :]), ALU.mult))
                    step(v.tensor_tensor(o1, o1, o2, ALU.add))
                    v.tensor_tensor(heads3(o1), banks3(2), heads3(o1), ALU.add).then_inc(ret_taken, 1)
                    v.wait_ge(ret_taken, b + 1)
                o3 = o1.rearrange("p (h e) -> p h e", h=HEADS)
                q3 = o2.rearrange("p (h e) -> p h e", h=HEADS)
                step(v.tensor_reduce(hstat[:, 0, :], o3, AX.X, ALU.add))
                step(v.tensor_scalar(hstat[:, 0, :], hstat[:, 0, :], 1.0 / DK, None, ALU.mult))
                step(v.tensor_tensor(o3, o3, hstat[:, 0, :].unsqueeze(2).to_broadcast([P, HEADS, DK]), ALU.subtract))
                step(v.tensor_tensor(o2, o1, o1, ALU.mult))
                step(v.tensor_reduce(hstat[:, 1, :], q3, AX.X, ALU.add))
                v.tensor_scalar(hstat[:, 1, :], hstat[:, 1, :], 1.0 / DK, GN_EPS, ALU.mult, ALU.add).then_inc(ret_var, 1)
                v.wait_ge(ret_root, b + 1)
                step(v.reciprocal(hstat[:, 3, :], hstat[:, 2, :]))
                step(v.tensor_tensor(o3, o3, hstat[:, 3, :].unsqueeze(2).to_broadcast([P, HEADS, DK]), ALU.mult))
                v.tensor_tensor(gates[:, b, :], gates[:, b, :], o1, ALU.mult).then_inc(ret_ready, 1)
                v.wait_ge(ret_ready, b + 1)
            add_projection(0)
            peer(0)

            norm(2)
            v.wait_ge(hT_ready[2], BLOCKS)
            v.wait_ge(conv_in, 16)
            dve.mark(v.memset(mean_w, 1.0 / D))
            for a, n in ((0, PAD), (P + PAD, 2 * PAD), (UW - PAD, PAD)):
                last = v.memset(u_pad[:, :, a:a + n], 0.0)
                dve.mark(last)
            v.wait_ge(dve.sem, dve.now())
            for t in range(0, KT, 2):
                for f in (t, t + 1):
                    v.wait_ge(sig_ready, f + 1)
                    for t0, n, _, u0, kind in segs:
                        last = v.tensor_tensor(u_pad[:, f, u0:u0 + n], bank[:, 4 * (f % 2) + kind, 0:n],
                                               sig[f % 2][:, t0:t0 + n], ALU.mult)
                        if kind == 0:
                            dve.mark(last)
                    last.then_inc(u_ready, 1)
                v.wait_ge(u_ready, t + 2)
                v.wait_ge(dve.sem, dve.now())
                for tap in range(TAPS):
                    for f in (t, t + 1):
                        src = u_pad[:, f, tap:tap + YW]
                        w = cols[:, f, tap:tap + 1]
                        if tap == 0:
                            dve.mark(v.tensor_scalar(y_conv[:, f, :], src, w, cols[:, f, TAPS:TAPS + 1], ALU.mult, ALU.add))
                            continue
                        v.wait_ge(dve.sem, dve.now() - (tap < TAPS - 1 or f == t))
                        ins = v.scalar_tensor_tensor(out=y_conv[:, f, :], in0=src, scalar=w, in1=y_conv[:, f, :],
                                                     op0=ALU.mult, op1=ALU.add)
                        if tap == TAPS - 1:
                            ins.then_inc(conv_ready, 1)
                        else:
                            dve.mark(ins)
                            continue
            v.wait_ge(ln_mean, 1)
            for f in range(KT):
                for t0, n, y0, _, kind in segs:
                    last = v.tensor_tensor(y_conv[:, f, y0:y0 + n], y_conv[:, f, y0:y0 + n], bank[:, kind, 0:n], ALU.subtract)
                    if kind == 0:
                        dve.mark(last)
                last.then_inc(centred, 1)
            v.wait_ge(sq_used, KT)
            for t0, n, _, _, kind in segs:
                last = v.tensor_scalar(ln_rs[:, t0:t0 + n], bank[:, 2 + kind, 0:n], GN_EPS, None, ALU.add)
                if kind == 0:
                    dve.mark(last)
            last.then_inc(ln_ve, 1)
            v.wait_ge(ln_root, 1)
            step(v.reciprocal(ln_rs, ln_rs))
            v.wait_ge(centred, KT)
            for f in range(KT):
                for t0, n, y0, _, kind in segs:
                    last = v.tensor_tensor(y_conv[:, f, y0:y0 + n], y_conv[:, f, y0:y0 + n], ln_rs[:, t0:t0 + n], ALU.mult)
                    if kind == 0:
                        dve.mark(last)
                last.then_inc(normed, 1)
            add_projection(1)
            peer(1)

            rsqrt_mean(4)
            v.wait_ge(ab_in[4], 16)
            for b in range(BLOCKS):
                v.scalar_tensor_tensor(out=peer_out[:, b, :], in0=x[:, b, :], scalar=tok_rs[:, b:b + 1],
                                       in1=bc[:, 0, :], op0=ALU.mult, op1=ALU.mult).then_inc(y_ready, 1)


_INS = ["x_in", "cond_t", "norm_gain", "final_gain", "ada_w", "ada_b", "ab_w_in", "ab_w_out", "decays", "states",
        "conv_w_in", "conv_cols", "conv_w_out", "peer_w_q", "keys_t", "peer_u", "peer_v", "const", "dft"]


def kernel(**a):
    import concourse.bacc as _bacc
    from concourse.bass_utils import run_bass_kernel_spmd as _run

    a = {k: np.asarray(w) for k, w in a.items()}
    const, dft = constants()
    feature = lambda w: w.reshape(-1, KT, P).transpose(2, 1, 0)
    laid = {
        "x_in": np.concatenate([a["x_prompt"][0], a["x_sample"][0]]),
        "cond_t": feature(np.stack([a["c_ctx"], a["c"][0]])),
        "norm_gain": a["norm_gain"].reshape(1, -1), "final_gain": a["final_gain"].reshape(1, -1),
        "ada_w": a["ada_w"], "ada_b": a["ada_b"],
        "ab_w_in": a["ab_w_in"][0], "ab_w_out": a["ab_w_out"][0],
        "decays": np.concatenate([a["ret_decay_fwd"], a["ret_decay_bwd"]], 1),
        "states": np.stack([a["state_ret_fwd"][0, 0], a["state_ret_bwd"][0, 0]]),
        "conv_w_in": a["conv_w_in"][0],
        "conv_cols": feature(np.concatenate([a["conv_dw_w"][0], a["conv_dw_b"], a["conv_ln_g"], a["conv_ln_b"]])),
        "conv_w_out": a["conv_w_out"][0],
        "peer_w_q": a["peer_w_q"],
        "keys_t": a["peer_sub_keys"].transpose(0, 4, 1, 2, 3).reshape(LAYERS, P, -1),
        "peer_u": a["peer_u"].reshape(-1, D), "peer_v": a["peer_v"].reshape(-1, D),
        "const": const, "dft": dft,
    }
    nc = _bacc.Bacc("TRN2", target_bir_lowering=False, num_devices=1)
    arrays, args = {}, []
    for name in _INS:
        w = np.ascontiguousarray(laid[name])
        arrays[f"in_{name}"] = w
        args.append(nc.dram_tensor(f"in_{name}", w.shape, mybir.dt.from_np(w.dtype), kind="ExternalInput").ap())
    y = nc.dram_tensor("out_y", (T, D), F32, kind="ExternalOutput").ap()
    st = nc.dram_tensor("out_states", (2, HEADS, DK, DK), F32, kind="ExternalOutput").ap()
    mod = nc.dram_tensor("mod_rows", (LAYERS, 2, 6 * D), F32, kind="Internal").ap()
    program(nc, *args, y, st, mod)
    r = _run(nc, [arrays], core_ids=[0])
    y, st = r.results[0]["out_y"], r.results[0]["out_states"]
    return y[:P][None], y[P:][None], st[0][None, None], st[1][None, None]
```

```python
from contextlib import ExitStack

import numpy as np
import concourse.bass as bass
from concourse import mybir

F32 = mybir.dt.float32
U32 = mybir.dt.uint32
ALU = mybir.AluOpType
ACT = mybir.ActivationFunctionType
AX = mybir.AxisListType

P = 128
D = 1024
KT = D // P
BLOCKS = 5
LATENT = BLOCKS - 1
T = BLOCKS * P
HEADS = 6
DK = 128
GRID_W = 64
RW = HEADS * DK
HALF = RW // 2
TAPS = 31
PAD = TAPS // 2
UW = (P + 2 * PAD) + (LATENT * P + 2 * PAD)
YW = UW - 2 * PAD
LAT_Y = P + 2 * PAD
PHEADS = 8
TOPK = 16
NKEYS = 128
EXPERTS = NKEYS * NKEYS
AHEAD = 2
U_RING, V_RING = 4, 8
QC = 2 * P
ADA2 = 6 * D // QC
PE_TILES = 2
NQ = BLOCKS * PHEADS
EPS = 1e-6
GN_EPS = 1e-5
LOWEST = -3.0e38
LAYERS = 2

C_IDENT, C_IOTA, C_POS = 0, 128, 144
C_REL, C_MASK = 148, 404
C_ROPE = 660
C_DFTF = C_ROPE + 2 * LATENT * 64
C_DFTP = C_DFTF + 256
C_KEEP = C_REL
C_ALL = C_DFTP + 256


def constants():
    c = np.zeros((P, C_ALL), np.float32)
    p = np.arange(P)
    c[:, C_IDENT:C_IDENT + P] = np.eye(P)
    c[:, C_IOTA:C_IOTA + TOPK] = np.arange(TOPK)
    c[:, C_POS:C_POS + 4] = np.stack([p + 1, P - 1 - p, P - p, p], 1)
    rel = p[None, :] - p[:, None]
    c[:, C_REL:C_REL + P] = np.maximum(rel, 0)
    c[:, C_REL + P:C_REL + 2 * P] = np.maximum(-rel, 0)
    c[:, C_MASK:C_MASK + P] = (rel >= 0) * DK ** -0.5
    c[:, C_MASK + P:C_MASK + 2 * P] = (rel <= 0) * DK ** -0.5
    nf = DK // 4
    freqs = (np.float32(10000.0) ** (-np.arange(nf, dtype=np.float32) / np.float32(nf))).astype(np.float32)
    tok = np.arange(LATENT * P).reshape(LATENT, P)
    for half, pos in enumerate((tok // GRID_W, tok % GRID_W)):
        ang = pos.astype(np.float32)[:, :, None] * freqs
        for which, fn in enumerate((np.cos, np.sin)):
            for b in range(LATENT):
                at = C_ROPE + which * LATENT * 64 + b * 64 + half * nf
                c[:, at:at + nf] = fn(ang[b])
    g = 64
    a = 2 * np.pi * np.outer(np.arange(g), np.arange(g)) / g
    for i in range(2):
        c[i * g:(i + 1) * g, C_DFTF + i * g:C_DFTF + (i + 1) * g] = np.cos(a) / np.sqrt(g)
        c[i * g:(i + 1) * g, C_DFTF + P + i * g:C_DFTF + P + (i + 1) * g] = np.sin(a) / np.sqrt(g)
    a = 2 * np.pi * (np.outer(p, p) % P) / P
    c[:, C_DFTP:C_DFTP + P] = np.cos(a) / np.sqrt(P)
    c[:, C_DFTP + P:C_DFTP + 2 * P] = -np.sin(a) / np.sqrt(P)
    n = LATENT * P
    k = np.arange(n)
    a = 2 * np.pi * (np.outer(k, k) % n) / n
    m = np.stack([np.cos(a), -np.sin(a)]) / np.sqrt(n)
    m = m.reshape(2, LATENT, P, n).transpose(2, 0, 1, 3)
    return c, np.ascontiguousarray(m.astype(np.float32))


class Count:

    def __init__(self, sem):
        self.sem, self.base, self.n = sem, 0, 0

    def mark(self, ins):
        ins.then_inc(self.sem, 1)
        self.n += 1
        return self.n

    def now(self):
        return self.base + self.n

    def loop(self, base):
        self.base, self.n = base, 0


def apart(eng, passed, sem, value):
    eng.wait_ge(sem, value)
    eng.sem_inc(passed, 1)


def program(nc, x_in, cond_t, norm_gain, final_gain, ada_w, ada_b, ada_fix_in, ab_w_in, ab_w_out, decays, states,
            conv_w_in, conv_cols, conv_w_out, peer_w_q, keys_t, peer_u, peer_v, const, dft,
            y_out, new_states, mod_rows):
    ctx = ExitStack()
    with ctx:
        def sb(name, shape, dt=F32):
            return ctx.enter_context(nc.sbuf_tensor(name, shape, dt))

        def sem(name):
            return ctx.enter_context(nc.semaphore(name))

        def per_stage(name, n):
            return [sem(f"{name}{i}") for i in range(n)]

        x = sb("x", [P, BLOCKS, D])
        work = sb("work", [P, 5120 + (NQ + AHEAD) * 256])
        hT_t = sb("hT", [P, KT * T])
        bc = sb("bc", [P, 6, D])
        ring = sb("ring", [P, 4 * 4096])
        diag = sb("diag", [P, TOPK, P])
        keep = sb("keep", [P, C_KEEP])
        small = sb("small", [P, 1536])
        zero_t = sb("zero_t", [P, P])
        qcur = sb("qcur", [P, 2, P])
        stat = sb("stat", [P, 96])
        idx_cur = sb("idx_cur", [P, 2, 2, TOPK], U32)
        dots = sb("dots", [P, 2, TOPK])
        bank = ctx.enter_context(nc.psum_tensor("bank", [P, 8, 512], F32))

        ident = keep[:, C_IDENT:C_IDENT + P]
        iota = keep[:, C_IOTA:C_IOTA + TOPK]
        pos = [keep[:, C_POS + i:C_POS + i + 1] for i in range(4)]
        hT = hT_t[:, :].rearrange("p (k t) -> p k t", k=KT)
        h_tok = work[:, 0:BLOCKS * D].rearrange("p (b d) -> p b d", b=BLOCKS)

        rows = work[0:2, 9728:9728 + 6 * D]
        gain_rows = hT_t[0:2, 0:2 * D]
        cond = stat[:, 0:2 * KT].rearrange("p (k c) -> p k c", k=KT)

        k_tok = work[:, 0:5 * RW].rearrange("p (b n) -> p b n", b=BLOCKS)
        v_tok = work[:, 5 * RW:10 * RW].rearrange("p (b n) -> p b n", b=BLOCKS)
        gates = work[:, 10 * RW:15 * RW].rearrange("p (b n) -> p b n", b=BLOCKS)
        qT = work[:, 15 * RW:20 * RW].rearrange("p (h t) -> p h t", h=HEADS)
        dft_p = work[:, 20 * RW:20 * RW + 512]
        xf = x[:, :, :].rearrange("p b d -> p (b d)")
        kT = xf[:, 0:5 * RW].rearrange("p (h t) -> p h t", h=HEADS)
        fT = xf[:, 5 * RW:5 * RW + 2 * T].rearrange("p (c t) -> p c t", c=2)
        bcf = bc[:, :, :].rearrange("p a d -> p (a d)")
        s_b = bcf[:, 0:4 * RW].rearrange("p (c n) -> p c n", c=LATENT)
        s_f = bcf[:, 4 * RW:5 * RW]
        diagf = diag[:, :, :].rearrange("p k t -> p (k t)")
        decay = diagf[:, 0:RW]
        rope = diagf[:, RW:RW + 2 * LATENT * 64].rearrange("p (w b c f) -> p w b c f", w=2, b=LATENT, c=2)
        rel = diagf[:, RW + 512:RW + 768]
        mask = diagf[:, RW + 768:RW + 1024]
        over = ring[:, 8192:16384]
        fmix = over[:, 0:2560].rearrange("p (b c w f) -> p b c w f", b=BLOCKS, c=2, w=2)
        att = over[:, 2560:2560 + RW]
        kz = [over[:, 3328 + i * RW:3328 + (i + 1) * RW] for i in range(2)]
        o1 = over[:, 4864:4864 + RW]
        o2 = over[:, 5632:5632 + RW]
        rot = [over[:, 6400 + i * HALF:6400 + (i + 1) * HALF] for i in range(2)]
        rot_t = over[:, 7168:7168 + 192]
        e_rel = [small[:, 0:RW], small[:, RW:2 * RW]]
        new_s = [small[:, i * RW:(i + 1) * RW] for i in range(2)]
        lg = stat[:, 16:28]
        dec_t = [stat[:, 28:40], stat[:, 40:52], stat[:, 52:64]]
        g_chunk = stat[:, 64:76]
        xi_zeta = sb("xi_zeta", [P, 4, HEADS])
        XI_F, ZETA_F, XI_B, ZETA_B = range(4)
        hstat = sb("hstat", [P, 4, HEADS])
        tok_ss = sb("tok_ss", [P, 8])
        tok_rs = sb("tok_rs", [P, 8])
        warm = sb("warm", [P, 5])

        u_pad = work[:, 0:KT * UW].rearrange("p (k t) -> p k t", k=KT)
        y_conv = work[:, KT * UW:KT * (UW + YW)].rearrange("p (k t) -> p k t", k=KT)
        w0 = KT * (UW + YW)
        sig = [work[:, w0 + i * T:w0 + (i + 1) * T] for i in range(2)]
        ln_rs = work[:, w0 + 2 * T:w0 + 3 * T]
        sq = [work[:, w0 + (3 + i) * T:w0 + (4 + i) * T] for i in range(2)]
        cols = small[:, 0:KT * (TAPS + 3)].rearrange("p (k c) -> p k c", k=KT)
        mean_w = small[:, 512:640]
        taps = bcf[:, 0:TAPS * P].rearrange("p (k t) -> p k t", k=TAPS)
        prod = [work[:, 14848 + i * 512:14848 + (i + 1) * 512] for i in range(2)]

        qP = work[:, 5120:5120 + (NQ + AHEAD) * 256]
        keys = bcf[:, 0:(PHEADS + AHEAD) * 256]
        k1 = (PHEADS + AHEAD) * 256
        idx_all = bcf[:, k1:k1 + (NQ + AHEAD) * TOPK].bitcast(U32)
        g_all = bcf[:, k1 + (NQ + AHEAD) * TOPK:k1 + 2 * (NQ + AHEAD) * TOPK]
        wide_w = [ring[:, i * KT * QC:(i + 1) * KT * QC].rearrange("p (k n) -> p k n", k=KT) for i in range(2)]
        u_rows = [ring[:, 4096 + s * D:4096 + (s + 1) * D] for s in range(U_RING)]
        v_rows = [ring[:, 8192 + s * D:8192 + (s + 1) * D] for s in range(V_RING)]
        ada_raw = [hT_t[0:2, 4 * D + i * QC:4 * D + (i + 1) * QC] for i in range(2)]
        ada_fix = hT_t[0:96, 4 * D + 2 * QC:5 * D].rearrange("p (a n) -> p a n", a=4)
        peer_out = hT_t[:, :].rearrange("p (b d) -> p b d", b=BLOCKS)
        left = small[:, 0:256].rearrange("p (s k) -> p s k", s=2)
        cand = small[:, 256:512]
        cand_left = small[:, 512:768]
        onehot = small[:, 768:1280].rearrange("p (s k a) -> p s k a", s=2, k=TOPK)
        side_v = small[:, 1280:1312].rearrange("p (s k) -> p s k", s=2)
        side_i = small[:, 1312:1344].bitcast(U32).rearrange("p (s k) -> p s k", s=2)
        top_v = small[:, 1344:1360]
        top_i = small[:, 1360:1376].bitcast(U32)
        top_e = small[:, 1376:1392]
        pair = small[:, 1392:1424].bitcast(U32).rearrange("p (s k) -> p s k", s=2)
        part_i = small[:, 1424:1456].rearrange("p (s k) -> p s k", s=2)
        top_n = small[:, 1456:1457]
        top_s = small[:, 1457:1458]
        top_r = small[:, 1458:1459]
        act16 = small[:, 1460:1476]
        wgt = small[:, 1476:1492]

        cond_in = sem("cond_in")
        loaded = sem("loaded")
        even_consts = sem("even_consts")
        slot_in = per_stage("slot_in", 4)
        cond_ready = sem("cond_ready")
        ada_sums = sem("ada_sums")
        ada_taken = sem("ada_taken")
        rows_ready = sem("rows_ready")
        rows_out = sem("rows_out")
        ab_in = per_stage("ab_in", 5)
        gate_in = per_stage("gate_in", 4)
        squares = sem("squares")
        mean_sq = sem("mean_sq")
        roots = sem("roots")
        h_ready = per_stage("h_ready", 4)
        h_turned = per_stage("h_turned", 4)
        hT_ready = per_stage("hT_ready", 4)
        x_done = per_stage("x_done", 4)
        dve = Count(sem("dve_steps"))
        act_own = Count(sem("act_steps"))
        dec_ax = sem("dec_ax"); dec_e = sem("dec_e"); dec_u = sem("dec_u"); dec_l = sem("dec_l")
        lg_ready = sem("lg_ready"); exps_ready = sem("exps_ready")
        proj = sem("proj")
        taken_a = sem("taken_a")
        taken_v = sem("taken_v")
        qk_turned = sem("qk_turned")
        qkT_ready = sem("qkT_ready")
        f_proj = sem("f_proj"); fT_ready = sem("fT_ready")
        fmix_sums = sem("fmix_sums"); fmix_ready = sem("fmix_ready")
        fseq_sums = sem("fseq_sums"); fseq_ready = sem("fseq_ready")
        kz_ready = sem("kz_ready"); upd_sums = sem("upd_sums"); state_ready = sem("state_ready")
        att_sums = sem("att_sums"); att_ready = sem("att_ready")
        ret_sums = sem("ret_sums"); ret_var = sem("ret_var"); ret_root = sem("ret_root")
        ret_taken = sem("ret_taken"); ret_ready = sem("ret_ready")
        ret_turned = sem("ret_turned"); retT_ready = sem("retT_ready")
        states_in = sem("states_in"); states_out = sem("states_out"); x_back = sem("x_back")
        conv_in = sem("conv_in"); glu_sums = sem("glu_sums"); sig_ready = sem("sig_ready")
        u_ready = sem("u_ready"); conv_ready = sem("conv_ready")
        ln_mean = sem("ln_mean"); centred = sem("centred"); sq_ready = sem("sq_ready")
        sq_used = sem("sq_used"); ln_var = sem("ln_var"); ln_ve = sem("ln_ve"); ln_root = sem("ln_root")
        normed = sem("normed"); swish_ready = sem("swish_ready")
        tap_diag = sem("tap_diag"); tap_used = sem("tap_used"); pe_y = sem("pe_y")
        ada2_sums = sem("ada2_sums"); ada2_raw = sem("ada2_raw"); ada2_out = per_stage("ada2_out", 2)
        ada2_in = sem("ada2_in"); ada2_fixed = sem("ada2_fixed")
        out_sums = per_stage("out_sums", LAYERS)
        out_taken = per_stage("out_taken", LAYERS)
        wq_sums = per_stage("wq_sums", LAYERS); q_ready = per_stage("q_ready", LAYERS)
        keys_in = per_stage("keys_in", LAYERS)
        q_head = per_stage("q_head", LAYERS); scores = per_stage("scores", LAYERS)
        top_ready = per_stage("top_ready", LAYERS); exp_ready = per_stage("exp_ready", LAYERS)
        scores_read = per_stage("scores_read", LAYERS)
        idx_ready = per_stage("idx_ready", LAYERS); idx_staged = per_stage("idx_staged", 2)
        w_in = per_stage("w_in", 2)
        u_in = per_stage("u_in", U_RING); v_in = per_stage("v_in", V_RING)
        u_free = per_stage("u_free", LAYERS); v_free = per_stage("v_free", LAYERS)
        gelu_ready = per_stage("gelu_ready", LAYERS)
        wgt_ready = per_stage("wgt_ready", LAYERS); diag_ready = per_stage("diag_ready", LAYERS)
        peer_steps = per_stage("peer_steps", LAYERS)
        block_out = per_stage("block_out", LAYERS)
        passed_v = sem("passed_v"); passed_a = sem("passed_a"); passed_p = sem("passed_p")
        y_ready = sem("y_ready"); y_stored = sem("y_stored")

        def tall(w, c0, n):
            return w[:, c0:c0 + n].rearrange("(k p) n -> p k n", p=P)

        def slot(s, n):
            return ring[:, s * 4096:s * 4096 + KT * n].rearrange("p (k n) -> p k n", k=KT)

        chunks = []

        def chunk(parts, s, done, after=None):
            chunks.append((parts, s, done, after))
            return len(chunks) - 1

        CH = 512
        ADA = 6 * D // CH
        ada_c = [chunk([(slot(c % 4, CH), tall(ada_w[0], c * CH, CH))], c % 4, (ada_sums, c + 1)) for c in range(ADA)]
        ab_c = [chunk([(slot(c % 2, HALF), tall(ab_w_in, c * HALF, HALF))], c % 2, (proj, 5 * c + 5))
                for c in range(8)]
        f_c = chunk([(slot(0, 256), tall(ab_w_in, 8 * HALF, 256))], 0, (f_proj, 2))
        dft_c = chunk([(ring[:, 4096:8192].rearrange("p (w b n) -> p w b n", w=2, b=LATENT), dft)], 1, (fseq_sums, 1))
        wo0_c = [chunk([(slot(c, CH), tall(ab_w_out, c * CH, CH))], c, (out_sums[0], 2 * BLOCKS - 1 + c)) for c in range(2)]
        cin_c = [chunk([(slot(c, CH)[:, :, 256 * i:256 * i + 256], tall(conv_w_in, i * D + 256 * c, 256))
                        for i in range(2)], c, (glu_sums, 2 * c + 2),
                       (ab_in[2], 64)) for c in range(4)]
        before_cin = cin_c[0]
        wo1_c = [chunk([(slot(c, CH), tall(conv_w_out, c * CH, CH))], c, (out_sums[1], 2 * BLOCKS - 1 + c)) for c in range(2)]
        landed_at, so_far = [], [0] * 4
        for parts, s, _, _ in chunks:
            so_far[s] += 16 * len(parts)
            landed_at.append((slot_in[s], so_far[s]))

        def arrived(eng, c):
            eng.wait_ge(*landed_at[c])

        items = [(c, b) for c in range(8) for b in range(BLOCKS)]
        takes, na, nv = [], 0, 0
        for c, b in items:
            if c < 4 and b > 0:
                nv += 1
                takes.append((taken_v, nv))
            else:
                na += 1
                takes.append((taken_a, na))
        updates = [("b", 4), ("b", 3), ("b", 2), ("b", 0), ("f", 0), ("f", 1), ("f", 2), ("f", 3)]
        order = [("u", 0), ("u", 1), ("u", 2), ("u", 3), ("u", 4), ("a", 0), ("a", 1), ("u", 5),
                 ("a", 2), ("u", 6), ("a", 3), ("u", 7), ("a", 4)]
        segs = [(0, P, 0, PAD, 0), (P, LATENT * P, LAT_Y, P + 3 * PAD, 1)]

        def heads3(ap):
            return ap.rearrange("p (b h i) -> p b h i", b=2, h=3)

        def banks3(b0):
            return bank[:, b0:b0 + 2, 0:HALF].rearrange("p b (h i) -> p b h i", h=3)

        def wide(ap, n=DK):
            return ap.rearrange("p (b h) -> p b h", b=2).unsqueeze(3).to_broadcast([P, 2, 3, n])

        def peer_loops(eng, l, two_heads):
            def whole(b0, b1, what):
                with eng.Fori(b0, b1) as b:
                    two_heads(b, 0, what, True)
                    with eng.Fori(1, PHEADS // 2) as h2:
                        two_heads(b, h2, what, False)

            two_heads(0, 0, "queries", True)
            with eng.Fori(1, (PHEADS - AHEAD) // 2) as h2:
                two_heads(0, h2, "queries", False)
            two_heads(0, (PHEADS - AHEAD) // 2, None, False)
            if l == 0:
                whole(1, 1 + ADA2 // PHEADS, "ada")
                whole(1 + ADA2 // PHEADS, BLOCKS, None)
            else:
                whole(1, BLOCKS, None)

        def part(i, n):
            return slice(i * n, (i + 1) * n) if isinstance(i, int) else bass.ds(i * n, n)

        block = ctx.enter_context(nc.Block())

        @block.sync
        def _(sp):
            def peer_weights(l):
                sp.wait_ge(out_sums[l], 2 * BLOCKS - 1)
                for h in range(2):
                    sp.dma_start(wide_w[h], tall(peer_w_q[l], h * QC, QC)).then_inc(w_in[h], 16)
                with sp.Fori(1, PHEADS // 2) as h2:
                    for par in range(2):
                        h = h2 * 2 + par
                        sp.wait_ge(wq_sums[l], h * 2 - 2)
                        sp.dma_start(wide_w[par], peer_w_q[l][:, bass.ds(h * QC, QC)].rearrange("(k p) n -> p k n", p=P))\
                            .then_inc(w_in[par], 16)
                if l == 1:
                    return
                sp.wait_ge(wq_sums[0], 2 * PHEADS)
                for j in range(2):
                    sp.dma_start(wide_w[j], tall(ada_w[1], j * QC, QC)).then_inc(w_in[j], 16)
                with sp.Fori(1, ADA2 // 2) as j2:
                    for par in range(2):
                        j = j2 * 2 + par
                        sp.wait_ge(ada2_sums, j - 1)
                        sp.dma_start(wide_w[par], ada_w[1][:, bass.ds(j * QC, QC)].rearrange("(k p) n -> p k n", p=P))\
                            .then_inc(w_in[par], 16)
                        sp.wait_ge(ada2_raw, j)
                        sp.dma_start(mod_rows[1][:, bass.ds(j * QC - 2 * QC, QC)], ada_raw[par]).then_inc(ada2_out[par], 16)
                for par in range(2):
                    j = ADA2 - 2 + par
                    sp.wait_ge(ada2_raw, j + 2)
                    sp.dma_start(mod_rows[1][:, j * QC:(j + 1) * QC], ada_raw[par]).then_inc(ada2_out[par], 16)
                for par in range(2):
                    sp.wait_ge(ada2_out[par], 16 * (ADA2 // 2 + 1))
                sp.dma_start(ada_fix[:, 0, :], mod_rows[1].rearrange("c (r n) -> (c r) n", n=P)).then_inc(ada2_in, 16)
                sp.dma_start(ada_fix[:, 1:4, :], ada_fix_in.rearrange("a p n -> p a n")).then_inc(ada2_in, 16)

            last_in_slot = {}
            for c, (parts, s, done, after) in enumerate(chunks):
                if c == before_cin:
                    peer_weights(0)
                if s in last_in_slot:
                    sp.wait_ge(*chunks[last_in_slot[s]][2])
                if after:
                    sp.wait_ge(*after)
                last_in_slot[s] = c
                for dst, src in parts:
                    sp.dma_start(dst, src).then_inc(slot_in[s], 16)
            peer_weights(1)
            for b in range(BLOCKS):
                sp.wait_ge(y_ready, b + 1)
                sp.dma_start(y_out[b * P:(b + 1) * P, :], peer_out[:, b, :]).then_inc(y_stored, 16)
            sp.wait_ge(y_stored, 16 * BLOCKS)
            sp.wait_ge(states_out, 32)

        @block.gpsimd
        def _(pool):
            def load(dst, src, s):
                nc.gpsimd.dma_start(dst, src).then_inc(s, 16)

            load(cond, cond_t, cond_in)
            load(rows, ada_b[0:1, :].to_broadcast([2, 6 * D]), loaded)
            load(keep[:, :], const[:, 0:C_KEEP], loaded)
            load(gain_rows, norm_gain[:, 0:2 * D].to_broadcast([2, 2 * D]), loaded)
            load(dec_t[0], decays.to_broadcast([P, 2 * HEADS]), loaded)
            load(x[:, :, :], x_in.rearrange("(b p) d -> p b d", p=P), loaded)
            load(diagf[:, RW:RW + 512], const[:, C_ROPE:C_ROPE + 512], even_consts)
            load(diagf[:, RW + 512:RW + 1024], const[:, C_REL:C_REL + 512], even_consts)

            def norm_rows(s):
                l, sub = s // 2, s % 2
                for kind in range(2):
                    for i, r in enumerate((3 * sub + 1, 3 * sub)):
                        load(bc[:, 2 * i + kind, :], mod_rows[l, kind:kind + 1, r * D:(r + 1) * D].to_broadcast([P, D]), ab_in[s])

            def gate_rows(s):
                l, sub = s // 2, s % 2
                for kind in range(2):
                    r = 3 * sub + 2
                    load(bc[:, 4 + kind, :], mod_rows[l, kind:kind + 1, r * D:(r + 1) * D].to_broadcast([P, D]), gate_in[s])

            for i, at in enumerate((slice(0, 2 * D), slice(2 * D, 6 * D))):
                pool.wait_ge(rows_ready, i + 1)
                nc.gpsimd.dma_start(mod_rows[0][:, at], rows[:, at]).then_inc(rows_out, 16)
                pool.wait_ge(rows_out, 16 * (i + 1))
                (norm_rows, gate_rows)[i](0)
            pool.wait_ge(h_ready[0], BLOCKS)
            for dst, i in ((s_f, 0), (s_b[:, LATENT - 1, :], 1)):
                load(dst.rearrange("p (h e) -> p h e", h=HEADS), states[i].rearrange("h d e -> d h e"), states_in)
            load(dft_p, const[:, C_DFTF:C_DFTF + 512], even_consts)
            pool.wait_ge(state_ready, 5)
            for i in range(2):
                nc.gpsimd.dma_start(new_states[i].rearrange("h d e -> d h e"),
                                    new_s[i].rearrange("p (h e) -> p h e", h=HEADS)).then_inc(states_out, 16)
            pool.wait_ge(ret_sums, BLOCKS)
            pool.wait_ge(fmix_ready, BLOCKS)
            load(x[:, :, :], x_in.rearrange("(b p) d -> p b d", p=P), x_back)
            norm_rows(1)

            for l in range(LAYERS):
                if l == 1:
                    pool.wait_ge(ada2_fixed, 1)
                    nc.gpsimd.dma_start(mod_rows[1].rearrange("c (r n) -> (c r) n", n=P), ada_fix[:, 0, :]).then_inc(rows_out, 16)
                    pool.wait_ge(rows_out, 48)
                    pool.wait_ge(block_out[0], BLOCKS + 1)
                    norm_rows(2)
                    load(cols, conv_cols, conv_in)
                    pool.wait_ge(x_done[1], BLOCKS)
                    gate_rows(2)
                    pool.wait_ge(tap_used, PE_TILES * TAPS)
                    norm_rows(3)
                pool.wait_ge(x_done[2 * l], BLOCKS)
                gate_rows(2 * l + 1)
                pool.wait_ge(h_ready[2 * l + 1], BLOCKS)
                load(keys[:, 0:PHEADS * 256], keys_t[l], keys_in[l])
                load(keys[:, PHEADS * 256:], keys_t[l][:, 0:AHEAD * 256], keys_in[l])
                pool.wait_ge(out_sums[l], 2 * BLOCKS)

                def gather(n, par, table, rows_, free, landed, which):
                    idx = idx_cur[:, which, par, :]
                    nc.gpsimd.tensor_copy(idx, idx_all[:, part(n, TOPK)]).then_inc(idx_staged[which], 1)
                    apart(pool, passed_p, idx_staged[which], l * NQ + n + 1)
                    for k in range(TOPK):
                        apart(pool, passed_p, free[l], n * TOPK + k + 1 + (TOPK - V_RING if which else 0))
                        nc.gpsimd.indirect_dma_start(
                            rows_[k % len(rows_)], None, table,
                            bass.IndirectOffsetOnAxis(ap=idx[:, k:k + 1], axis=0),
                        ).then_inc(landed[k % len(rows_)], 16)

                def gather_u(n, par):
                    apart(pool, passed_p, idx_ready[l], n + 1)
                    gather(n, par, peer_u, u_rows, u_free, u_in, 0)

                def gather_v(n, par):
                    gather(n, par, peer_v, v_rows, v_free, v_in, 1)

                gather_u(0, 0)
                with pool.Fori(0, NQ // 2 - 1) as n2:
                    for par in range(2):
                        gather_u(n2 * 2 + par + 1, 1 - par)
                        gather_v(n2 * 2 + par, par)
                gather_u(NQ - 1, 1)
                gather_v(NQ - 2, 0)
                gather_v(NQ - 1, 1)
            pool.wait_ge(x_done[3], BLOCKS)
            load(bc[:, 0, :], final_gain.to_broadcast([P, D]), ab_in[4])

        @block.tensor
        def _(pe):
            def mm(out, lhsT, rhs, start, stop, **kw):
                return nc.tensor.matmul(out, lhsT, rhs, start=start, stop=stop, **kw)

            pe.wait_ge(cond_ready, 1)
            for c in range(ADA):
                arrived(pe, ada_c[c])
                if c >= 4:
                    pe.wait_ge(ada_taken, c - 3)
                for k in range(KT):
                    last = mm(bank[0:2, c % 4, :], cond[:, k, :], slot(c % 4, CH)[:, k, :], k == 0, k == KT - 1)
                last.then_inc(ada_sums, 1)

            def turn(s):
                for b in range(BLOCKS):
                    pe.wait_ge(h_ready[s], b + 1)
                    if b >= 4:
                        pe.wait_ge(hT_ready[s], b - 3)
                    b0 = 2 * (b % 4)
                    for k in range(KT):
                        last = nc.tensor.transpose(bank[:, b0 + k // 4, (k % 4) * P:(k % 4 + 1) * P],
                                                   h_tok[:, b, k * P:(k + 1) * P], ident)
                    last.then_inc(h_turned[s], 1)
                pe.wait_ge(hT_ready[s], BLOCKS)

            def project_out(l, b, cs, banks):
                for c in range(2):
                    if b == 0:
                        arrived(pe, cs[c])
                    for k in range(KT):
                        last = mm(bank[:, banks[c], :], hT[:, k, b * P:(b + 1) * P], slot(c, CH)[:, k, :], k == 0, k == KT - 1)
                    last.then_inc(out_sums[l], 1)

            def peer(l):
                turn(2 * l + 1)
                def queries(h, par):
                    pe.wait_ge(w_in[par], (h + (2 - par)) * 8 + l * (PHEADS + ADA2) * 8)
                    for half in range(2):
                        if not isinstance(h, int) or h:
                            pe.wait_ge(q_ready[l], h * 2 + half - 1)
                        b0 = (2, 5)[half]
                        w = wide_w[par][:, :, half * P:(half + 1) * P]
                        for k in range(KT):
                            mm(bank[:, b0, :], w[:, k, :], hT[:, k, 0:512], k == 0, k == KT - 1)
                        for k in range(KT):
                            last = mm(bank[:, b0 + 1, 0:P], w[:, k, :], hT[:, k, 512:T], k == 0, k == KT - 1)
                        last.then_inc(wq_sums[l], 1)

                def ada_chunk(j, par):
                    pe.wait_ge(w_in[par], (j + (2 - par)) * 8 + PHEADS * 8)
                    pe.wait_ge(ada2_raw, j + 1)
                    for k in range(KT):
                        last = mm(bank[0:2, 7, 0:QC], cond[:, k, :], wide_w[par][:, k, :], k == 0, k == KT - 1)
                    last.then_inc(ada2_sums, 1)

                def score(h):
                    for s in range(2):
                        last = mm(bank[:, 4, s * P:(s + 1) * P], qcur[:, s, :],
                                  keys[:, bass.ds(h * 256 + s * P, P)] if not isinstance(h, int)
                                  else keys[:, h * 256 + s * P:h * 256 + (s + 1) * P], True, True)
                    last.then_inc(scores[l], 1)

                for m in range(AHEAD):
                    queries(m, m)
                    if m == 0:
                        pe.wait_ge(keys_in[l], 32)
                    pe.wait_ge(q_head[l], m + 1)
                    if m:
                        pe.wait_ge(scores_read[l], m)
                    score(m)

                def open_block(b):
                    pe.wait_ge(block_out[l], b + 1)
                    for i in range(8):
                        mm(bank[:, i // 4, (i % 4) * P:(i % 4 + 1) * P], zero_t[:, :], ident, i % 4 == 0, False,
                           skip_group_check=True)

                def front(b, h, par, what):
                    n = b * PHEADS + h
                    if what == "queries":
                        queries(h + AHEAD, par)
                    pe.wait_ge(q_head[l], n + AHEAD + 1)
                    pe.wait_ge(scores_read[l], n + AHEAD)
                    score(h + AHEAD)
                    if what == "ada":
                        ada_chunk(n - PHEADS, par)

                def sums(b, h):
                    n = b * PHEADS + h
                    for k in range(TOPK):
                        pe.wait_ge(diag_ready[l], n * TOPK + k + 1)
                        pe.wait_ge(v_in[k % V_RING], (l * NQ * 2 + n * 2 + k // V_RING + 1) * 16)
                        for half in range(2):
                            last = mm(bank[:, half, :], diag[:, k, :],
                                      v_rows[k % V_RING][:, half * 512:(half + 1) * 512], False, False,
                                      skip_group_check=True)
                        last.then_inc(v_free[l], 1)

                def two_heads(b, h2, what, opens=False, next_front=True):
                    for par in range(2):
                        h = h2 * 2 + par
                        if par == 0:
                            front(b, h + 1, 1, what[0])
                        elif next_front:
                            front(*((b + 1, 0) if isinstance(h, int) and h == PHEADS - 1 else (b, h + 1)), 0, what[1])
                        if opens and par == 0:
                            open_block(b)
                        sums(b, h)

                ada = "ada" if l == 0 else None
                front(0, 0, 0, "queries")
                for h2 in range(PHEADS // 2):
                    whats = ["queries" if 2 * h2 + i + AHEAD < PHEADS else ada if 2 * h2 + i == PHEADS else None for i in (1, 2)]
                    two_heads(0, h2, whats, opens=h2 == 0)
                with pe.Fori(1, ADA2 // PHEADS) as b:
                    two_heads(b, 0, (ada, ada), opens=True)
                    with pe.Fori(1, PHEADS // 2 - 1) as h2:
                        two_heads(b, h2, (ada, ada))
                    two_heads(b, PHEADS // 2 - 1, (ada, ada))
                for b, what in ((ADA2 // PHEADS, ada), (BLOCKS - 1, None)):
                    two_heads(b, 0, (what, what), opens=True)
                    with pe.Fori(1, PHEADS // 2 - 1) as h2:
                        two_heads(b, h2, (what, what))
                    two_heads(b, PHEADS // 2 - 1, (what, None), next_front=b < BLOCKS - 1)

            pe.wait_ge(ada_taken, ADA)
            turn(0)
            def project(i):
                c, b = items[i]
                if b == 0:
                    arrived(pe, ab_c[c])
                if i >= 4:
                    pe.wait_ge(*takes[i - 4])
                for k in range(KT):
                    last = mm(bank[:, i % 4, 0:HALF], hT[:, k, b * P:(b + 1) * P], slot(c % 2, HALF)[:, k, :],
                              k == 0, k == KT - 1)
                last.then_inc(proj, 1)

            def turn_qk(i):
                c, b = items[i]
                pe.wait_ge(*takes[i])
                if i >= 4:
                    pe.wait_ge(qkT_ready, i - 3)
                src = rot[i % 2] if c < 2 else k_tok[:, b, (c - 2) * HALF:(c - 1) * HALF]
                for h in range(3):
                    last = nc.tensor.transpose(bank[:, 4 + i % 4, h * P:(h + 1) * P], src[:, h * P:(h + 1) * P], ident)
                last.then_inc(qk_turned, 1)

            for i in range(len(items)):
                project(i)
                if 0 <= i - 1 < 4 * BLOCKS:
                    turn_qk(i - 1)
            arrived(pe, f_c)
            for c in range(2):
                pe.wait_ge(*takes[36 + 2 * c])
                pe.wait_ge(*takes[37 + 2 * c])
                for t0, n, bk in ((0, 512, 2 * c), (512, P, 2 * c + 1)):
                    for k in range(KT):
                        last = mm(bank[:, bk, 0:n], slot(0, 256)[:, k, c * P:(c + 1) * P], hT[:, k, t0:t0 + n],
                                  k == 0, k == KT - 1)
                last.then_inc(f_proj, 1)
            pe.wait_ge(qkT_ready, 4 * BLOCKS)
            pe.wait_ge(even_consts, 48)
            for b in range(BLOCKS):
                pe.wait_ge(fT_ready, 2)
                for c in range(2):
                    last = mm(bank[:, b, c * 256:(c + 1) * 256] if b < 4 else bank[:, 4, c * 256:(c + 1) * 256],
                              fT[:, c, b * P:(b + 1) * P], dft_p[:, 0:256], True, True)
                last.then_inc(fmix_sums, 1)
            pe.wait_ge(fmix_ready, BLOCKS)
            arrived(pe, dft_c)
            dft_s = ring[:, 4096:8192].rearrange("p (w b n) -> p w b n", w=2, b=LATENT)
            for c in range(2):
                for w in range(2):
                    for b in range(LATENT):
                        mm(bank[:, c, :], fmix[:, b + 1, c, w, :], dft_s[:, w, b, :], w + b == 0, w == 1 and b == LATENT - 1)
                for w in range(2):
                    last = mm(bank[:, 2 + c, 0:P], fmix[:, 0, c, w, :], dft_p[:, 256 + w * P:256 + (w + 1) * P], w == 0, w == 1)
            last.then_inc(fseq_sums, 1)
            pe.wait_ge(fseq_ready, 1)

            for what, j in order:
                if what == "u":
                    b = updates[j][1]
                    pe.wait_ge(kz_ready, j + 1)
                    if j > 4:
                        pe.wait_ge(out_taken[0], 2 * (j - 4))
                    if j >= 1:
                        pe.wait_ge(state_ready, j)
                    for h in range(HEADS):
                        last = mm(bank[:, h // 3, (h % 3) * P:(h % 3 + 1) * P], kz[j % 2][:, h * P:(h + 1) * P],
                                  v_tok[:, b, h * P:(h + 1) * P], True, True)
                    last.then_inc(upd_sums, 1)
                    continue
                b = j
                tok = slice(b * P, (b + 1) * P)
                pe.wait_ge(state_ready, {0: 5, 1: 5, 2: 6, 3: 7, 4: 8}[b])
                pe.wait_ge(states_in, 32)
                if b:
                    pe.wait_ge(retT_ready, b)
                if b > 1:
                    pe.wait_ge(out_taken[0], 2 * (b - 1))
                for h in range(HEADS):
                    last = mm(bank[:, h // 3, (h % 3) * P:(h % 3 + 1) * P], kT[:, h, tok], qT[:, h, tok], True, True)
                last.then_inc(att_sums, 1)
                if b:
                    for h in range(HEADS):
                        at = slice((h % 3) * P, (h % 3 + 1) * P)
                        mm(bank[:, 4 + h // 3, at], qT[:, h, tok], s_f[:, h * P:(h + 1) * P], True, True)
                        mm(bank[:, 6 + h // 3, at], qT[:, h, tok], s_b[:, b - 1, h * P:(h + 1) * P], True, True)
                pe.wait_ge(att_ready, b + 1)
                for h in range(HEADS):
                    last = mm(bank[:, 2 + h // 3, (h % 3) * P:(h % 3 + 1) * P], att[:, h * P:(h + 1) * P],
                              v_tok[:, b, h * P:(h + 1) * P], True, True)
                last.then_inc(ret_sums, 1)
                if b:
                    project_out(0, b - 1, wo0_c, (0, 1))
                pe.wait_ge(ret_ready, b + 1)
                for h in range(HEADS):
                    last = nc.tensor.transpose(bank[:, 2 + h // 3, (h % 3) * P:(h % 3 + 1) * P],
                                               gates[:, b, h * P:(h + 1) * P], ident)
                last.then_inc(ret_turned, 1)
            pe.wait_ge(retT_ready, BLOCKS)
            pe.wait_ge(out_taken[0], 2 * LATENT)
            project_out(0, LATENT, wo0_c, (0, 1))
            pe.wait_ge(out_taken[0], 2 * BLOCKS)
            peer(0)

            turn(2)
            for f in range(KT):
                if f % 2 == 0:
                    arrived(pe, cin_c[f // 2])
                if f >= 2:
                    pe.wait_ge(u_ready, f - 1)
                w = slot(f // 2, CH)
                for part in range(2):
                    at = part * 256 + (f % 2) * P
                    for t0, n, _, _, kind in segs:
                        for k in range(KT):
                            last = mm(bank[:, 4 * (f % 2) + 2 * part + kind, 0:n], w[:, k, at:at + P],
                                      hT[:, k, t0:t0 + n], k == 0, k == KT - 1)
                last.then_inc(glu_sums, 1)
            for i in range(PE_TILES):
                f = KT - PE_TILES + i
                pe.wait_ge(u_ready, f + 1)
                for tap in range(TAPS):
                    pe.wait_ge(tap_diag, i * TAPS + tap + 1)
                    for t0, n, _, u0, kind in segs:
                        last = mm(bank[:, 2 * i + kind, 0:n], taps[:, tap, :], u_pad[:, f, u0 - PAD + tap:u0 - PAD + tap + n],
                                  tap == 0, tap == TAPS - 1)
                    last.then_inc(tap_used, 1)
            for f in range(KT):
                if f < KT - PE_TILES:
                    pe.wait_ge(conv_ready, f + 1)
                else:
                    pe.wait_ge(pe_y, PE_TILES)
                for t0, n, y0, _, kind in segs:
                    last = mm(bank[:, 4 + kind, 0:n], mean_w, y_conv[:, f, y0:y0 + n], f == 0, f == KT - 1)
            last.then_inc(ln_mean, 1)
            for f in range(KT):
                pe.wait_ge(sq_ready, f + 1)
                for t0, n, _, _, kind in segs:
                    last = mm(bank[:, 6 + kind, 0:n], mean_w, sq[f % 2][:, t0:t0 + n], f == 0, f == KT - 1)
                last.then_inc(sq_used, 1)
            pe.wait_ge(swish_ready, KT)
            for b in range(BLOCKS):
                if b >= 2:
                    pe.wait_ge(out_taken[1], 2 * b - 2)
                project_out(1, b, wo1_c, (b % 2 * 2, b % 2 * 2 + 1))
            pe.wait_ge(out_taken[1], 2 * BLOCKS)
            peer(1)

        @block.scalar
        def _(act):
            def f(out, in_, func=ACT.Copy, **kw):
                return nc.scalar.activation(out, in_, func, **kw)

            act.wait_ge(cond_in, 16)
            f(cond, cond, ACT.Silu).then_inc(cond_ready, 1)
            act.wait_ge(loaded, 16 * 5)
            act.wait_ge(dec_ax, 1)
            f(dec_t[1], dec_t[1], ACT.Exp, scale=-1.0).then_inc(dec_e, 1)
            act.wait_ge(dec_u, 1)
            f(lg, dec_t[2], ACT.Ln).then_inc(dec_l, 1)
            act.wait_ge(lg_ready, 1)
            act.wait_ge(even_consts, 32)
            for i in range(4):
                f(xi_zeta[:, i, :], lg[:, (i // 2) * HEADS:(i // 2 + 1) * HEADS], ACT.Exp, scale=pos[i])
            f(g_chunk, lg, ACT.Exp, scale=float(P))
            for d in range(2):
                for h in range(HEADS):
                    last = f(e_rel[d][:, h * P:(h + 1) * P], rel[:, d * P:(d + 1) * P], ACT.Exp,
                             scale=lg[:, d * HEADS + h:d * HEADS + h + 1])
            last.then_inc(exps_ready, 1)

            def norm(s):
                for b in range(BLOCKS):
                    if s:
                        act.wait_ge(x_done[s - 1], b + 1)
                    dst = h_tok[:, b, :] if s < 4 else hT_t[:, b * D:(b + 1) * D]
                    last = f(dst, x[:, b, :], ACT.Square, accum_out=tok_ss[:, b:b + 1])
                last.then_inc(squares, 1)
                act.wait_ge(mean_sq, s + 1)
                f(tok_rs[:, 0:BLOCKS], tok_ss[:, 0:BLOCKS], ACT.Sqrt).then_inc(roots, 1)

            def take_turned(s):
                for b in range(BLOCKS):
                    act.wait_ge(h_turned[s], b + 1)
                    b0 = 2 * (b % 4)
                    f(hT[:, :, b * P:(b + 1) * P], bank[:, b0:b0 + 2, :].rearrange("p b (k t) -> p (b k) t", k=4))\
                        .then_inc(hT_ready[s], 1)

            def peer(l):
                norm(2 * l + 1)
                take_turned(2 * l + 1)
                q4 = qP[:, 0:NQ * 256].rearrange("p (b f t) -> p b f t", b=BLOCKS, f=2 * PHEADS)

                def take_queries(h):
                    for half in range(2):
                        apart(act, passed_a, wq_sums[l], h * 2 + half + 1)
                        b0 = (2, 5)[half]
                        ft = h * 2 + half
                        at = slice(ft, ft + 1) if isinstance(ft, int) else bass.ds(ft, 1)
                        f(q4[:, 0:4, at, :], bank[:, b0, :].rearrange("p (b o t) -> p b o t", b=4, o=1))
                        f(q4[:, 4, at, :], bank[:, b0 + 1, 0:P].unsqueeze(1)).then_inc(q_ready[l], 1)
                    apart(act, passed_a, q_ready[l], h * 2 + 2)

                def head_in(m):
                    f(qcur[:, :, :].rearrange("p s t -> p (s t)"), qP[:, part(m, 256)]).then_inc(q_head[l], 1)

                def soft(m):
                    apart(act, passed_a, top_ready[l], m + 1)
                    f(top_e, top_v, ACT.Exp, bias=top_n, accum_out=top_s).then_inc(exp_ready[l], 1)

                for m in range(AHEAD):
                    take_queries(m)
                    if m:
                        act.wait_ge(scores[l], m)
                    head_in(m)
                for m in range(AHEAD):
                    soft(m)

                def two_heads(b, h2, what, first):
                    for par in range(2):
                        n = b * PHEADS + h2 * 2 + par
                        if what == "queries":
                            take_queries(n + AHEAD)
                        apart(act, passed_a, scores[l], n + AHEAD)
                        head_in(n + AHEAD)
                        if what == "ada":
                            j = n - PHEADS
                            apart(act, passed_a, ada2_out[par], j * 8 + (16 - 8 * par))
                            apart(act, passed_a, ada2_sums, j + 1)
                            f(ada_raw[par], bank[0:2, 7, 0:QC]).then_inc(ada2_raw, 1)
                        apart(act, passed_a, u_free[l], U_RING + (n + 1) * TOPK)
                        f(act16, dots[:, par, :], ACT.Gelu_apprx_tanh).then_inc(gelu_ready[l], 1)
                        soft(n + AHEAD)
                        apart(act, passed_a, wgt_ready[l], n + 1)
                        for k in range(TOPK):
                            act.wait_ge(v_free[l], n * TOPK + k + 1)
                            f(diag[:, k, :], ident, scale=wgt[:, k:k + 1]).then_inc(diag_ready[l], 1)
                        if first and par == 0 and not (isinstance(b, int) and b == 0):
                            close(b - 1)

                def close(b):
                    apart(act, passed_a, v_free[l], TOPK + (b + 1) * PHEADS * TOPK)
                    f(peer_out[:, part(b, 1), :].rearrange("p b d -> p (b d)"),
                      bank[:, 0:2, :].rearrange("p b d -> p (b d)")).then_inc(block_out[l], 1)

                peer_loops(act, l, two_heads)
                if l == 0:
                    act.wait_ge(rows_out, 48)
                close(BLOCKS - 1)

            norm(0)
            take_turned(0)
            act.wait_ge(rows_out, 32)
            for i in range(len(items) + 1):
                if i < len(items):
                    c, b = items[i]
                    if takes[i][0] is taken_a:
                        act.wait_ge(proj, i + 1)
                        if c < 2 and i >= 2:
                            act.wait_ge(qk_turned, i - 1)
                        cc = (c % 2) * HALF
                        dst = (rot[i % 2] if c < 2 else k_tok[:, b, cc:cc + HALF] if c < 4 else
                               v_tok[:, b, cc:cc + HALF] if c < 6 else gates[:, b, cc:cc + HALF])
                        f(dst, bank[:, i % 4, 0:HALF], ACT.Silu if c >= 6 else ACT.Copy).then_inc(taken_a, 1)
                if 0 <= i - 1 < 4 * BLOCKS:
                    c, b = items[i - 1]
                    act.wait_ge(qk_turned, i)
                    dst = qT if c < 2 else kT
                    f(dst[:, (c % 2) * 3:(c % 2) * 3 + 3, b * P:(b + 1) * P],
                      bank[:, 4 + (i - 1) % 4, 0:HALF].rearrange("p (h t) -> p h t", h=3)).then_inc(qkT_ready, 1)
            for c in range(2):
                act.wait_ge(f_proj, c + 1)
                f(fT[:, c, 0:512], bank[:, 2 * c, :])
                f(fT[:, c, 512:T], bank[:, 2 * c + 1, 0:P]).then_inc(fT_ready, 1)
            for b in range(BLOCKS):
                act.wait_ge(fmix_sums, b + 1)
                f(fmix[:, b, :, :, :].rearrange("p c w f -> p (c w f)"), bank[:, b, :]).then_inc(fmix_ready, 1)
            act.wait_ge(fseq_sums, 1)
            for c in range(2):
                f(hT[:, 6 + c, P:T], bank[:, c, :])
                last = f(hT[:, 6 + c, 0:P], bank[:, 2 + c, 0:P])
            last.then_inc(fseq_ready, 1)
            for b in range(BLOCKS):
                act.wait_ge(ret_var, b + 1)
                f(hstat[:, 2, :], hstat[:, 1, :], ACT.Sqrt).then_inc(ret_root, 1)
                act.wait_ge(ret_turned, b + 1)
                f(hT[:, 0:6, b * P:(b + 1) * P].rearrange("p (b h) t -> p b h t", b=2), banks3(2)).then_inc(retT_ready, 1)
            peer(0)

            norm(2)
            take_turned(2)
            for t in range(KT):
                act.wait_ge(glu_sums, t + 1)
                if t >= 2:
                    act.wait_ge(u_ready, t - 1)
                for t0, n, _, _, kind in segs:
                    last = f(sig[t % 2][:, t0:t0 + n], bank[:, 4 * (t % 2) + 2 + kind, 0:n], ACT.Sigmoid)
                last.then_inc(sig_ready, 1)
            for i in range(PE_TILES):
                t = KT - PE_TILES + i
                for tap in range(TAPS):
                    if i:
                        act.wait_ge(tap_used, (i - 1) * TAPS + tap + 1)
                    f(taps[:, tap, :], ident, scale=cols[:, t, tap:tap + 1]).then_inc(tap_diag, 1)
            for i in range(PE_TILES):
                t = KT - PE_TILES + i
                act.wait_ge(tap_used, (i + 1) * TAPS)
                for t0, n, y0, _, kind in segs:
                    last = f(y_conv[:, t, y0:y0 + n], bank[:, 2 * i + kind, 0:n], ACT.Identity, bias=cols[:, t, TAPS:TAPS + 1])
                last.then_inc(pe_y, 1)
            for t in range(KT):
                act.wait_ge(centred, t + 1)
                if t >= 2:
                    act.wait_ge(sq_used, t - 1)
                for t0, n, y0, _, kind in segs:
                    last = f(sq[t % 2][:, t0:t0 + n], y_conv[:, t, y0:y0 + n], ACT.Square)
                last.then_inc(sq_ready, 1)
            act.wait_ge(ln_ve, 1)
            f(ln_rs, ln_rs, ACT.Sqrt).then_inc(ln_root, 1)
            for t in range(KT):
                act.wait_ge(normed, t + 1)
                for t0, n, y0, _, kind in segs:
                    last = f(hT[:, t, t0:t0 + n], y_conv[:, t, y0:y0 + n], ACT.Silu,
                             scale=cols[:, t, TAPS + 1:TAPS + 2], bias=cols[:, t, TAPS + 2:TAPS + 3])
                last.then_inc(swish_ready, 1)
            peer(1)
            norm(4)

        @block.vector
        def _(v):
            def step(ins):
                dve.mark(ins)
                v.wait_ge(dve.sem, dve.now())

            step(v.memset(zero_t[:, :], 0.0))
            v.wait_ge(loaded, 16 * 5)
            step(v.tensor_scalar(dec_t[1], dec_t[0], -1.0, None, ALU.mult))
            v.tensor_tensor(dec_t[1], dec_t[1], dec_t[0], ALU.max).then_inc(dec_ax, 1)
            v.wait_ge(dec_e, 1)
            v.tensor_scalar(dec_t[2], dec_t[1], 1.0, None, ALU.add).then_inc(dec_u, 1)
            v.wait_ge(dec_u, 1)
            ctmp, rtmp = stat[:, 76:88], dec_t[0]
            step(v.scalar_tensor_tensor(out=ctmp, in0=dec_t[2], scalar=1.0, in1=dec_t[1], op0=ALU.subtract, op1=ALU.subtract))
            step(v.tensor_scalar(rtmp, dec_t[0], 0.0, None, ALU.min))
            v.wait_ge(dec_l, 1)
            step(v.tensor_tensor(rtmp, rtmp, lg, ALU.subtract))
            step(v.reciprocal(dec_t[2], dec_t[2]))
            step(v.tensor_tensor(ctmp, ctmp, dec_t[2], ALU.mult))
            v.tensor_tensor(lg, rtmp, ctmp, ALU.add).then_inc(lg_ready, 1)
            v.wait_ge(exps_ready, 1)
            for d in range(2):
                e3 = e_rel[d].rearrange("p (h i) -> p h i", h=HEADS)
                m3 = mask[:, d * P:(d + 1) * P].unsqueeze(1).to_broadcast([P, HEADS, P])
                step(v.tensor_tensor(e3, e3, m3, ALU.mult))
            step(v.tensor_tensor(decay, e_rel[0], e_rel[1], ALU.add))
            for i in (ZETA_F, ZETA_B):
                step(v.tensor_scalar(xi_zeta[:, i, :], xi_zeta[:, i, :], DK ** -0.5, None, ALU.mult))

            def rsqrt_mean(s):
                v.wait_ge(squares, s + 1)
                v.tensor_scalar(tok_ss[:, 0:BLOCKS], tok_ss[:, 0:BLOCKS], 1.0 / D, EPS, ALU.mult, ALU.add)\
                    .then_inc(mean_sq, 1)
                v.wait_ge(roots, s + 1)
                step(v.reciprocal(tok_rs[:, 0:BLOCKS], tok_rs[:, 0:BLOCKS]))

            def norm(s):
                rsqrt_mean(s)
                v.wait_ge(ab_in[s], 64)
                for b in range(BLOCKS):
                    kind = min(b, 1)
                    step(v.scalar_tensor_tensor(out=h_tok[:, b, :], in0=x[:, b, :], scalar=tok_rs[:, b:b + 1],
                                                in1=bc[:, kind, :], op0=ALU.mult, op1=ALU.mult))
                    v.tensor_tensor(h_tok[:, b, :], h_tok[:, b, :], bc[:, 2 + kind, :], ALU.add).then_inc(h_ready[s], 1)

            def gated(b):
                return v_tok[:, b, 0:CH], gates[:, b, 0:CH]

            def gate_projection(b):
                if b == 0:
                    v.wait_ge(gate_in[0], 32)
                v.wait_ge(ret_turned, b + 1)
                for c in range(2):
                    v.wait_ge(out_sums[0], 2 * b + c + 1)
                    v.tensor_tensor(gated(b)[c], bank[:, c, :], bc[:, 4 + min(b, 1), c * CH:(c + 1) * CH], ALU.mult)\
                        .then_inc(out_taken[0], 1)
                v.wait_ge(out_taken[0], 2 * b + 2)

            def add_projection():
                v.wait_ge(gate_in[2], 32)
                for g, (b, c) in enumerate((b, c) for b in range(BLOCKS) for c in range(2)):
                    v.wait_ge(out_sums[1], g + 1)
                    v.tensor_tensor(prod[g % 2], bank[:, g % 4, :], bc[:, 4 + min(b, 1), c * CH:(c + 1) * CH], ALU.mult)\
                        .then_inc(out_taken[1], 1)
                    v.wait_ge(out_taken[1], g + 1)
                    xs = x[:, b, c * CH:(c + 1) * CH]
                    ins = v.tensor_tensor(xs, xs, prod[g % 2], ALU.add)
                    if c == 1:
                        ins.then_inc(x_done[2], 1)
                        v.wait_ge(x_done[2], b + 1)
                    else:
                        step(ins)

            def peer(l):
                norm(2 * l + 1)
                own = Count(peer_steps[l])
                v.memset(dots[:, :, :], 0.0).then_inc(u_free[l], U_RING)
                v.memset(warm[:, 0:1], 0.0).then_inc(v_free[l], TOPK)
                v.memset(warm[:, 1:2], 0.0).then_inc(block_out[l], 1)
                if l == 0:
                    v.memset(warm[:, 2:3], 0.0).then_inc(ada2_raw, 1)
                    for i in range(2):
                        v.memset(warm[:, 3 + i:4 + i], 0.0).then_inc(ada2_out[i], 16)
                v.wait_ge(hT_ready[2 * l + 1], BLOCKS)
                own.mark(v.memset(qP[:, NQ * 256:], 0.0))


                def settle():
                    apart(v, passed_v, own.sem, own.now())

                def choose(m):
                    apart(v, passed_v, scores[l], m + 1)
                    sc = [bank[:, 4, s * P:(s + 1) * P] for s in range(2)]
                    for s in range(2):
                        own.mark(v.max(side_v[:, s, 0:8], sc[s]))
                    settle()
                    for s in range(2):
                        own.mark(v.match_replace(left[:, s, :], side_v[:, s, 0:8], sc[s], LOWEST))
                    for s in range(2):
                        ins = v.max_index(side_i[:, s, 0:8], side_v[:, s, 0:8], sc[s])
                        if s:
                            ins.then_inc(scores_read[l], 1)
                        else:
                            own.mark(ins)
                    settle()
                    for s in range(2):
                        own.mark(v.max(side_v[:, s, 8:16], left[:, s, :]))
                    settle()
                    for s in range(2):
                        own.mark(v.max_index(side_i[:, s, 8:16], side_v[:, s, 8:16], left[:, s, :]))
                    own.mark(v.tensor_tensor(cand.rearrange("p (a b) -> p a b", a=TOPK),
                                             side_v[:, 0, :].unsqueeze(2).to_broadcast([P, TOPK, TOPK]),
                                             side_v[:, 1, :].unsqueeze(1).to_broadcast([P, TOPK, TOPK]), ALU.add))
                    settle()
                    own.mark(v.max(top_v[:, 0:8], cand))
                    settle()
                    own.mark(v.match_replace(cand_left, top_v[:, 0:8], cand, LOWEST))
                    own.mark(v.tensor_scalar(top_n, top_v[:, 0:1], -1.0, None, ALU.mult))
                    own.mark(v.max_index(top_i[:, 0:8], top_v[:, 0:8], cand))
                    settle()
                    v.max(top_v[:, 8:16], cand_left).then_inc(top_ready[l], 1)
                    apart(v, passed_v, top_ready[l], m + 1)
                    own.mark(v.max_index(top_i[:, 8:16], top_v[:, 8:16], cand_left))
                    settle()
                    own.mark(v.tensor_scalar(pair[:, 0, :], top_i, 4, None, ALU.logical_shift_right))
                    own.mark(v.tensor_scalar(pair[:, 1, :], top_i, TOPK - 1, None, ALU.bitwise_and))
                    settle()
                    own.mark(v.tensor_tensor(onehot.rearrange("p s k a -> p (s k) a"),
                                             pair.rearrange("p s k -> p (s k)").unsqueeze(2).to_broadcast([P, 2 * TOPK, TOPK]),
                                             iota.unsqueeze(1).to_broadcast([P, 2 * TOPK, TOPK]), ALU.is_equal))
                    settle()
                    own.mark(v.tensor_tensor(onehot, onehot, side_i.unsqueeze(2).to_broadcast([P, 2, TOPK, TOPK]), ALU.mult))
                    settle()
                    own.mark(v.tensor_reduce(part_i.rearrange("p s k -> p (s k)"),
                                             onehot.rearrange("p s k a -> p (s k) a"), AX.X, ALU.add))
                    settle()
                    own.mark(v.scalar_tensor_tensor(out=part_i[:, 0, :], in0=part_i[:, 0, :], scalar=float(NKEYS),
                                                    in1=part_i[:, 1, :], op0=ALU.mult, op1=ALU.add))
                    apart(v, passed_v, exp_ready[l], m + 1)
                    own.mark(v.reciprocal(top_r, top_s))
                    settle()
                    at = slice(m * TOPK, (m + 1) * TOPK) if isinstance(m, int) else bass.ds(m * TOPK, TOPK)
                    own.mark(v.tensor_scalar(g_all[:, at], top_e, top_r, None, ALU.mult))
                    v.tensor_scalar(idx_all[:, at], part_i[:, 0, :], float(l * EXPERTS), None, ALU.add)\
                        .then_inc(idx_ready[l], 1)
                    settle()
                    apart(v, passed_v, idx_ready[l], m + 1)

                v.wait_ge(keys_in[l], 32)
                for m in range(AHEAD):
                    choose(m)
                before = own.n
                per = (before - 1) // AHEAD

                def two_heads(b, h2, what, first):
                    for par in range(2):
                        n = b * PHEADS + h2 * 2 + par
                        own.loop(n * per + before)
                        for k in range(TOPK):
                            apart(v, passed_v, u_in[k % U_RING],
                                  ((l * NQ + n) * (TOPK // U_RING) + k // U_RING + 1) * 16)
                            row = u_rows[k % U_RING]
                            v.scalar_tensor_tensor(out=row, in0=row, scalar=1.0,
                                                   in1=h_tok[:, (slice(b, b + 1) if isinstance(b, int) else bass.ds(b, 1)), :]
                                                   .rearrange("p b d -> p (b d)"),
                                                   op0=ALU.mult, op1=ALU.mult,
                                                   accum_out=dots[:, par, k:k + 1]).then_inc(u_free[l], 1)
                        apart(v, passed_v, gelu_ready[l], n + 1)
                        v.tensor_tensor(wgt, act16, g_all[:, part(n, TOPK)], ALU.mult).then_inc(wgt_ready[l], 1)
                        choose(n + AHEAD)
                        assert own.n == per

                peer_loops(v, l, two_heads)
                if l == 0:
                    v.wait_ge(ada2_in, 32)
                    t = ada_fix[:, 0, :]
                    step(v.tensor_tensor(t, t, ada_fix[:, 1, :], ALU.add))
                    step(v.tensor_tensor(t, t, ada_fix[:, 2, :], ALU.add))
                    v.tensor_tensor(t, t, ada_fix[:, 3, :], ALU.mult).then_inc(ada2_fixed, 1)
                v.wait_ge(gate_in[2 * l + 1], 32)
                for b in range(BLOCKS):
                    v.wait_ge(block_out[l], b + 2)
                    step(v.tensor_tensor(peer_out[:, b, :], peer_out[:, b, :], bc[:, 4 + min(b, 1), :], ALU.mult))
                    v.tensor_tensor(x[:, b, :], x[:, b, :], peer_out[:, b, :], ALU.add).then_inc(x_done[2 * l + 1], 1)
                    v.wait_ge(x_done[2 * l + 1], b + 1)

            for c in range(ADA):
                if c == ADA - 3:
                    norm(0)
                v.wait_ge(ada_sums, c + 1)
                r = rows[:, c * CH:(c + 1) * CH]
                v.tensor_tensor(r, bank[0:2, c % 4, :], r, ALU.add).then_inc(ada_taken, 1)
                if (c + 1) * CH in (2 * D, 5 * D):
                    sub = (c + 1) * CH // (3 * D)
                    r = rows[:, (3 * sub + 1) * D:(3 * sub + 2) * D]
                    v.wait_ge(ada_taken, c + 1)
                    ins = v.scalar_tensor_tensor(out=r, in0=r, scalar=1.0, in1=gain_rows[:, sub * D:(sub + 1) * D],
                                                 op0=ALU.add, op1=ALU.mult)
                    if sub == 0:
                        ins.then_inc(rows_ready, 1)
                    else:
                        dve.mark(ins)
            v.wait_ge(ada_taken, ADA)
            v.wait_ge(dve.sem, dve.now())
            v.memset(warm[:, 0:1], 0.0).then_inc(rows_ready, 1)

            rt = rot_t.rearrange("p (c h f) -> p c h f", c=2, h=3)
            for i, (c, b) in enumerate(items):
                if takes[i][0] is not taken_v:
                    continue
                v.wait_ge(proj, i + 1)
                if c < 2 and i >= 2:
                    v.wait_ge(qk_turned, i - 1)
                dst = rot[i % 2] if c < 2 else k_tok[:, b, (c - 2) * HALF:(c - 1) * HALF]
                src6 = bank[:, i % 4, 0:HALF].rearrange("p (h c j f) -> p c j h f", h=3, c=2, j=2)
                dst6 = dst.rearrange("p (h c j f) -> p c j h f", h=3, c=2, j=2)
                cos, sin = ([rope[:, w, b - 1, ax, :].unsqueeze(1).to_broadcast([P, 3, 32]) for ax in range(2)] for w in range(2))
                for j, op in ((0, ALU.subtract), (1, ALU.add)):
                    if j == 0 and takes[i][1] > 1:
                        v.wait_ge(taken_v, takes[i][1] - 1)
                    for ax in range(2):
                        dve.mark(v.tensor_tensor(dst6[:, ax, j], src6[:, ax, j], cos[ax], ALU.mult))
                        dve.mark(v.tensor_tensor(rt[:, ax], src6[:, ax, 1 - j], sin[ax], ALU.mult))
                    v.wait_ge(dve.sem, dve.now())
                    for ax in range(2):
                        ins = v.tensor_tensor(dst6[:, ax, j], dst6[:, ax, j], rt[:, ax], op)
                        if j == 1 and ax == 1:
                            ins.then_inc(taken_v, 1)
                        else:
                            dve.mark(ins)
                    if j == 0:
                        v.wait_ge(dve.sem, dve.now())

            v.wait_ge(states_in, 32)
            v.wait_ge(*takes[39])
            v.wait_ge(taken_v, nv)

            def scaled_k(j):
                d, b = updates[j]
                if j >= 2:
                    v.wait_ge(upd_sums, j - 1)
                z = xi_zeta[:, ZETA_F if d == "f" else ZETA_B, :].unsqueeze(2).to_broadcast([P, HEADS, DK])
                v.tensor_tensor(kz[j % 2].rearrange("p (h e) -> p h e", h=HEADS),
                                k_tok[:, b, :].rearrange("p (h e) -> p h e", h=HEADS), z, ALU.mult).then_inc(kz_ready, 1)

            scaled_k(0)
            for what, j in order:
                if what == "u":
                    if j + 1 < len(updates):
                        scaled_k(j + 1)
                    d, b = updates[j]
                    v.wait_ge(upd_sums, j + 1)
                    if b == 0:
                        v.tensor_copy(heads3(new_s[d == "b"]), banks3(0)).then_inc(state_ready, 1)
                    else:
                        old, new = (s_f, s_f) if d == "f" else (s_b[:, b - 1, :], s_b[:, b - 2, :])
                        g = g_chunk[:, 0:HEADS] if d == "f" else g_chunk[:, HEADS:2 * HEADS]
                        if d == "f":
                            v.wait_ge(ret_sums, b + 1)
                        step(v.tensor_tensor(heads3(new), heads3(old), wide(g), ALU.mult))
                        v.tensor_tensor(heads3(new), heads3(new), banks3(0), ALU.add).then_inc(state_ready, 1)
                        v.wait_ge(state_ready, j + 1)
                    continue
                b = j
                v.wait_ge(att_sums, b + 1)
                v.tensor_tensor(heads3(att), banks3(0), heads3(decay), ALU.mult).then_inc(att_ready, 1)
                v.wait_ge(ret_sums, b + 1)
                if b == 0:
                    v.tensor_copy(heads3(o1), banks3(2)).then_inc(ret_taken, 1)
                    v.wait_ge(ret_taken, 1)
                else:
                    dve.mark(v.tensor_tensor(heads3(o1), banks3(4), wide(xi_zeta[:, XI_F, :]), ALU.mult))
                    step(v.tensor_tensor(heads3(o2), banks3(6), wide(xi_zeta[:, XI_B, :]), ALU.mult))
                    step(v.tensor_tensor(o1, o1, o2, ALU.add))
                    v.tensor_tensor(heads3(o1), banks3(2), heads3(o1), ALU.add).then_inc(ret_taken, 1)
                    v.wait_ge(ret_taken, b + 1)
                o3 = o1.rearrange("p (h e) -> p h e", h=HEADS)
                q3 = o2.rearrange("p (h e) -> p h e", h=HEADS)
                step(v.tensor_reduce(hstat[:, 0, :], o3, AX.X, ALU.add))
                step(v.tensor_scalar(hstat[:, 0, :], hstat[:, 0, :], 1.0 / DK, None, ALU.mult))
                step(v.tensor_tensor(o3, o3, hstat[:, 0, :].unsqueeze(2).to_broadcast([P, HEADS, DK]), ALU.subtract))
                step(v.tensor_tensor(o2, o1, o1, ALU.mult))
                step(v.tensor_reduce(hstat[:, 1, :], q3, AX.X, ALU.add))
                v.tensor_scalar(hstat[:, 1, :], hstat[:, 1, :], 1.0 / DK, GN_EPS, ALU.mult, ALU.add).then_inc(ret_var, 1)
                v.wait_ge(ret_root, b + 1)
                step(v.reciprocal(hstat[:, 3, :], hstat[:, 2, :]))
                step(v.tensor_tensor(o3, o3, hstat[:, 3, :].unsqueeze(2).to_broadcast([P, HEADS, DK]), ALU.mult))
                v.tensor_tensor(gates[:, b, :], gates[:, b, :], o1, ALU.mult).then_inc(ret_ready, 1)
                v.wait_ge(ret_ready, b + 1)
                if b:
                    gate_projection(b - 1)
            gate_projection(LATENT)
            v.wait_ge(x_back, 16)
            for b in range(BLOCKS):
                for c in range(2):
                    xs = x[:, b, c * CH:(c + 1) * CH]
                    ins = v.tensor_tensor(xs, xs, gated(b)[c], ALU.add)
                    if c == 1:
                        ins.then_inc(x_done[0], 1)
                        v.wait_ge(x_done[0], b + 1)
                    else:
                        dve.mark(ins)
            peer(0)

            norm(2)
            v.wait_ge(hT_ready[2], BLOCKS)
            v.wait_ge(conv_in, 16)
            dve.mark(v.memset(mean_w, 1.0 / D))
            for a, n in ((0, PAD), (P + PAD, 2 * PAD), (UW - PAD, PAD)):
                last = v.memset(u_pad[:, :, a:a + n], 0.0)
                dve.mark(last)
            v.wait_ge(dve.sem, dve.now())

            def glu(f):
                v.wait_ge(sig_ready, f + 1)
                for t0, n, _, u0, kind in segs:
                    last = v.tensor_tensor(u_pad[:, f, u0:u0 + n], bank[:, 4 * (f % 2) + kind, 0:n],
                                           sig[f % 2][:, t0:t0 + n], ALU.mult)
                    if kind == 0:
                        dve.mark(last)
                last.then_inc(u_ready, 1)

            between = {(0, 11): 2, (0, 21): 3, (2, 1): 4, (2, 11): 5, (2, 21): 6, (4, 1): 7}
            glu(0)
            glu(1)
            for t in range(0, KT - PE_TILES, 2):
                v.wait_ge(u_ready, t + 2)
                v.wait_ge(dve.sem, dve.now())
                for tap in range(TAPS):
                    if (t, tap) in between:
                        glu(between[t, tap])
                    for f in (t, t + 1):
                        src = u_pad[:, f, tap:tap + YW]
                        w = cols[:, f, tap:tap + 1]
                        if tap == 0:
                            dve.mark(v.tensor_scalar(y_conv[:, f, :], src, w, cols[:, f, TAPS:TAPS + 1], ALU.mult, ALU.add))
                            continue
                        v.wait_ge(dve.sem, dve.now() - (tap < TAPS - 1 or f == t))
                        ins = v.scalar_tensor_tensor(out=y_conv[:, f, :], in0=src, scalar=w, in1=y_conv[:, f, :],
                                                     op0=ALU.mult, op1=ALU.add)
                        if tap == TAPS - 1:
                            ins.then_inc(conv_ready, 1)
                        else:
                            dve.mark(ins)
                            continue
            v.wait_ge(ln_mean, 1)
            for f in range(KT):
                for t0, n, y0, _, kind in segs:
                    last = v.tensor_tensor(y_conv[:, f, y0:y0 + n], y_conv[:, f, y0:y0 + n], bank[:, 4 + kind, 0:n], ALU.subtract)
                    if kind == 0:
                        dve.mark(last)
                last.then_inc(centred, 1)
            v.wait_ge(sq_used, KT)
            for t0, n, _, _, kind in segs:
                last = v.tensor_scalar(ln_rs[:, t0:t0 + n], bank[:, 6 + kind, 0:n], GN_EPS, None, ALU.add)
                if kind == 0:
                    dve.mark(last)
            last.then_inc(ln_ve, 1)
            v.wait_ge(ln_root, 1)
            step(v.reciprocal(ln_rs, ln_rs))
            v.wait_ge(centred, KT)
            for f in range(KT):
                for t0, n, y0, _, kind in segs:
                    last = v.tensor_tensor(y_conv[:, f, y0:y0 + n], y_conv[:, f, y0:y0 + n], ln_rs[:, t0:t0 + n], ALU.mult)
                    if kind == 0:
                        dve.mark(last)
                last.then_inc(normed, 1)
            add_projection()
            peer(1)

            rsqrt_mean(4)
            v.wait_ge(ab_in[4], 16)
            for b in range(BLOCKS):
                v.scalar_tensor_tensor(out=peer_out[:, b, :], in0=x[:, b, :], scalar=tok_rs[:, b:b + 1],
                                       in1=bc[:, 0, :], op0=ALU.mult, op1=ALU.mult).then_inc(y_ready, 1)


_INS = ["x_in", "cond_t", "norm_gain", "final_gain", "ada_w", "ada_b", "ada_fix_in", "ab_w_in", "ab_w_out", "decays", "states",
        "conv_w_in", "conv_cols", "conv_w_out", "peer_w_q", "keys_t", "peer_u", "peer_v", "const", "dft"]


def kernel(**a):
    import concourse.bacc as _bacc
    from concourse.bass_utils import run_bass_kernel_spmd as _run

    a = {k: np.asarray(w) for k, w in a.items()}
    const, dft = constants()
    ones, none = np.ones(D, np.float32), np.zeros(D, np.float32)
    g = a["norm_gain"][1]
    fixes = [np.tile(np.concatenate(v), 2).reshape(-1, P) for v in
             ([none, ones, none, none, ones, none], [ones, g[0], ones, ones, g[1], ones])]
    feature = lambda w: w.reshape(-1, KT, P).transpose(2, 1, 0)
    laid = {
        "x_in": np.concatenate([a["x_prompt"][0], a["x_sample"][0]]),
        "cond_t": feature(np.stack([a["c_ctx"], a["c"][0]])),
        "norm_gain": a["norm_gain"].reshape(1, -1), "final_gain": a["final_gain"].reshape(1, -1),
        "ada_w": a["ada_w"], "ada_b": a["ada_b"],
        "ada_fix_in": np.stack([np.tile(a["ada_b"][1].reshape(-1, P), (2, 1)), *fixes]).reshape(3, 2 * 48, P),
        "ab_w_in": a["ab_w_in"][0], "ab_w_out": a["ab_w_out"][0],
        "decays": np.concatenate([a["ret_decay_fwd"], a["ret_decay_bwd"]], 1),
        "states": np.stack([a["state_ret_fwd"][0, 0], a["state_ret_bwd"][0, 0]]),
        "conv_w_in": a["conv_w_in"][0],
        "conv_cols": feature(np.concatenate([a["conv_dw_w"][0], a["conv_dw_b"], a["conv_ln_g"], a["conv_ln_b"]])),
        "conv_w_out": a["conv_w_out"][0],
        "peer_w_q": a["peer_w_q"],
        "keys_t": a["peer_sub_keys"].transpose(0, 4, 1, 2, 3).reshape(LAYERS, P, -1),
        "peer_u": a["peer_u"].reshape(-1, D), "peer_v": a["peer_v"].reshape(-1, D),
        "const": const, "dft": dft,
    }
    nc = _bacc.Bacc("TRN2", target_bir_lowering=False, num_devices=1)
    arrays, args = {}, []
    for name in _INS:
        w = np.ascontiguousarray(laid[name])
        arrays[f"in_{name}"] = w
        args.append(nc.dram_tensor(f"in_{name}", w.shape, mybir.dt.from_np(w.dtype), kind="ExternalInput").ap())
    y = nc.dram_tensor("out_y", (T, D), F32, kind="ExternalOutput").ap()
    st = nc.dram_tensor("out_states", (2, HEADS, DK, DK), F32, kind="ExternalOutput").ap()
    mod = nc.dram_tensor("mod_rows", (LAYERS, 2, 6 * D), F32, kind="Internal").ap()
    program(nc, *args, y, st, mod)
    r = _run(nc, [arrays], core_ids=[0])
    y, st = r.results[0]["out_y"], r.results[0]["out_states"]
    return y[:P][None], y[P:][None], st[0][None, None], st[1][None, None]
```

```python
from contextlib import ExitStack

import numpy as np
import concourse.bass as bass
from concourse import mybir

F32 = mybir.dt.float32
U32 = mybir.dt.uint32
ALU = mybir.AluOpType
ACT = mybir.ActivationFunctionType
AX = mybir.AxisListType

P = 128
D = 1024
KT = D // P
BLOCKS = 5
LATENT = BLOCKS - 1
T = BLOCKS * P
HEADS = 6
DK = 128
GRID_W = 64
RW = HEADS * DK
HALF = RW // 2
TAPS = 31
PAD = TAPS // 2
UW = (P + 2 * PAD) + (LATENT * P + 2 * PAD)
YW = UW - 2 * PAD
LAT_Y = P + 2 * PAD
PHEADS = 8
TOPK = 16
NKEYS = 128
EXPERTS = NKEYS * NKEYS
AHEAD = 2
U_RING, V_RING = 4, 8
QC = 2 * P
ADA2 = 6 * D // QC
PE_TILES = 2
NQ = BLOCKS * PHEADS
LATE = PHEADS - AHEAD
SPLIT = 4
WQ = PHEADS + SPLIT
EPS = 1e-6
GN_EPS = 1e-5
LOWEST = -3.0e38
LAYERS = 2

C_IDENT, C_IOTA, C_POS = 0, 128, 144
C_REL, C_MASK = 148, 404
C_ROPE = 660
C_DFTF = C_ROPE + 2 * LATENT * 64
C_DFTP = C_DFTF + 256
C_KEEP = C_REL
C_ALL = C_DFTP + 256


def constants():
    c = np.zeros((P, C_ALL), np.float32)
    p = np.arange(P)
    c[:, C_IDENT:C_IDENT + P] = np.eye(P)
    c[:, C_IOTA:C_IOTA + TOPK] = np.arange(TOPK)
    c[:, C_POS:C_POS + 4] = np.stack([p + 1, P - 1 - p, P - p, p], 1)
    rel = p[None, :] - p[:, None]
    c[:, C_REL:C_REL + P] = np.maximum(rel, 0)
    c[:, C_REL + P:C_REL + 2 * P] = np.maximum(-rel, 0)
    c[:, C_MASK:C_MASK + P] = (rel >= 0) * DK ** -0.5
    c[:, C_MASK + P:C_MASK + 2 * P] = (rel <= 0) * DK ** -0.5
    nf = DK // 4
    freqs = (np.float32(10000.0) ** (-np.arange(nf, dtype=np.float32) / np.float32(nf))).astype(np.float32)
    tok = np.arange(LATENT * P).reshape(LATENT, P)
    for half, pos in enumerate((tok // GRID_W, tok % GRID_W)):
        ang = pos.astype(np.float32)[:, :, None] * freqs
        for which, fn in enumerate((np.cos, np.sin)):
            for b in range(LATENT):
                at = C_ROPE + which * LATENT * 64 + b * 64 + half * nf
                c[:, at:at + nf] = fn(ang[b])
    g = 64
    a = 2 * np.pi * np.outer(np.arange(g), np.arange(g)) / g
    for i in range(2):
        c[i * g:(i + 1) * g, C_DFTF + i * g:C_DFTF + (i + 1) * g] = np.cos(a) / np.sqrt(g)
        c[i * g:(i + 1) * g, C_DFTF + P + i * g:C_DFTF + P + (i + 1) * g] = np.sin(a) / np.sqrt(g)
    a = 2 * np.pi * (np.outer(p, p) % P) / P
    c[:, C_DFTP:C_DFTP + P] = np.cos(a) / np.sqrt(P)
    c[:, C_DFTP + P:C_DFTP + 2 * P] = -np.sin(a) / np.sqrt(P)
    n = LATENT * P
    k = np.arange(n)
    a = 2 * np.pi * (np.outer(k, k) % n) / n
    m = np.stack([np.cos(a), -np.sin(a)]) / np.sqrt(n)
    m = m.reshape(2, LATENT, P, n).transpose(2, 0, 1, 3)
    return c, np.ascontiguousarray(m.astype(np.float32))


class Count:

    def __init__(self, sem):
        self.sem, self.base, self.n = sem, 0, 0

    def mark(self, ins):
        ins.then_inc(self.sem, 1)
        self.n += 1
        return self.n

    def now(self):
        return self.base + self.n

    def loop(self, base):
        self.base, self.n = base, 0


def apart(eng, passed, sem, value):
    eng.wait_ge(sem, value)
    eng.sem_inc(passed, 1)


def program(nc, x_in, cond_t, norm_gain, final_gain, ada_w, ada_b, ada_fix_in, ab_w_in, ab_w_out, decays, states,
            conv_w_in, conv_cols, conv_w_out, peer_w_q, keys_t, peer_u, peer_v, const, dft,
            y_out, new_states, mod_rows):
    ctx = ExitStack()
    with ctx:
        def sb(name, shape, dt=F32):
            return ctx.enter_context(nc.sbuf_tensor(name, shape, dt))

        def sem(name):
            return ctx.enter_context(nc.semaphore(name))

        def per_stage(name, n):
            return [sem(f"{name}{i}") for i in range(n)]

        x = sb("x", [P, BLOCKS, D])
        work = sb("work", [P, 5120 + (NQ + AHEAD) * 256])
        hT_t = sb("hT", [P, KT * T])
        bc = sb("bc", [P, 6, D])
        ring = sb("ring", [P, 4 * 4096])
        diag = sb("diag", [P, TOPK, P])
        keep = sb("keep", [P, C_KEEP])
        small = sb("small", [P, 1536])
        zero_t = sb("zero_t", [P, P])
        qcur = sb("qcur", [P, 2, P])
        stat = sb("stat", [P, 96])
        idx_cur = sb("idx_cur", [P, 2, 2, TOPK], U32)
        dots = sb("dots", [P, 2, TOPK])
        bank = ctx.enter_context(nc.psum_tensor("bank", [P, 8, 512], F32))

        ident = keep[:, C_IDENT:C_IDENT + P]
        iota = keep[:, C_IOTA:C_IOTA + TOPK]
        pos = [keep[:, C_POS + i:C_POS + i + 1] for i in range(4)]
        hT = hT_t[:, :].rearrange("p (k t) -> p k t", k=KT)
        h_tok = work[:, 0:BLOCKS * D].rearrange("p (b d) -> p b d", b=BLOCKS)

        rows = work[0:2, 9728:9728 + 6 * D]
        gain_rows = hT_t[0:2, 0:2 * D]
        cond = stat[:, 0:2 * KT].rearrange("p (k c) -> p k c", k=KT)

        k_tok = work[:, 0:5 * RW].rearrange("p (b n) -> p b n", b=BLOCKS)
        v_tok = work[:, 5 * RW:10 * RW].rearrange("p (b n) -> p b n", b=BLOCKS)
        gates = work[:, 10 * RW:15 * RW].rearrange("p (b n) -> p b n", b=BLOCKS)
        qT = work[:, 15 * RW:20 * RW].rearrange("p (h t) -> p h t", h=HEADS)
        dft_p = work[:, 20 * RW:20 * RW + 512]
        xf = x[:, :, :].rearrange("p b d -> p (b d)")
        kT = xf[:, 0:5 * RW].rearrange("p (h t) -> p h t", h=HEADS)
        fT = xf[:, 5 * RW:5 * RW + 2 * T].rearrange("p (c t) -> p c t", c=2)
        bcf = bc[:, :, :].rearrange("p a d -> p (a d)")
        s_b = bcf[:, 0:4 * RW].rearrange("p (c n) -> p c n", c=LATENT)
        s_f = bcf[:, 4 * RW:5 * RW]
        diagf = diag[:, :, :].rearrange("p k t -> p (k t)")
        decay = diagf[:, 0:RW]
        rope = diagf[:, RW:RW + 2 * LATENT * 64].rearrange("p (w b c f) -> p w b c f", w=2, b=LATENT, c=2)
        rel = diagf[:, RW + 512:RW + 768]
        mask = diagf[:, RW + 768:RW + 1024]
        over = ring[:, 8192:16384]
        fmix = over[:, 0:2560].rearrange("p (b c w f) -> p b c w f", b=BLOCKS, c=2, w=2)
        att = over[:, 2560:2560 + RW]
        kz = [over[:, 3328 + i * RW:3328 + (i + 1) * RW] for i in range(2)]
        o1 = over[:, 4864:4864 + RW]
        o2 = over[:, 5632:5632 + RW]
        rot = [over[:, 6400 + i * HALF:6400 + (i + 1) * HALF] for i in range(2)]
        rot_t = over[:, 7168:7168 + 192]
        e_rel = [small[:, 0:RW], small[:, RW:2 * RW]]
        new_s = [small[:, i * RW:(i + 1) * RW] for i in range(2)]
        lg = stat[:, 16:28]
        dec_t = [stat[:, 28:40], stat[:, 40:52], stat[:, 52:64]]
        g_chunk = stat[:, 64:76]
        xi_zeta = sb("xi_zeta", [P, 4, HEADS])
        XI_F, ZETA_F, XI_B, ZETA_B = range(4)
        hstat = sb("hstat", [P, 4, HEADS])
        tok_ss = sb("tok_ss", [P, 8])
        tok_rs = sb("tok_rs", [P, 8])
        warm = sb("warm", [P, 5])

        u_pad = work[:, 0:KT * UW].rearrange("p (k t) -> p k t", k=KT)
        y_conv = work[:, KT * UW:KT * (UW + YW)].rearrange("p (k t) -> p k t", k=KT)
        w0 = KT * (UW + YW)
        sig = [work[:, w0 + i * T:w0 + (i + 1) * T] for i in range(2)]
        ln_rs = work[:, w0 + 2 * T:w0 + 3 * T]
        sq = [work[:, w0 + (3 + i) * T:w0 + (4 + i) * T] for i in range(2)]
        cols = small[:, 0:KT * (TAPS + 3)].rearrange("p (k c) -> p k c", k=KT)
        mean_w = small[:, 512:640]
        taps = bcf[:, 0:TAPS * P].rearrange("p (k t) -> p k t", k=TAPS)
        prod = [work[:, 14848 + i * 512:14848 + (i + 1) * 512] for i in range(2)]

        qP = work[:, 5120:5120 + (NQ + AHEAD) * 256]
        idx_all = bcf[:, 0:(NQ + AHEAD) * TOPK].bitcast(U32)
        g_all = bcf[:, (NQ + AHEAD) * TOPK:2 * (NQ + AHEAD) * TOPK]
        keys = bcf[:, 2 * (NQ + AHEAD) * TOPK:2 * (NQ + AHEAD) * TOPK + (PHEADS + AHEAD) * 256]
        wide_w = [ring[:, i * KT * QC:(i + 1) * KT * QC].rearrange("p (k n) -> p k n", k=KT) for i in range(2)]
        u_rows = [ring[:, 4096 + s * D:4096 + (s + 1) * D] for s in range(U_RING)]
        v_rows = [ring[:, 8192 + s * D:8192 + (s + 1) * D] for s in range(V_RING)]
        ada_raw = [qP[0:2, NQ * 256 + i * QC:NQ * 256 + (i + 1) * QC] for i in range(2)]
        ada_fix = hT_t[0:96, 4 * D + 2 * QC:5 * D].rearrange("p (a n) -> p a n", a=4)
        peer_out = h_tok
        left = small[:, 0:256].rearrange("p (s k) -> p s k", s=2)
        cand = small[:, 256:512]
        cand_left = small[:, 512:768]
        onehot = small[:, 768:1280].rearrange("p (s k a) -> p s k a", s=2, k=TOPK)
        side_v = small[:, 1280:1312].rearrange("p (s k) -> p s k", s=2)
        side_i = small[:, 1312:1344].bitcast(U32).rearrange("p (s k) -> p s k", s=2)
        top_v = small[:, 1344:1360]
        top_i = small[:, 1360:1376].bitcast(U32)
        top_e = small[:, 1376:1392]
        pair = small[:, 1392:1424].bitcast(U32).rearrange("p (s k) -> p s k", s=2)
        part_i = small[:, 1424:1456].rearrange("p (s k) -> p s k", s=2)
        top_n = small[:, 1456:1457]
        top_s = small[:, 1457:1458]
        top_r = small[:, 1458:1459]
        act16 = small[:, 1460:1476]
        wgt = small[:, 1476:1492]

        cond_in = sem("cond_in")
        loaded = sem("loaded")
        even_consts = sem("even_consts")
        slot_in = per_stage("slot_in", 4)
        cond_ready = sem("cond_ready")
        ada_sums = sem("ada_sums")
        ada_taken = sem("ada_taken")
        rows_ready = sem("rows_ready")
        rows_out = sem("rows_out")
        ab_in = per_stage("ab_in", 5)
        gate_in = per_stage("gate_in", 4)
        squares = sem("squares")
        mean_sq = sem("mean_sq")
        roots = sem("roots")
        h_ready = per_stage("h_ready", 4)
        h_turned = per_stage("h_turned", 4)
        hT_ready = per_stage("hT_ready", 4)
        x_done = per_stage("x_done", 4)
        dve = Count(sem("dve_steps"))
        dec_ax = sem("dec_ax"); dec_e = sem("dec_e"); dec_u = sem("dec_u"); dec_l = sem("dec_l")
        lg_ready = sem("lg_ready"); exps_ready = sem("exps_ready")
        proj = sem("proj")
        taken_a = sem("taken_a")
        taken_v = sem("taken_v")
        qk_turned = sem("qk_turned")
        qkT_ready = sem("qkT_ready")
        f_proj = sem("f_proj"); fT_ready = sem("fT_ready")
        fmix_sums = sem("fmix_sums"); fmix_ready = sem("fmix_ready")
        fseq_sums = sem("fseq_sums"); fseq_ready = sem("fseq_ready")
        kz_ready = sem("kz_ready"); upd_sums = sem("upd_sums"); state_ready = sem("state_ready")
        att_sums = sem("att_sums"); att_ready = sem("att_ready")
        ret_sums = sem("ret_sums"); ret_var = sem("ret_var"); ret_root = sem("ret_root")
        ret_taken = sem("ret_taken"); ret_ready = sem("ret_ready")
        ret_turned = sem("ret_turned"); retT_ready = sem("retT_ready")
        states_in = sem("states_in"); states_out = sem("states_out"); x_back = sem("x_back")
        conv_in = sem("conv_in"); glu_sums = sem("glu_sums"); sig_ready = sem("sig_ready")
        u_ready = sem("u_ready"); conv_ready = sem("conv_ready")
        ln_mean = sem("ln_mean"); centred = sem("centred"); sq_ready = sem("sq_ready")
        sq_used = sem("sq_used"); ln_var = sem("ln_var"); ln_ve = sem("ln_ve"); ln_root = sem("ln_root")
        normed = sem("normed"); swish_ready = sem("swish_ready")
        tap_diag = sem("tap_diag"); tap_used = sem("tap_used"); pe_y = sem("pe_y")
        ada2_sums = sem("ada2_sums"); ada2_raw = sem("ada2_raw"); ada2_out = per_stage("ada2_out", 2)
        ada2_in = sem("ada2_in"); ada2_fixed = sem("ada2_fixed")
        out_sums = per_stage("out_sums", LAYERS)
        out_taken = per_stage("out_taken", LAYERS)
        early_sums = sem("early_sums")
        early_taken = sem("early_taken")
        wq_sums = per_stage("wq_sums", LAYERS); q_ready = per_stage("q_ready", LAYERS)
        keys_in = per_stage("keys_in", LAYERS)
        more_keys_in = sem("more_keys_in")
        q_head = per_stage("q_head", LAYERS); scores = per_stage("scores", LAYERS)
        top_ready = per_stage("top_ready", LAYERS); exp_ready = per_stage("exp_ready", LAYERS)
        scores_read = per_stage("scores_read", LAYERS)
        idx_ready = per_stage("idx_ready", LAYERS); idx_staged = per_stage("idx_staged", 2)
        w_in = per_stage("w_in", 2)
        u_in = per_stage("u_in", U_RING); v_in = per_stage("v_in", V_RING)
        u_free = per_stage("u_free", LAYERS); v_free = per_stage("v_free", LAYERS)
        gelu_ready = per_stage("gelu_ready", LAYERS)
        wgt_ready = per_stage("wgt_ready", LAYERS); diag_ready = per_stage("diag_ready", LAYERS)
        peer_steps = per_stage("peer_steps", LAYERS)
        block_out = per_stage("block_out", LAYERS)
        passed_v = sem("passed_v"); passed_a = sem("passed_a"); passed_p = sem("passed_p")
        y_ready = sem("y_ready"); y_stored = sem("y_stored")

        def tall(w, c0, n):
            return w[:, c0:c0 + n].rearrange("(k p) n -> p k n", p=P)

        def slot(s, n):
            return ring[:, s * 4096:s * 4096 + KT * n].rearrange("p (k n) -> p k n", k=KT)

        chunks = []

        def chunk(parts, s, done, after=None):
            chunks.append((parts, s, done, after))
            return len(chunks) - 1

        CH = 512
        ADA = 6 * D // CH
        ada_c = [chunk([(slot(c % 4, CH), tall(ada_w[0], c * CH, CH))], c % 4, (ada_sums, c + 1)) for c in range(ADA)]
        ab_c = [chunk([(slot(c % 2, HALF), tall(ab_w_in, c * HALF, HALF))], c % 2, (proj, 5 * c + 5))
                for c in range(8)]
        f_c = chunk([(slot(0, 256), tall(ab_w_in, 8 * HALF, 256))], 0, (f_proj, 2))
        dft_c = chunk([(ring[:, 4096:8192].rearrange("p (w b n) -> p w b n", w=2, b=LATENT), dft)], 1, (fseq_sums, 1))
        wo0_c = [chunk([(slot(c, CH), tall(ab_w_out, c * CH, CH))], c, (out_sums[0], 2 * BLOCKS - 1 + c)) for c in range(2)]
        cin_c = [chunk([(slot(c, CH)[:, :, 256 * i:256 * i + 256], tall(conv_w_in, i * D + 256 * c, 256))
                        for i in range(2)], c, (glu_sums, 2 * c + 2),
                       (ab_in[2], 64)) for c in range(4)]
        before_cin = cin_c[0]
        wo1_c = [chunk([(slot(2 + c, CH), tall(conv_w_out, c * CH, CH))], 2 + c, (out_sums[1], 2 * BLOCKS - 1 + c)) for c in range(2)]
        landed_at, so_far = [], [0] * 4
        for parts, s, _, _ in chunks:
            so_far[s] += 16 * len(parts)
            landed_at.append((slot_in[s], so_far[s]))

        def arrived(eng, c):
            eng.wait_ge(*landed_at[c])

        items = [(c, b) for c in range(8) for b in range(BLOCKS)]
        takes, na, nv = [], 0, 0
        for c, b in items:
            if c < 4 and b > 0:
                nv += 1
                takes.append((taken_v, nv))
            else:
                na += 1
                takes.append((taken_a, na))
        updates = [("b", 4), ("b", 3), ("b", 2), ("b", 0), ("f", 0), ("f", 1), ("f", 2), ("f", 3)]
        order = [("u", 0), ("u", 1), ("u", 2), ("u", 3), ("u", 4), ("a", 0), ("a", 1), ("u", 5),
                 ("a", 2), ("u", 6), ("a", 3), ("u", 7), ("a", 4)]
        norms_before = [0, 1, 1 + BLOCKS, 2 + BLOCKS, 2 + 2 * BLOCKS]
        segs = [(0, P, 0, PAD, 0), (P, LATENT * P, LAT_Y, P + 3 * PAD, 1)]

        def heads3(ap):
            return ap.rearrange("p (b h i) -> p b h i", b=2, h=3)

        def banks3(b0):
            return bank[:, b0:b0 + 2, 0:HALF].rearrange("p b (h i) -> p b h i", h=3)

        def wide(ap, n=DK):
            return ap.rearrange("p (b h) -> p b h", b=2).unsqueeze(3).to_broadcast([P, 2, 3, n])

        def peer_loops(eng, l, two_heads):
            ada = "ada" if l == 0 else None
            pairs = PHEADS // 2
            two_heads(0, 0, "early", True)
            with eng.Fori(1, pairs - 1) as h2:
                two_heads(0, h2, "both", False)
            two_heads(0, pairs - 1, "late", False)
            two_heads(1, 0, "late", True)
            with eng.Fori(1, pairs) as h2:
                two_heads(1, h2, ada, False)
            with eng.Fori(2, BLOCKS - (l == 0)) as b:
                two_heads(b, 0, ada, True)
                with eng.Fori(1, pairs) as h2:
                    two_heads(b, h2, ada, False)
            if l == 0:
                two_heads(BLOCKS - 1, 0, ada, True)
                with eng.Fori(1, pairs) as h2:
                    two_heads(BLOCKS - 1, h2, None, False)

        def part(i, n):
            return slice(i * n, (i + 1) * n) if isinstance(i, int) else bass.ds(i * n, n)

        block = ctx.enter_context(nc.Block())

        @block.sync
        def _(sp):
            def peer_weights(l):
                sp.wait_ge(*((out_sums[0], 2 * BLOCKS - 1), (glu_sums, 2))[l])
                for i, h in enumerate([*range(PHEADS), *range(SPLIT)]):
                    if i == 4:
                        sp.wait_ge(h_ready[2 * l + 1], BLOCKS)
                        sp.dma_start(keys[:, AHEAD * 256:PHEADS * 256], keys_t[l][:, AHEAD * 256:]).then_inc(more_keys_in, 16)
                        sp.dma_start(keys[:, PHEADS * 256:], keys_t[l][:, 0:AHEAD * 256]).then_inc(more_keys_in, 16)
                    if 2 <= i < 2 + SPLIT:
                        sp.wait_ge(early_sums, l * PHEADS + i - 1)
                    elif i >= 2 + SPLIT:
                        sp.wait_ge(wq_sums[l], 2 * (i - 1 - SPLIT))
                    sp.dma_start(wide_w[i % 2], tall(peer_w_q[l], h * QC, QC)).then_inc(w_in[i % 2], 16)
                if l == 1:
                    return
                sp.wait_ge(wq_sums[0], 2 * PHEADS)
                for j in range(2):
                    sp.dma_start(wide_w[j], tall(ada_w[1], j * QC, QC)).then_inc(w_in[j], 16)
                with sp.Fori(1, ADA2 // 2) as j2:
                    for par in range(2):
                        j = j2 * 2 + par
                        sp.wait_ge(ada2_sums, j - 1)
                        sp.dma_start(wide_w[par], ada_w[1][:, bass.ds(j * QC, QC)].rearrange("(k p) n -> p k n", p=P))\
                            .then_inc(w_in[par], 16)
                        sp.wait_ge(ada2_raw, j)
                        sp.dma_start(mod_rows[1][:, bass.ds(j * QC - 2 * QC, QC)], ada_raw[par]).then_inc(ada2_out[par], 16)
                for par in range(2):
                    j = ADA2 - 2 + par
                    sp.wait_ge(ada2_raw, j + 2)
                    sp.dma_start(mod_rows[1][:, j * QC:(j + 1) * QC], ada_raw[par]).then_inc(ada2_out[par], 16)
                for par in range(2):
                    sp.wait_ge(ada2_out[par], 16 * (ADA2 // 2 + 1))
                sp.dma_start(ada_fix[:, 0, :], mod_rows[1].rearrange("c (r n) -> (c r) n", n=P)).then_inc(ada2_in, 16)
                sp.dma_start(ada_fix[:, 1:4, :], ada_fix_in.rearrange("a p n -> p a n")).then_inc(ada2_in, 16)

            last_in_slot = {}
            for c, (parts, s, done, after) in enumerate(chunks):
                if c == before_cin:
                    peer_weights(0)
                if s in last_in_slot:
                    sp.wait_ge(*chunks[last_in_slot[s]][2])
                if after:
                    sp.wait_ge(*after)
                last_in_slot[s] = c
                for dst, src in parts:
                    sp.dma_start(dst, src).then_inc(slot_in[s], 16)
            peer_weights(1)
            for b in range(BLOCKS):
                sp.wait_ge(y_ready, b + 1)
                sp.dma_start(y_out[b * P:(b + 1) * P, :], peer_out[:, b, :]).then_inc(y_stored, 16)
            sp.wait_ge(y_stored, 16 * BLOCKS)
            sp.wait_ge(states_out, 32)

        @block.gpsimd
        def _(pool):
            def load(dst, src, s):
                nc.gpsimd.dma_start(dst, src).then_inc(s, 16)

            load(cond, cond_t, cond_in)
            load(rows, ada_b[0:1, :].to_broadcast([2, 6 * D]), loaded)
            load(keep[:, :], const[:, 0:C_KEEP], loaded)
            load(gain_rows, norm_gain[:, 0:2 * D].to_broadcast([2, 2 * D]), loaded)
            load(dec_t[0], decays.to_broadcast([P, 2 * HEADS]), loaded)
            load(x[:, :, :], x_in.rearrange("(b p) d -> p b d", p=P), loaded)
            load(diagf[:, RW:RW + 512], const[:, C_ROPE:C_ROPE + 512], even_consts)
            load(diagf[:, RW + 512:RW + 1024], const[:, C_REL:C_REL + 512], even_consts)

            def norm_rows(s):
                l, sub = s // 2, s % 2
                for kind in range(2):
                    for i, r in enumerate((3 * sub + 1, 3 * sub)):
                        load(bc[:, 2 * kind + i, :], mod_rows[l, kind:kind + 1, r * D:(r + 1) * D].to_broadcast([P, D]), ab_in[s])

            def gate_rows(s):
                l, sub = s // 2, s % 2
                for kind in range(2):
                    r = 3 * sub + 2
                    load(bc[:, 4 + kind, :], mod_rows[l, kind:kind + 1, r * D:(r + 1) * D].to_broadcast([P, D]), gate_in[s])

            for i, at in enumerate((slice(0, 2 * D), slice(2 * D, 6 * D))):
                pool.wait_ge(rows_ready, i + 1)
                nc.gpsimd.dma_start(mod_rows[0][:, at], rows[:, at]).then_inc(rows_out, 16)
                pool.wait_ge(rows_out, 16 * (i + 1))
                (norm_rows, gate_rows)[i](0)
            pool.wait_ge(h_ready[0], BLOCKS)
            for dst, i in ((s_f, 0), (s_b[:, LATENT - 1, :], 1)):
                load(dst.rearrange("p (h e) -> p h e", h=HEADS), states[i].rearrange("h d e -> d h e"), states_in)
            load(dft_p, const[:, C_DFTF:C_DFTF + 512], even_consts)
            pool.wait_ge(state_ready, 5)
            for i in range(2):
                nc.gpsimd.dma_start(new_states[i].rearrange("h d e -> d h e"),
                                    new_s[i].rearrange("p (h e) -> p h e", h=HEADS)).then_inc(states_out, 16)
            pool.wait_ge(ret_sums, BLOCKS)
            pool.wait_ge(fmix_ready, BLOCKS)
            load(x[:, :, :], x_in.rearrange("(b p) d -> p b d", p=P), x_back)
            norm_rows(1)

            for l in range(LAYERS):
                if l == 1:
                    pool.wait_ge(ada2_fixed, 1)
                    nc.gpsimd.dma_start(mod_rows[1].rearrange("c (r n) -> (c r) n", n=P), ada_fix[:, 0, :]).then_inc(rows_out, 16)
                    pool.wait_ge(rows_out, 48)
                    pool.wait_ge(block_out[0], BLOCKS + 1)
                    norm_rows(2)
                    load(cols, conv_cols, conv_in)
                    pool.wait_ge(x_done[1], BLOCKS)
                    gate_rows(2)
                    pool.wait_ge(tap_used, PE_TILES * TAPS)
                    norm_rows(3)
                pool.wait_ge(h_ready[2 * l + 1], 1)
                load(keys[:, 0:AHEAD * 256], keys_t[l][:, 0:AHEAD * 256], keys_in[l])
                if l == 0:
                    pool.wait_ge(x_done[0], BLOCKS)
                    gate_rows(1)
                    pool.wait_ge(out_sums[0], 2 * BLOCKS)

                def gather(n, par, table, rows_, free, landed, which):
                    idx = idx_cur[:, which, par, :]
                    nc.gpsimd.tensor_copy(idx, idx_all[:, part(n, TOPK)]).then_inc(idx_staged[which], 1)
                    apart(pool, passed_p, idx_staged[which], l * NQ + n + 1)
                    for k in range(TOPK):
                        apart(pool, passed_p, free[l], n * TOPK + k + 1 + (TOPK - V_RING if which else 0))
                        nc.gpsimd.indirect_dma_start(
                            rows_[k % len(rows_)], None, table,
                            bass.IndirectOffsetOnAxis(ap=idx[:, k:k + 1], axis=0),
                        ).then_inc(landed[k % len(rows_)], 16)

                def gather_u(n, par):
                    apart(pool, passed_p, idx_ready[l], n + 1)
                    gather(n, par, peer_u, u_rows, u_free, u_in, 0)

                def gather_v(n, par):
                    gather(n, par, peer_v, v_rows, v_free, v_in, 1)

                gather_u(0, 0)
                if l == 1:
                    pool.wait_ge(x_done[2], BLOCKS)
                    gate_rows(3)
                    pool.wait_ge(out_sums[1], 2 * BLOCKS)
                with pool.Fori(0, NQ // 2 - 1) as n2:
                    for par in range(2):
                        gather_u(n2 * 2 + par + 1, 1 - par)
                        gather_v(n2 * 2 + par, par)
                gather_u(NQ - 1, 1)
                gather_v(NQ - 2, 0)
                if l == 1:
                    pool.wait_ge(scores[1], NQ + AHEAD)
                    load(bc[:, 3, :], final_gain.to_broadcast([P, D]), ab_in[4])
                gather_v(NQ - 1, 1)

        @block.tensor
        def _(pe):
            def mm(out, lhsT, rhs, start, stop, **kw):
                return nc.tensor.matmul(out, lhsT, rhs, start=start, stop=stop, **kw)

            pe.wait_ge(cond_ready, 1)
            for c in range(ADA):
                arrived(pe, ada_c[c])
                if c >= 4:
                    pe.wait_ge(ada_taken, c - 3)
                for k in range(KT):
                    last = mm(bank[0:2, c % 4, :], cond[:, k, :], slot(c % 4, CH)[:, k, :], k == 0, k == KT - 1)
                last.then_inc(ada_sums, 1)

            def turn(s):
                for b in range(BLOCKS):
                    pe.wait_ge(h_ready[s], b + 1)
                    if b >= 4:
                        pe.wait_ge(hT_ready[s], b - 3)
                    b0 = 2 * (b % 4)
                    for k in range(KT):
                        last = nc.tensor.transpose(bank[:, b0 + k // 4, (k % 4) * P:(k % 4 + 1) * P],
                                                   h_tok[:, b, k * P:(k + 1) * P], ident)
                    last.then_inc(h_turned[s], 1)
                pe.wait_ge(hT_ready[s], BLOCKS)

            def project_out(l, b, cs, banks):
                for c in range(2):
                    if b == 0:
                        arrived(pe, cs[c])
                    for k in range(KT):
                        last = mm(bank[:, banks[c], :], hT[:, k, b * P:(b + 1) * P], slot(2 * l + c, CH)[:, k, :],
                                  k == 0, k == KT - 1)
                    last.then_inc(out_sums[l], 1)

            def peer(l, out):
                s = 2 * l + 1

                def turn_block(b):
                    pe.wait_ge(h_ready[s], b + 1)
                    if b:
                        pe.wait_ge(hT_ready[s], b)
                    for k in range(KT):
                        last = nc.tensor.transpose(bank[:, 6 + k // 4, (k % 4) * P:(k % 4 + 1) * P],
                                                   h_tok[:, b, k * P:(k + 1) * P], ident)
                    last.then_inc(h_turned[s], 1)

                def early(h, par):
                    pe.wait_ge(w_in[par], (h + (2 - par)) * 8 + l * (WQ + ADA2) * 8)
                    if not isinstance(h, int) or h:
                        pe.wait_ge(q_head[l], h)
                    for half in range(2):
                        for k in range(KT):
                            last = mm(bank[:, 5, half * P:(half + 1) * P], wide_w[par][:, k, half * P:(half + 1) * P],
                                      hT[:, k, 0:P], k == 0, k == KT - 1)
                    last.then_inc(early_sums, 1)

                def late(i, par):
                    if i >= LATE - AHEAD:
                        pe.wait_ge(w_in[par], (i + SPLIT + (2 - par)) * 8 + l * (WQ + ADA2) * 8)
                    if i == 0:
                        pe.wait_ge(hT_ready[s], BLOCKS)
                    for half in range(2):
                        if i:
                            pe.wait_ge(q_ready[l], i * 2 + half - 1)
                        for k in range(KT):
                            last = mm(bank[:, (2, 6)[half], :], wide_w[par][:, k, half * P:(half + 1) * P],
                                      hT[:, k, P:T], k == 0, k == KT - 1)
                        last.then_inc(wq_sums[l], 1)

                def ada_chunk(j, par):
                    pe.wait_ge(w_in[par], (j + (2 - par)) * 8 + WQ * 8)
                    pe.wait_ge(ada2_raw, j + 1)
                    for k in range(KT):
                        last = mm(bank[0:2, 7, 0:QC], cond[:, k, :], wide_w[par][:, k, :], k == 0, k == KT - 1)
                    last.then_inc(ada2_sums, 1)

                def score(h):
                    for s in range(2):
                        last = mm(bank[:, 4, s * P:(s + 1) * P], qcur[:, s, :],
                                  keys[:, bass.ds(h * 256 + s * P, P)] if not isinstance(h, int)
                                  else keys[:, h * 256 + s * P:h * 256 + (s + 1) * P], True, True)
                    last.then_inc(scores[l], 1)

                def second_scores():
                    pe.wait_ge(q_head[l], 2)
                    pe.wait_ge(scores_read[l], 1)
                    score(1)

                out(0)
                out(1)
                turn_block(0)
                pe.wait_ge(hT_ready[s], 1)
                early(0, 0)
                pe.wait_ge(keys_in[l], 16)
                pe.wait_ge(q_head[l], 1)
                score(0)
                if l == 0:
                    turn_block(1)
                early(1, 1)
                out(2)
                if l == 1:
                    turn_block(1)
                out(3)
                turn_block(2)
                if l == 1:
                    second_scores()
                out(4)
                turn_block(3)
                turn_block(4)
                if l == 0:
                    second_scores()
                pe.wait_ge(out_taken[l], 2 * BLOCKS)
                pe.wait_ge(more_keys_in, 32 * (l + 1))

                def open_block(b):
                    pe.wait_ge(block_out[l], b + 1)
                    for i in range(8):
                        mm(bank[:, i // 4, (i % 4) * P:(i % 4 + 1) * P], zero_t[:, :], ident, i % 4 == 0, False,
                           skip_group_check=True)

                def front(b, h, par, what):
                    n = b * PHEADS + h
                    if what in ("early", "both"):
                        early(h + AHEAD, par)
                    if what == "late":
                        late(n - AHEAD, par)
                    pe.wait_ge(q_head[l], n + AHEAD + 1)
                    pe.wait_ge(scores_read[l], n + AHEAD)
                    score(h + AHEAD)
                    if what == "both":
                        late(n - AHEAD, par)
                    if what == "ada":
                        ada_chunk(n - LATE - SPLIT, par)

                def sums(b, h):
                    n = b * PHEADS + h
                    for k in range(TOPK):
                        pe.wait_ge(diag_ready[l], n * TOPK + k + 1)
                        pe.wait_ge(v_in[k % V_RING], (l * NQ * 2 + n * 2 + k // V_RING + 1) * 16)
                        for half in range(2):
                            last = mm(bank[:, half, :], diag[:, k, :],
                                      v_rows[k % V_RING][:, half * 512:(half + 1) * 512], False, False,
                                      skip_group_check=True)
                        last.then_inc(v_free[l], 1)

                def two_heads(b, h2, what, opens=False, next_front=True):
                    for par in range(2):
                        h = h2 * 2 + par
                        if par == 0:
                            front(b, h + 1, 1, what[0])
                        elif next_front:
                            front(*((b + 1, 0) if isinstance(h, int) and h == PHEADS - 1 else (b, h + 1)), 0, what[1])
                        if opens and par == 0:
                            open_block(b)
                        sums(b, h)

                ada = "ada" if l == 0 else None

                def what_at(n):
                    return ("early" if n < SPLIT - AHEAD else "both" if n < LATE else "late" if n < LATE + SPLIT else
                            ada if n < LATE + SPLIT + ADA2 else None)

                def whats(b, h2):
                    n = b * PHEADS + 2 * h2
                    return what_at(n + 1), what_at(n + 2)

                front(0, 0, 0, "early")
                for b in range(2):
                    for h2 in range(PHEADS // 2):
                        two_heads(b, h2, whats(b, h2), opens=h2 == 0)
                with pe.Fori(2, BLOCKS - 1) as b:
                    two_heads(b, 0, (ada, ada), opens=True)
                    with pe.Fori(1, PHEADS // 2 - 1) as h2:
                        two_heads(b, h2, (ada, ada))
                    two_heads(b, PHEADS // 2 - 1, (ada, ada))
                for h2 in range(PHEADS // 2):
                    two_heads(BLOCKS - 1, h2, whats(BLOCKS - 1, h2), opens=h2 == 0, next_front=h2 < PHEADS // 2 - 1)

            pe.wait_ge(ada_taken, ADA)
            turn(0)
            def project(i):
                c, b = items[i]
                if b == 0:
                    arrived(pe, ab_c[c])
                if i >= 4:
                    pe.wait_ge(*takes[i - 4])
                for k in range(KT):
                    last = mm(bank[:, i % 4, 0:HALF], hT[:, k, b * P:(b + 1) * P], slot(c % 2, HALF)[:, k, :],
                              k == 0, k == KT - 1)
                last.then_inc(proj, 1)

            def turn_qk(i):
                c, b = items[i]
                pe.wait_ge(*takes[i])
                if i >= 4:
                    pe.wait_ge(qkT_ready, i - 3)
                src = rot[i % 2] if c < 2 else k_tok[:, b, (c - 2) * HALF:(c - 1) * HALF]
                for h in range(3):
                    last = nc.tensor.transpose(bank[:, 4 + i % 4, h * P:(h + 1) * P], src[:, h * P:(h + 1) * P], ident)
                last.then_inc(qk_turned, 1)

            for i in range(len(items)):
                project(i)
                if 0 <= i - 1 < 4 * BLOCKS:
                    turn_qk(i - 1)
            arrived(pe, f_c)
            for c in range(2):
                pe.wait_ge(*takes[36 + 2 * c])
                pe.wait_ge(*takes[37 + 2 * c])
                for t0, n, bk in ((0, 512, 2 * c), (512, P, 2 * c + 1)):
                    for k in range(KT):
                        last = mm(bank[:, bk, 0:n], slot(0, 256)[:, k, c * P:(c + 1) * P], hT[:, k, t0:t0 + n],
                                  k == 0, k == KT - 1)
                last.then_inc(f_proj, 1)
            pe.wait_ge(qkT_ready, 4 * BLOCKS)
            pe.wait_ge(even_consts, 48)
            for b in range(BLOCKS):
                pe.wait_ge(fT_ready, 2)
                for c in range(2):
                    last = mm(bank[:, b, c * 256:(c + 1) * 256] if b < 4 else bank[:, 4, c * 256:(c + 1) * 256],
                              fT[:, c, b * P:(b + 1) * P], dft_p[:, 0:256], True, True)
                last.then_inc(fmix_sums, 1)
            pe.wait_ge(fmix_ready, BLOCKS)
            arrived(pe, dft_c)
            dft_s = ring[:, 4096:8192].rearrange("p (w b n) -> p w b n", w=2, b=LATENT)
            for c in range(2):
                for w in range(2):
                    for b in range(LATENT):
                        mm(bank[:, c, :], fmix[:, b + 1, c, w, :], dft_s[:, w, b, :], w + b == 0, w == 1 and b == LATENT - 1)
                for w in range(2):
                    last = mm(bank[:, 2 + c, 0:P], fmix[:, 0, c, w, :], dft_p[:, 256 + w * P:256 + (w + 1) * P], w == 0, w == 1)
            last.then_inc(fseq_sums, 1)
            pe.wait_ge(fseq_ready, 1)

            for what, j in order:
                if what == "u":
                    b = updates[j][1]
                    pe.wait_ge(kz_ready, j + 1)
                    if j > 4:
                        pe.wait_ge(out_taken[0], 2 * (j - 4))
                    if j >= 1:
                        pe.wait_ge(state_ready, j)
                    for h in range(HEADS):
                        last = mm(bank[:, h // 3, (h % 3) * P:(h % 3 + 1) * P], kz[j % 2][:, h * P:(h + 1) * P],
                                  v_tok[:, b, h * P:(h + 1) * P], True, True)
                    last.then_inc(upd_sums, 1)
                    continue
                b = j
                tok = slice(b * P, (b + 1) * P)
                pe.wait_ge(state_ready, {0: 5, 1: 5, 2: 6, 3: 7, 4: 8}[b])
                pe.wait_ge(states_in, 32)
                if b:
                    pe.wait_ge(retT_ready, b)
                if b > 1:
                    pe.wait_ge(out_taken[0], 2 * (b - 1))
                for h in range(HEADS):
                    last = mm(bank[:, h // 3, (h % 3) * P:(h % 3 + 1) * P], kT[:, h, tok], qT[:, h, tok], True, True)
                last.then_inc(att_sums, 1)
                if b:
                    for h in range(HEADS):
                        at = slice((h % 3) * P, (h % 3 + 1) * P)
                        mm(bank[:, 4 + h // 3, at], qT[:, h, tok], s_f[:, h * P:(h + 1) * P], True, True)
                        mm(bank[:, 6 + h // 3, at], qT[:, h, tok], s_b[:, b - 1, h * P:(h + 1) * P], True, True)
                pe.wait_ge(att_ready, b + 1)
                for h in range(HEADS):
                    last = mm(bank[:, 2 + h // 3, (h % 3) * P:(h % 3 + 1) * P], att[:, h * P:(h + 1) * P],
                              v_tok[:, b, h * P:(h + 1) * P], True, True)
                last.then_inc(ret_sums, 1)
                if b:
                    project_out(0, b - 1, wo0_c, (0, 1))
                pe.wait_ge(ret_ready, b + 1)
                for h in range(HEADS):
                    last = nc.tensor.transpose(bank[:, 2 + h // 3, (h % 3) * P:(h % 3 + 1) * P],
                                               gates[:, b, h * P:(h + 1) * P], ident)
                last.then_inc(ret_turned, 1)
            pe.wait_ge(retT_ready, BLOCKS)
            pe.wait_ge(out_taken[0], 2 * LATENT)
            project_out(0, LATENT, wo0_c, (0, 1))
            peer(0, lambda b: None)

            turn(2)
            for f in range(KT):
                if f % 2 == 0:
                    arrived(pe, cin_c[f // 2])
                if f >= 2:
                    pe.wait_ge(u_ready, f - 1)
                w = slot(f // 2, CH)
                for part in range(2):
                    at = part * 256 + (f % 2) * P
                    for t0, n, _, _, kind in segs:
                        for k in range(KT):
                            last = mm(bank[:, 4 * (f % 2) + 2 * part + kind, 0:n], w[:, k, at:at + P],
                                      hT[:, k, t0:t0 + n], k == 0, k == KT - 1)
                last.then_inc(glu_sums, 1)
            for i in range(PE_TILES):
                f = KT - PE_TILES + i
                pe.wait_ge(u_ready, f + 1)
                for tap in range(TAPS):
                    pe.wait_ge(tap_diag, i * TAPS + tap + 1)
                    for t0, n, _, u0, kind in segs:
                        last = mm(bank[:, 2 * i + kind, 0:n], taps[:, tap, :], u_pad[:, f, u0 - PAD + tap:u0 - PAD + tap + n],
                                  tap == 0, tap == TAPS - 1)
                    last.then_inc(tap_used, 1)
            for f in range(KT):
                if f < KT - PE_TILES:
                    pe.wait_ge(conv_ready, f + 1)
                else:
                    pe.wait_ge(pe_y, PE_TILES)
                for t0, n, y0, _, kind in segs:
                    last = mm(bank[:, 4 + kind, 0:n], mean_w, y_conv[:, f, y0:y0 + n], f == 0, f == KT - 1)
            last.then_inc(ln_mean, 1)
            for f in range(KT):
                pe.wait_ge(sq_ready, f + 1)
                for t0, n, _, _, kind in segs:
                    last = mm(bank[:, 6 + kind, 0:n], mean_w, sq[f % 2][:, t0:t0 + n], f == 0, f == KT - 1)
                last.then_inc(sq_used, 1)

            def out1(b):
                pe.wait_ge(swish_ready, KT * (1 + min(b, 1)))
                if b >= 2:
                    pe.wait_ge(out_taken[1], 2 * b - 2)
                project_out(1, b, wo1_c, (b % 2 * 2, b % 2 * 2 + 1))

            peer(1, out1)

        @block.scalar
        def _(act):
            def f(out, in_, func=ACT.Copy, **kw):
                return nc.scalar.activation(out, in_, func, **kw)

            act.wait_ge(cond_in, 16)
            f(cond, cond, ACT.Silu).then_inc(cond_ready, 1)
            act.wait_ge(loaded, 16 * 5)
            act.wait_ge(dec_ax, 1)
            f(dec_t[1], dec_t[1], ACT.Exp, scale=-1.0).then_inc(dec_e, 1)
            act.wait_ge(dec_u, 1)
            f(lg, dec_t[2], ACT.Ln).then_inc(dec_l, 1)
            act.wait_ge(lg_ready, 1)
            act.wait_ge(even_consts, 32)
            for i in range(4):
                f(xi_zeta[:, i, :], lg[:, (i // 2) * HEADS:(i // 2 + 1) * HEADS], ACT.Exp, scale=pos[i])
            f(g_chunk, lg, ACT.Exp, scale=float(P))
            for d in range(2):
                for h in range(HEADS):
                    last = f(e_rel[d][:, h * P:(h + 1) * P], rel[:, d * P:(d + 1) * P], ACT.Exp,
                             scale=lg[:, d * HEADS + h:d * HEADS + h + 1])
            last.then_inc(exps_ready, 1)

            def square(s, b):
                if s:
                    act.wait_ge(x_done[s - 1], b + 1)
                dst = h_tok[:, b, :] if s < 4 else peer_out[:, b, :]
                return f(dst, x[:, b, :], ACT.Square, accum_out=tok_ss[:, b:b + 1])

            def norm(s):
                for b in range(LATENT if s else 0, BLOCKS):
                    last = square(s, b)
                last.then_inc(squares, 1)
                act.wait_ge(mean_sq, norms_before[s] + 1)
                f(tok_rs[:, 0:BLOCKS], tok_ss[:, 0:BLOCKS], ACT.Sqrt).then_inc(roots, 1)

            def norm_block(s, b):
                act.wait_ge(x_done[s - 1], b + 1)
                f(h_tok[:, b, :], x[:, b, :], ACT.Square, accum_out=tok_ss[:, b:b + 1]).then_inc(squares, 1)
                act.wait_ge(mean_sq, norms_before[s] + b + 1)
                f(tok_rs[:, b:b + 1], tok_ss[:, b:b + 1], ACT.Sqrt).then_inc(roots, 1)

            def take_turned(s, blocks=range(BLOCKS)):
                for b in blocks:
                    act.wait_ge(h_turned[s], b + 1)
                    b0 = 6 if s % 2 else 2 * (b % 4)
                    f(hT[:, :, b * P:(b + 1) * P], bank[:, b0:b0 + 2, :].rearrange("p b (k t) -> p (b k) t", k=4))\
                        .then_inc(hT_ready[s], 1)

            def peer(l):
                s = 2 * l + 1
                q4 = qP[:, 0:NQ * 256].rearrange("p (b f t) -> p b f t", b=BLOCKS, f=2 * PHEADS)

                def take_early(h):
                    apart(act, passed_a, early_sums, l * PHEADS + h + 1)
                    f(qP[:, part(h, 256)], bank[:, 5, 0:256]).then_inc(early_taken, 1)
                    apart(act, passed_a, early_taken, l * PHEADS + h + 1)

                def take_late(i, h):
                    for half in range(2):
                        apart(act, passed_a, wq_sums[l], i * 2 + half + 1)
                        ft = h * 2 + half
                        at = slice(ft, ft + 1) if isinstance(ft, int) else bass.ds(ft, 1)
                        f(q4[:, 1:BLOCKS, at, :], bank[:, (2, 6)[half], :].rearrange("p (b o t) -> p b o t", b=4, o=1))\
                            .then_inc(q_ready[l], 1)
                    apart(act, passed_a, q_ready[l], i * 2 + 2)

                def head_in(m):
                    f(qcur[:, :, :].rearrange("p s t -> p (s t)"), qP[:, part(m, 256)]).then_inc(q_head[l], 1)

                def soft(m):
                    apart(act, passed_a, top_ready[l], m + 1)
                    f(top_e, top_v, ACT.Exp, bias=top_n, accum_out=top_s).then_inc(exp_ready[l], 1)

                def first_query(m):
                    take_early(m)
                    if m:
                        act.wait_ge(scores[l], m)
                    head_in(m)

                norm_block(s, 0)
                norm_block(s, 1)
                if l == 0:
                    norm_block(s, 2)
                    norm_block(s, 3)
                    take_turned(s, [0])
                    norm_block(s, 4)
                    first_query(0)
                    take_turned(s, [1])
                    first_query(1)
                    take_turned(s, [2, 3])
                    soft(0)
                    take_turned(s, [4])
                    soft(1)
                else:
                    take_turned(s, [0])
                    first_query(0)
                    first_query(1)
                    soft(0)
                    take_turned(s, [1])
                    norm_block(s, 2)
                    take_turned(s, [2])
                    norm_block(s, 3)
                    soft(1)
                    norm_block(s, 4)
                    take_turned(s, [3, 4])

                def two_heads(b, h2, what, first):
                    for par in range(2):
                        n = b * PHEADS + h2 * 2 + par
                        if what in ("early", "both"):
                            take_early(n + AHEAD)
                        if what == "late":
                            take_late(n - AHEAD, n - LATE)
                        if what is None and l == 0:
                            apart(act, passed_a, ada2_raw, ADA2 + 1)
                        apart(act, passed_a, scores[l], n + AHEAD)
                        head_in(n + AHEAD)
                        if what == "ada":
                            j = n - LATE - SPLIT
                            apart(act, passed_a, ada2_out[par], j * 8 + (16 - 8 * par))
                            apart(act, passed_a, ada2_sums, j + 1)
                            f(ada_raw[par], bank[0:2, 7, 0:QC]).then_inc(ada2_raw, 1)
                        apart(act, passed_a, u_free[l], U_RING + (n + 1) * TOPK)
                        f(act16, dots[:, par, :], ACT.Gelu_apprx_tanh).then_inc(gelu_ready[l], 1)
                        if what == "both":
                            take_late(n - AHEAD, n + AHEAD)
                        soft(n + AHEAD)
                        apart(act, passed_a, wgt_ready[l], n + 1)
                        for k in range(TOPK):
                            act.wait_ge(v_free[l], n * TOPK + k + 1)
                            f(diag[:, k, :], ident, scale=wgt[:, k:k + 1]).then_inc(diag_ready[l], 1)
                        if first and par == 0 and not (isinstance(b, int) and b == 0):
                            close(b - 1)

                def close(b):
                    apart(act, passed_a, v_free[l], TOPK + (b + 1) * PHEADS * TOPK)
                    f(peer_out[:, part(b, 1), :].rearrange("p b d -> p (b d)"),
                      bank[:, 0:2, :].rearrange("p b d -> p (b d)")).then_inc(block_out[l], 1)

                peer_loops(act, l, two_heads)
                for b in range(LATENT):
                    last = square(2 * l + 2, b)
                if l == 1:
                    last.then_inc(squares, 1)
                    act.wait_ge(mean_sq, norms_before[4] + 1)
                    f(tok_rs[:, 0:LATENT], tok_ss[:, 0:LATENT], ACT.Sqrt).then_inc(roots, 1)
                close(BLOCKS - 1)

            norm(0)
            take_turned(0)
            act.wait_ge(rows_out, 32)
            for i in range(len(items) + 1):
                if i < len(items):
                    c, b = items[i]
                    if takes[i][0] is taken_a:
                        act.wait_ge(proj, i + 1)
                        if c < 2 and i >= 2:
                            act.wait_ge(qk_turned, i - 1)
                        cc = (c % 2) * HALF
                        dst = (rot[i % 2] if c < 2 else k_tok[:, b, cc:cc + HALF] if c < 4 else
                               v_tok[:, b, cc:cc + HALF] if c < 6 else gates[:, b, cc:cc + HALF])
                        f(dst, bank[:, i % 4, 0:HALF], ACT.Silu if c >= 6 else ACT.Copy).then_inc(taken_a, 1)
                if 0 <= i - 1 < 4 * BLOCKS:
                    c, b = items[i - 1]
                    act.wait_ge(qk_turned, i)
                    dst = qT if c < 2 else kT
                    f(dst[:, (c % 2) * 3:(c % 2) * 3 + 3, b * P:(b + 1) * P],
                      bank[:, 4 + (i - 1) % 4, 0:HALF].rearrange("p (h t) -> p h t", h=3)).then_inc(qkT_ready, 1)
            for c in range(2):
                act.wait_ge(f_proj, c + 1)
                f(fT[:, c, 0:512], bank[:, 2 * c, :])
                f(fT[:, c, 512:T], bank[:, 2 * c + 1, 0:P]).then_inc(fT_ready, 1)
            for b in range(BLOCKS):
                act.wait_ge(fmix_sums, b + 1)
                f(fmix[:, b, :, :, :].rearrange("p c w f -> p (c w f)"), bank[:, b, :]).then_inc(fmix_ready, 1)
            act.wait_ge(fseq_sums, 1)
            for c in range(2):
                f(hT[:, 6 + c, P:T], bank[:, c, :])
                last = f(hT[:, 6 + c, 0:P], bank[:, 2 + c, 0:P])
            last.then_inc(fseq_ready, 1)
            for b in range(BLOCKS):
                act.wait_ge(ret_var, b + 1)
                f(hstat[:, 2, :], hstat[:, 1, :], ACT.Sqrt).then_inc(ret_root, 1)
                act.wait_ge(ret_turned, b + 1)
                f(hT[:, 0:6, b * P:(b + 1) * P].rearrange("p (b h) t -> p b h t", b=2), banks3(2)).then_inc(retT_ready, 1)
            peer(0)

            norm(2)
            take_turned(2)
            for t in range(KT):
                act.wait_ge(glu_sums, t + 1)
                if t >= 2:
                    act.wait_ge(u_ready, t - 1)
                for t0, n, _, _, kind in segs:
                    last = f(sig[t % 2][:, t0:t0 + n], bank[:, 4 * (t % 2) + 2 + kind, 0:n], ACT.Sigmoid)
                last.then_inc(sig_ready, 1)
            for i in range(PE_TILES):
                t = KT - PE_TILES + i
                for tap in range(TAPS):
                    if i:
                        act.wait_ge(tap_used, (i - 1) * TAPS + tap + 1)
                    f(taps[:, tap, :], ident, scale=cols[:, t, tap:tap + 1]).then_inc(tap_diag, 1)
            for i in range(PE_TILES):
                t = KT - PE_TILES + i
                act.wait_ge(tap_used, (i + 1) * TAPS)
                for t0, n, y0, _, kind in segs:
                    last = f(y_conv[:, t, y0:y0 + n], bank[:, 2 * i + kind, 0:n], ACT.Identity, bias=cols[:, t, TAPS:TAPS + 1])
                last.then_inc(pe_y, 1)
            for t in range(KT):
                act.wait_ge(centred, t + 1)
                if t >= 2:
                    act.wait_ge(sq_used, t - 1)
                for t0, n, y0, _, kind in segs:
                    last = f(sq[t % 2][:, t0:t0 + n], y_conv[:, t, y0:y0 + n], ACT.Square)
                last.then_inc(sq_ready, 1)
            act.wait_ge(ln_ve, 1)
            f(ln_rs, ln_rs, ACT.Sqrt).then_inc(ln_root, 1)
            for t0, n, y0, _, kind in segs:
                for t in range(KT):
                    act.wait_ge(normed, kind * KT + t + 1)
                    f(hT[:, t, t0:t0 + n], y_conv[:, t, y0:y0 + n], ACT.Silu,
                      scale=cols[:, t, TAPS + 1:TAPS + 2], bias=cols[:, t, TAPS + 2:TAPS + 3]).then_inc(swish_ready, 1)
            peer(1)
            act.wait_ge(x_done[3], BLOCKS)
            f(peer_out[:, LATENT, :], x[:, LATENT, :], ACT.Square, accum_out=tok_ss[:, LATENT:BLOCKS]).then_inc(squares, 1)
            act.wait_ge(mean_sq, norms_before[4] + 2)
            f(tok_rs[:, LATENT:BLOCKS], tok_ss[:, LATENT:BLOCKS], ACT.Sqrt).then_inc(roots, 1)

        @block.vector
        def _(v):
            def step(ins):
                dve.mark(ins)
                v.wait_ge(dve.sem, dve.now())

            step(v.memset(zero_t[:, :], 0.0))
            v.wait_ge(loaded, 16 * 5)
            step(v.tensor_scalar(dec_t[1], dec_t[0], -1.0, None, ALU.mult))
            v.tensor_tensor(dec_t[1], dec_t[1], dec_t[0], ALU.max).then_inc(dec_ax, 1)
            v.wait_ge(dec_e, 1)
            v.tensor_scalar(dec_t[2], dec_t[1], 1.0, None, ALU.add).then_inc(dec_u, 1)
            v.wait_ge(dec_u, 1)
            ctmp, rtmp = stat[:, 76:88], dec_t[0]
            step(v.scalar_tensor_tensor(out=ctmp, in0=dec_t[2], scalar=1.0, in1=dec_t[1], op0=ALU.subtract, op1=ALU.subtract))
            step(v.tensor_scalar(rtmp, dec_t[0], 0.0, None, ALU.min))
            v.wait_ge(dec_l, 1)
            step(v.tensor_tensor(rtmp, rtmp, lg, ALU.subtract))
            step(v.reciprocal(dec_t[2], dec_t[2]))
            step(v.tensor_tensor(ctmp, ctmp, dec_t[2], ALU.mult))
            v.tensor_tensor(lg, rtmp, ctmp, ALU.add).then_inc(lg_ready, 1)
            v.wait_ge(exps_ready, 1)
            for d in range(2):
                e3 = e_rel[d].rearrange("p (h i) -> p h i", h=HEADS)
                m3 = mask[:, d * P:(d + 1) * P].unsqueeze(1).to_broadcast([P, HEADS, P])
                step(v.tensor_tensor(e3, e3, m3, ALU.mult))
            step(v.tensor_tensor(decay, e_rel[0], e_rel[1], ALU.add))
            for i in (ZETA_F, ZETA_B):
                step(v.tensor_scalar(xi_zeta[:, i, :], xi_zeta[:, i, :], DK ** -0.5, None, ALU.mult))

            def rsqrt_mean(s, b0=0, b1=BLOCKS):
                n = norms_before[s] + (b0 > 0 if s == 4 else b0) + 1
                v.wait_ge(squares, n)
                v.tensor_scalar(tok_ss[:, b0:b1], tok_ss[:, b0:b1], 1.0 / D, EPS, ALU.mult, ALU.add).then_inc(mean_sq, 1)
                v.wait_ge(roots, n)
                step(v.reciprocal(tok_rs[:, b0:b1], tok_rs[:, b0:b1]))

            def modulated(s, b):
                kind = min(b, 1)
                step(v.scalar_tensor_tensor(out=h_tok[:, b, :], in0=x[:, b, :], scalar=tok_rs[:, b:b + 1],
                                            in1=bc[:, 2 * kind, :], op0=ALU.mult, op1=ALU.mult))
                v.tensor_tensor(h_tok[:, b, :], h_tok[:, b, :], bc[:, 2 * kind + 1, :], ALU.add).then_inc(h_ready[s], 1)

            def final(b0, b1):
                rsqrt_mean(4, b0, b1)
                v.wait_ge(ab_in[4], 16)
                for b in range(b0, b1):
                    v.scalar_tensor_tensor(out=peer_out[:, b, :], in0=x[:, b, :], scalar=tok_rs[:, b:b + 1],
                                           in1=bc[:, 3, :], op0=ALU.mult, op1=ALU.mult).then_inc(y_ready, 1)

            def norm(s):
                rsqrt_mean(s)
                v.wait_ge(ab_in[s], 64)
                for b in range(BLOCKS):
                    modulated(s, b)

            def gated(b):
                return v_tok[:, b, 0:CH], gates[:, b, 0:CH]

            def gate_projection(b):
                if b == 0:
                    v.wait_ge(gate_in[0], 32)
                v.wait_ge(ret_turned, b + 1)
                for c in range(2):
                    v.wait_ge(out_sums[0], 2 * b + c + 1)
                    v.tensor_tensor(gated(b)[c], bank[:, c, :], bc[:, 4 + min(b, 1), c * CH:(c + 1) * CH], ALU.mult)\
                        .then_inc(out_taken[0], 1)
                v.wait_ge(out_taken[0], 2 * b + 2)

            def add_gated(b):
                for c in range(2):
                    xs = x[:, b, c * CH:(c + 1) * CH]
                    ins = v.tensor_tensor(xs, xs, gated(b)[c], ALU.add)
                    if c == 1:
                        ins.then_inc(x_done[0], 1)
                        v.wait_ge(x_done[0], b + 1)
                    else:
                        dve.mark(ins)

            def add_projection(b):
                if b == 0:
                    v.wait_ge(gate_in[2], 32)
                for c in range(2):
                    g = 2 * b + c
                    v.wait_ge(out_sums[1], g + 1)
                    v.tensor_tensor(prod[g % 2], bank[:, g % 4, :], bc[:, 4 + min(b, 1), c * CH:(c + 1) * CH], ALU.mult)\
                        .then_inc(out_taken[1], 1)
                    v.wait_ge(out_taken[1], g + 1)
                    xs = x[:, b, c * CH:(c + 1) * CH]
                    ins = v.tensor_tensor(xs, xs, prod[g % 2], ALU.add)
                    if c == 1:
                        ins.then_inc(x_done[2], 1)
                        v.wait_ge(x_done[2], b + 1)
                    else:
                        step(ins)

            def peer(l):
                own = Count(peer_steps[l])
                v.memset(dots[:, :, :], 0.0).then_inc(u_free[l], U_RING)
                v.memset(warm[:, 0:1], 0.0).then_inc(v_free[l], TOPK)
                if l == 0:
                    v.memset(warm[:, 2:3], 0.0).then_inc(ada2_raw, 1)
                    for i in range(2):
                        v.memset(warm[:, 3 + i:4 + i], 0.0).then_inc(ada2_out[i], 16)

                def settle():
                    apart(v, passed_v, own.sem, own.now())

                def choose(m):
                    apart(v, passed_v, scores[l], m + 1)
                    sc = [bank[:, 4, s * P:(s + 1) * P] for s in range(2)]
                    for s in range(2):
                        own.mark(v.max(side_v[:, s, 0:8], sc[s]))
                    settle()
                    for s in range(2):
                        own.mark(v.match_replace(left[:, s, :], side_v[:, s, 0:8], sc[s], LOWEST))
                    for s in range(2):
                        ins = v.max_index(side_i[:, s, 0:8], side_v[:, s, 0:8], sc[s])
                        if s:
                            ins.then_inc(scores_read[l], 1)
                        else:
                            own.mark(ins)
                    settle()
                    for s in range(2):
                        own.mark(v.max(side_v[:, s, 8:16], left[:, s, :]))
                    settle()
                    for s in range(2):
                        own.mark(v.max_index(side_i[:, s, 8:16], side_v[:, s, 8:16], left[:, s, :]))
                    own.mark(v.tensor_tensor(cand.rearrange("p (a b) -> p a b", a=TOPK),
                                             side_v[:, 0, :].unsqueeze(2).to_broadcast([P, TOPK, TOPK]),
                                             side_v[:, 1, :].unsqueeze(1).to_broadcast([P, TOPK, TOPK]), ALU.add))
                    settle()
                    own.mark(v.max(top_v[:, 0:8], cand))
                    settle()
                    own.mark(v.match_replace(cand_left, top_v[:, 0:8], cand, LOWEST))
                    own.mark(v.tensor_scalar(top_n, top_v[:, 0:1], -1.0, None, ALU.mult))
                    own.mark(v.max_index(top_i[:, 0:8], top_v[:, 0:8], cand))
                    settle()
                    v.max(top_v[:, 8:16], cand_left).then_inc(top_ready[l], 1)
                    apart(v, passed_v, top_ready[l], m + 1)
                    own.mark(v.max_index(top_i[:, 8:16], top_v[:, 8:16], cand_left))
                    settle()
                    own.mark(v.tensor_scalar(pair[:, 0, :], top_i, 4, None, ALU.logical_shift_right))
                    own.mark(v.tensor_scalar(pair[:, 1, :], top_i, TOPK - 1, None, ALU.bitwise_and))
                    settle()
                    own.mark(v.tensor_tensor(onehot.rearrange("p s k a -> p (s k) a"),
                                             pair.rearrange("p s k -> p (s k)").unsqueeze(2).to_broadcast([P, 2 * TOPK, TOPK]),
                                             iota.unsqueeze(1).to_broadcast([P, 2 * TOPK, TOPK]), ALU.is_equal))
                    settle()
                    own.mark(v.tensor_tensor(onehot, onehot, side_i.unsqueeze(2).to_broadcast([P, 2, TOPK, TOPK]), ALU.mult))
                    settle()
                    own.mark(v.tensor_reduce(part_i.rearrange("p s k -> p (s k)"),
                                             onehot.rearrange("p s k a -> p (s k) a"), AX.X, ALU.add))
                    settle()
                    own.mark(v.scalar_tensor_tensor(out=part_i[:, 0, :], in0=part_i[:, 0, :], scalar=float(NKEYS),
                                                    in1=part_i[:, 1, :], op0=ALU.mult, op1=ALU.add))
                    apart(v, passed_v, exp_ready[l], m + 1)
                    own.mark(v.reciprocal(top_r, top_s))
                    settle()
                    at = slice(m * TOPK, (m + 1) * TOPK) if isinstance(m, int) else bass.ds(m * TOPK, TOPK)
                    own.mark(v.tensor_scalar(g_all[:, at], top_e, top_r, None, ALU.mult))
                    v.tensor_scalar(idx_all[:, at], part_i[:, 0, :], float(l * EXPERTS), None, ALU.add)\
                        .then_inc(idx_ready[l], 1)
                    settle()
                    apart(v, passed_v, idx_ready[l], m + 1)

                def norm_block(b):
                    if l == 1:
                        add_projection(b)
                    elif b == LATENT:
                        gate_projection(b)
                        add_gated(b)
                    rsqrt_mean(2 * l + 1, b, b + 1)
                    if b == 0:
                        v.wait_ge(ab_in[2 * l + 1], 64)
                    modulated(2 * l + 1, b)

                def dot(n, par, b, k):
                    row = u_rows[k % U_RING]
                    v.scalar_tensor_tensor(out=row, in0=row, scalar=1.0,
                                           in1=h_tok[:, (slice(b, b + 1) if isinstance(b, int) else bass.ds(b, 1)), :]
                                           .rearrange("p b d -> p (b d)"),
                                           op0=ALU.mult, op1=ALU.mult,
                                           accum_out=dots[:, par, k:k + 1]).then_inc(u_free[l], 1)

                def dots_of(n, par, b, ks):
                    for k in ks:
                        apart(v, passed_v, u_in[k % U_RING],
                              ((l * NQ + n) * (TOPK // U_RING) + k // U_RING + 1) * 16)
                        dot(n, par, b, k)

                norm_block(0)
                norm_block(1)
                if l == 0:
                    norm_block(2)
                    norm_block(3)
                    norm_block(4)
                    choose(0)
                    choose(1)
                    done = 0
                else:
                    choose(0)
                    norm_block(2)
                    dots_of(0, 0, 0, range(0, 4))
                    norm_block(3)
                    choose(1)
                    dots_of(0, 0, 0, range(4, 8))
                    norm_block(4)
                    done = 8
                v.memset(warm[:, 1:2], 0.0).then_inc(block_out[l], 1)
                own.mark(v.memset(qP[:, NQ * 256:], 0.0))
                before = own.n
                per = (before - 1) // AHEAD

                def two_heads(b, h2, what, first):
                    for par in range(2):
                        n = b * PHEADS + h2 * 2 + par
                        own.loop(n * per + before)
                        first_head = isinstance(n, int) and n == 0
                        dots_of(n, par, b, range(done if first_head else 0, TOPK))
                        apart(v, passed_v, gelu_ready[l], n + 1)
                        v.tensor_tensor(wgt, act16, g_all[:, part(n, TOPK)], ALU.mult).then_inc(wgt_ready[l], 1)
                        choose(n + AHEAD)
                        assert own.n == per

                peer_loops(v, l, two_heads)
                if l == 0:
                    v.wait_ge(ada2_in, 32)
                    t = ada_fix[:, 0, :]
                    step(v.tensor_tensor(t, t, ada_fix[:, 1, :], ALU.add))
                    step(v.tensor_tensor(t, t, ada_fix[:, 2, :], ALU.add))
                    v.tensor_tensor(t, t, ada_fix[:, 3, :], ALU.mult).then_inc(ada2_fixed, 1)
                v.wait_ge(gate_in[2 * l + 1], 32)
                for b in range(BLOCKS):
                    if l == 1 and b == LATENT:
                        final(0, b)
                    v.wait_ge(block_out[l], b + 2)
                    step(v.tensor_tensor(peer_out[:, b, :], peer_out[:, b, :], bc[:, 4 + min(b, 1), :], ALU.mult))
                    v.tensor_tensor(x[:, b, :], x[:, b, :], peer_out[:, b, :], ALU.add).then_inc(x_done[2 * l + 1], 1)
                    v.wait_ge(x_done[2 * l + 1], b + 1)

            for c in range(ADA):
                if c == ADA - 3:
                    norm(0)
                v.wait_ge(ada_sums, c + 1)
                r = rows[:, c * CH:(c + 1) * CH]
                v.tensor_tensor(r, bank[0:2, c % 4, :], r, ALU.add).then_inc(ada_taken, 1)
                if (c + 1) * CH in (2 * D, 5 * D):
                    sub = (c + 1) * CH // (3 * D)
                    r = rows[:, (3 * sub + 1) * D:(3 * sub + 2) * D]
                    v.wait_ge(ada_taken, c + 1)
                    ins = v.scalar_tensor_tensor(out=r, in0=r, scalar=1.0, in1=gain_rows[:, sub * D:(sub + 1) * D],
                                                 op0=ALU.add, op1=ALU.mult)
                    if sub == 0:
                        ins.then_inc(rows_ready, 1)
                    else:
                        dve.mark(ins)
            v.wait_ge(ada_taken, ADA)
            v.wait_ge(dve.sem, dve.now())
            v.memset(warm[:, 0:1], 0.0).then_inc(rows_ready, 1)

            rt = rot_t.rearrange("p (c h f) -> p c h f", c=2, h=3)
            for i, (c, b) in enumerate(items):
                if takes[i][0] is not taken_v:
                    continue
                v.wait_ge(proj, i + 1)
                if c < 2 and i >= 2:
                    v.wait_ge(qk_turned, i - 1)
                dst = rot[i % 2] if c < 2 else k_tok[:, b, (c - 2) * HALF:(c - 1) * HALF]
                src6 = bank[:, i % 4, 0:HALF].rearrange("p (h c j f) -> p c j h f", h=3, c=2, j=2)
                dst6 = dst.rearrange("p (h c j f) -> p c j h f", h=3, c=2, j=2)
                cos, sin = ([rope[:, w, b - 1, ax, :].unsqueeze(1).to_broadcast([P, 3, 32]) for ax in range(2)] for w in range(2))
                for j, op in ((0, ALU.subtract), (1, ALU.add)):
                    if j == 0 and takes[i][1] > 1:
                        v.wait_ge(taken_v, takes[i][1] - 1)
                    for ax in range(2):
                        dve.mark(v.tensor_tensor(dst6[:, ax, j], src6[:, ax, j], cos[ax], ALU.mult))
                        dve.mark(v.tensor_tensor(rt[:, ax], src6[:, ax, 1 - j], sin[ax], ALU.mult))
                    v.wait_ge(dve.sem, dve.now())
                    for ax in range(2):
                        ins = v.tensor_tensor(dst6[:, ax, j], dst6[:, ax, j], rt[:, ax], op)
                        if j == 1 and ax == 1:
                            ins.then_inc(taken_v, 1)
                        else:
                            dve.mark(ins)
                    if j == 0:
                        v.wait_ge(dve.sem, dve.now())

            v.wait_ge(states_in, 32)
            v.wait_ge(*takes[39])
            v.wait_ge(taken_v, nv)

            def scaled_k(j):
                d, b = updates[j]
                if j >= 2:
                    v.wait_ge(upd_sums, j - 1)
                z = xi_zeta[:, ZETA_F if d == "f" else ZETA_B, :].unsqueeze(2).to_broadcast([P, HEADS, DK])
                v.tensor_tensor(kz[j % 2].rearrange("p (h e) -> p h e", h=HEADS),
                                k_tok[:, b, :].rearrange("p (h e) -> p h e", h=HEADS), z, ALU.mult).then_inc(kz_ready, 1)

            scaled_k(0)
            for what, j in order:
                if what == "u":
                    if j + 1 < len(updates):
                        scaled_k(j + 1)
                    d, b = updates[j]
                    v.wait_ge(upd_sums, j + 1)
                    if b == 0:
                        v.tensor_copy(heads3(new_s[d == "b"]), banks3(0)).then_inc(state_ready, 1)
                    else:
                        old, new = (s_f, s_f) if d == "f" else (s_b[:, b - 1, :], s_b[:, b - 2, :])
                        g = g_chunk[:, 0:HEADS] if d == "f" else g_chunk[:, HEADS:2 * HEADS]
                        if d == "f":
                            v.wait_ge(ret_sums, b + 1)
                        step(v.tensor_tensor(heads3(new), heads3(old), wide(g), ALU.mult))
                        v.tensor_tensor(heads3(new), heads3(new), banks3(0), ALU.add).then_inc(state_ready, 1)
                        v.wait_ge(state_ready, j + 1)
                    continue
                b = j
                v.wait_ge(att_sums, b + 1)
                v.tensor_tensor(heads3(att), banks3(0), heads3(decay), ALU.mult).then_inc(att_ready, 1)
                v.wait_ge(ret_sums, b + 1)
                if b == 0:
                    v.tensor_copy(heads3(o1), banks3(2)).then_inc(ret_taken, 1)
                    v.wait_ge(ret_taken, 1)
                else:
                    dve.mark(v.tensor_tensor(heads3(o1), banks3(4), wide(xi_zeta[:, XI_F, :]), ALU.mult))
                    step(v.tensor_tensor(heads3(o2), banks3(6), wide(xi_zeta[:, XI_B, :]), ALU.mult))
                    step(v.tensor_tensor(o1, o1, o2, ALU.add))
                    v.tensor_tensor(heads3(o1), banks3(2), heads3(o1), ALU.add).then_inc(ret_taken, 1)
                    v.wait_ge(ret_taken, b + 1)
                o3 = o1.rearrange("p (h e) -> p h e", h=HEADS)
                q3 = o2.rearrange("p (h e) -> p h e", h=HEADS)
                step(v.tensor_reduce(hstat[:, 0, :], o3, AX.X, ALU.add))
                step(v.tensor_scalar(hstat[:, 0, :], hstat[:, 0, :], 1.0 / DK, None, ALU.mult))
                step(v.tensor_tensor(o3, o3, hstat[:, 0, :].unsqueeze(2).to_broadcast([P, HEADS, DK]), ALU.subtract))
                step(v.tensor_tensor(o2, o1, o1, ALU.mult))
                step(v.tensor_reduce(hstat[:, 1, :], q3, AX.X, ALU.add))
                v.tensor_scalar(hstat[:, 1, :], hstat[:, 1, :], 1.0 / DK, GN_EPS, ALU.mult, ALU.add).then_inc(ret_var, 1)
                v.wait_ge(ret_root, b + 1)
                step(v.reciprocal(hstat[:, 3, :], hstat[:, 2, :]))
                step(v.tensor_tensor(o3, o3, hstat[:, 3, :].unsqueeze(2).to_broadcast([P, HEADS, DK]), ALU.mult))
                v.tensor_tensor(gates[:, b, :], gates[:, b, :], o1, ALU.mult).then_inc(ret_ready, 1)
                v.wait_ge(ret_ready, b + 1)
                if b:
                    gate_projection(b - 1)
            v.wait_ge(x_back, 16)
            for b in range(LATENT):
                add_gated(b)
            peer(0)

            norm(2)
            v.wait_ge(hT_ready[2], BLOCKS)
            v.wait_ge(conv_in, 16)
            dve.mark(v.memset(mean_w, 1.0 / D))
            for a, n in ((0, PAD), (P + PAD, 2 * PAD), (UW - PAD, PAD)):
                last = v.memset(u_pad[:, :, a:a + n], 0.0)
                dve.mark(last)
            v.wait_ge(dve.sem, dve.now())

            def glu(f):
                v.wait_ge(sig_ready, f + 1)
                for t0, n, _, u0, kind in segs:
                    last = v.tensor_tensor(u_pad[:, f, u0:u0 + n], bank[:, 4 * (f % 2) + kind, 0:n],
                                           sig[f % 2][:, t0:t0 + n], ALU.mult)
                    if kind == 0:
                        dve.mark(last)
                last.then_inc(u_ready, 1)

            between = {(0, 11): 2, (0, 21): 3, (2, 1): 4, (2, 11): 5, (2, 21): 6, (4, 1): 7}
            glu(0)
            glu(1)
            for t in range(0, KT - PE_TILES, 2):
                v.wait_ge(u_ready, t + 2)
                v.wait_ge(dve.sem, dve.now())
                for tap in range(TAPS):
                    if (t, tap) in between:
                        glu(between[t, tap])
                    for f in (t, t + 1):
                        src = u_pad[:, f, tap:tap + YW]
                        w = cols[:, f, tap:tap + 1]
                        if tap == 0:
                            dve.mark(v.tensor_scalar(y_conv[:, f, :], src, w, cols[:, f, TAPS:TAPS + 1], ALU.mult, ALU.add))
                            continue
                        v.wait_ge(dve.sem, dve.now() - (tap < TAPS - 1 or f == t))
                        ins = v.scalar_tensor_tensor(out=y_conv[:, f, :], in0=src, scalar=w, in1=y_conv[:, f, :],
                                                     op0=ALU.mult, op1=ALU.add)
                        if tap == TAPS - 1:
                            ins.then_inc(conv_ready, 1)
                        else:
                            dve.mark(ins)
                            continue
            v.wait_ge(ln_mean, 1)
            for f in range(KT):
                for t0, n, y0, _, kind in segs:
                    last = v.tensor_tensor(y_conv[:, f, y0:y0 + n], y_conv[:, f, y0:y0 + n], bank[:, 4 + kind, 0:n], ALU.subtract)
                    if kind == 0:
                        dve.mark(last)
                last.then_inc(centred, 1)
            v.wait_ge(sq_used, KT)
            for t0, n, _, _, kind in segs:
                last = v.tensor_scalar(ln_rs[:, t0:t0 + n], bank[:, 6 + kind, 0:n], GN_EPS, None, ALU.add)
                if kind == 0:
                    dve.mark(last)
            last.then_inc(ln_ve, 1)
            v.wait_ge(ln_root, 1)
            v.wait_ge(centred, KT)
            for t0, n, y0, _, kind in segs:
                step(v.reciprocal(ln_rs[:, t0:t0 + n], ln_rs[:, t0:t0 + n]))
                for f in range(KT):
                    v.tensor_tensor(y_conv[:, f, y0:y0 + n], y_conv[:, f, y0:y0 + n], ln_rs[:, t0:t0 + n], ALU.mult)\
                        .then_inc(normed, 1)
            peer(1)

            final(LATENT, BLOCKS)


_INS = ["x_in", "cond_t", "norm_gain", "final_gain", "ada_w", "ada_b", "ada_fix_in", "ab_w_in", "ab_w_out", "decays", "states",
        "conv_w_in", "conv_cols", "conv_w_out", "peer_w_q", "keys_t", "peer_u", "peer_v", "const", "dft"]


def kernel(**a):
    import concourse.bacc as _bacc
    from concourse.bass_utils import run_bass_kernel_spmd as _run

    a = {k: np.asarray(w) for k, w in a.items()}
    const, dft = constants()
    ones, none = np.ones(D, np.float32), np.zeros(D, np.float32)
    g = a["norm_gain"][1]
    fixes = [np.tile(np.concatenate(v), 2).reshape(-1, P) for v in
             ([none, ones, none, none, ones, none], [ones, g[0], ones, ones, g[1], ones])]
    feature = lambda w: w.reshape(-1, KT, P).transpose(2, 1, 0)
    laid = {
        "x_in": np.concatenate([a["x_prompt"][0], a["x_sample"][0]]),
        "cond_t": feature(np.stack([a["c_ctx"], a["c"][0]])),
        "norm_gain": a["norm_gain"].reshape(1, -1), "final_gain": a["final_gain"].reshape(1, -1),
        "ada_w": a["ada_w"], "ada_b": a["ada_b"],
        "ada_fix_in": np.stack([np.tile(a["ada_b"][1].reshape(-1, P), (2, 1)), *fixes]).reshape(3, 2 * 48, P),
        "ab_w_in": a["ab_w_in"][0], "ab_w_out": a["ab_w_out"][0],
        "decays": np.concatenate([a["ret_decay_fwd"], a["ret_decay_bwd"]], 1),
        "states": np.stack([a["state_ret_fwd"][0, 0], a["state_ret_bwd"][0, 0]]),
        "conv_w_in": a["conv_w_in"][0],
        "conv_cols": feature(np.concatenate([a["conv_dw_w"][0], a["conv_dw_b"], a["conv_ln_g"], a["conv_ln_b"]])),
        "conv_w_out": a["conv_w_out"][0],
        "peer_w_q": a["peer_w_q"],
        "keys_t": a["peer_sub_keys"].transpose(0, 4, 1, 2, 3).reshape(LAYERS, P, -1),
        "peer_u": a["peer_u"].reshape(-1, D), "peer_v": a["peer_v"].reshape(-1, D),
        "const": const, "dft": dft,
    }
    nc = _bacc.Bacc("TRN2", target_bir_lowering=False, num_devices=1)
    arrays, args = {}, []
    for name in _INS:
        w = np.ascontiguousarray(laid[name])
        arrays[f"in_{name}"] = w
        args.append(nc.dram_tensor(f"in_{name}", w.shape, mybir.dt.from_np(w.dtype), kind="ExternalInput").ap())
    y = nc.dram_tensor("out_y", (T, D), F32, kind="ExternalOutput").ap()
    st = nc.dram_tensor("out_states", (2, HEADS, DK, DK), F32, kind="ExternalOutput").ap()
    mod = nc.dram_tensor("mod_rows", (LAYERS, 2, 6 * D), F32, kind="Internal").ap()
    program(nc, *args, y, st, mod)
    r = _run(nc, [arrays], core_ids=[0])
    y, st = r.results[0]["out_y"], r.results[0]["out_states"]
    return y[:P][None], y[P:][None], st[0][None, None], st[1][None, None]
```
